# Optimizing a Trainium2 kernel written in Bass

```python
import math
import jax, jax.numpy as jnp
from jax import lax
import numpy as np

D_MODEL = 1024
BATCH = 1
SEQ = 1024
DEPTH = 2
DEC_BATCH = 8
DEC_SEQ = 4
PAST_LEN = 2048
PAGE_SIZE = 128

RET_HEADS = 4
RET_QK_DIM = D_MODEL // RET_HEADS
RET_V_DIM = 2 * RET_QK_DIM
RET_CHUNK = 128
SWA_HEAD_DIM = 64
SWA_Q_HEADS = D_MODEL // SWA_HEAD_DIM
SWA_KV_HEADS = 4
SWA_GROUP = SWA_Q_HEADS // SWA_KV_HEADS
WINDOW = 128
SWA_BLOCK = WINDOW
D_FF = 4 * D_MODEL
ROPE_THETA = 10000.0
EPS = 1e-6
NEG_INF = -1e30
N_RET = (DEPTH + 1) // 2
N_SWA = DEPTH // 2

kernel_name = "hybrid_retention_swa_sink_decoder_step"

def rms_norm(x, g):
    xf = x.astype(jnp.float32)
    y = xf * lax.rsqrt(jnp.mean(xf * xf, axis=-1, keepdims=True) + EPS)
    return (y * g.astype(jnp.float32)).astype(x.dtype)

def rope(x, pos):
    d = x.shape[-1]
    half = d // 2
    inv = ROPE_THETA ** (-jnp.arange(half, dtype=jnp.float32) / half)
    ang = pos.astype(jnp.float32)[:, None] * inv[None, :]
    cos = jnp.cos(ang)[:, None, :]
    sin = jnp.sin(ang)[:, None, :]
    xf = x.astype(jnp.float32)
    x1, x2 = xf[..., :half], xf[..., half:]
    return jnp.concatenate([x1 * cos - x2 * sin, x2 * cos + x1 * sin], axis=-1).astype(x.dtype)

def retention(h, s0, pos, w_in, w_out):
    B, T, _ = h.shape
    H, dk, dv = RET_HEADS, RET_QK_DIM, RET_V_DIM
    proj = (h @ w_in).astype(jnp.float32)
    q = proj[..., :H * dk].reshape(B, T, H, dk)
    k = proj[..., H * dk:2 * H * dk].reshape(B, T, H, dk)
    v = proj[..., 2 * H * dk:2 * H * dk + H * dv].reshape(B, T, H, dv)
    g = proj[..., 2 * H * dk + H * dv:]
    q = rope(q, pos)
    k = rope(k, pos) * (dk ** -0.5)
    C = RET_CHUNK if T % RET_CHUNK == 0 else T
    nc = T // C
    log_g = jnp.log1p(-jnp.exp2(-5.0 - jnp.arange(H, dtype=jnp.float32)))
    idx = jnp.arange(C, dtype=jnp.float32)
    diff = idx[:, None] - idx[None, :]
    dmat = jnp.where(diff >= 0, jnp.exp(jnp.maximum(diff, 0.0)[None] * log_g[:, None, None]), 0.0)
    q_dec = jnp.exp((idx + 1.0)[:, None] * log_g[None, :])
    k_dec = jnp.exp((C - 1.0 - idx)[:, None] * log_g[None, :])
    c_dec = jnp.exp(C * log_g)
    qc = q.reshape(B, nc, C, H, dk)
    kc = k.reshape(B, nc, C, H, dk)
    vc = v.reshape(B, nc, C, H, dv)
    scores = jnp.einsum('bnihd,bnjhd->bnhij', qc, kc) * dmat[None, None]
    intra = jnp.einsum('bnhij,bnjhe->bnihe', scores, vc)

    def step(S, xs):
        qi, ki, vi = xs
        cross = jnp.einsum('bihd,bhde->bihe', qi * q_dec[None, :, :, None], S)
        S = S * c_dec[None, :, None, None] + jnp.einsum('bjhd,bjhe->bhde', ki * k_dec[None, :, :, None], vi)
        return S, cross

    s_fin, cross = lax.scan(step, s0.astype(jnp.float32),
                            (qc.transpose(1, 0, 2, 3, 4), kc.transpose(1, 0, 2, 3, 4), vc.transpose(1, 0, 2, 3, 4)))
    o = (intra + cross.transpose(1, 0, 2, 3, 4)).reshape(B, T, H, dv)
    o = o * lax.rsqrt(jnp.mean(o * o, axis=-1, keepdims=True) + EPS)
    o = o.reshape(B, T, H * dv) * jax.nn.silu(g)
    return o.astype(h.dtype) @ w_out, s_fin

def sink_softmax(s, mask, sinks):
    s = jnp.where(mask, s, NEG_INF)
    sk = sinks.astype(jnp.float32)[:, :, None, None]
    m = jnp.maximum(jnp.max(s, axis=-1, keepdims=True), sk)
    p = jnp.exp(s - m)
    return p / (jnp.sum(p, axis=-1, keepdims=True) + jnp.exp(sk - m))

def swa_qkv(h, pos, w_qkv, q_norm, k_norm):
    B, T, _ = h.shape
    Hq, Hkv, dh = SWA_Q_HEADS, SWA_KV_HEADS, SWA_HEAD_DIM
    proj = h @ w_qkv
    q = proj[..., :Hq * dh].reshape(B, T, Hq, dh)
    k = proj[..., Hq * dh:(Hq + Hkv) * dh].reshape(B, T, Hkv, dh)
    v = proj[..., (Hq + Hkv) * dh:].reshape(B, T, Hkv, dh)
    q = rope(rms_norm(q, q_norm), pos)
    k = rope(rms_norm(k, k_norm), pos)
    return q.reshape(B, T, Hkv, SWA_GROUP, dh), k, v

def swa_prompt(h, pos, w_qkv, q_norm, k_norm, sinks, w_o):
    B, T, _ = h.shape
    q, k, v = swa_qkv(h, pos, w_qkv, q_norm, k_norm)
    nb = T // SWA_BLOCK
    qb = q.reshape(B, nb, SWA_BLOCK, SWA_KV_HEADS, SWA_GROUP, SWA_HEAD_DIM)
    kb = k.reshape(B, nb, SWA_BLOCK, SWA_KV_HEADS, SWA_HEAD_DIM)
    vb = v.reshape(B, nb, SWA_BLOCK, SWA_KV_HEADS, SWA_HEAD_DIM)
    shift = lambda a: jnp.concatenate([jnp.zeros_like(a[:, :1]), a[:, :-1]], axis=1)
    kk = jnp.concatenate([shift(kb), kb], axis=2)
    vv = jnp.concatenate([shift(vb), vb], axis=2)
    blk = jnp.arange(nb)[:, None]
    qpos = blk * SWA_BLOCK + jnp.arange(SWA_BLOCK)[None, :]
    kpos = (blk - 1) * SWA_BLOCK + jnp.arange(2 * SWA_BLOCK)[None, :]
    d = qpos[:, :, None] - kpos[:, None, :]
    mask = (d >= 0) & (d < WINDOW) & (kpos[:, None, :] >= 0)
    s = jnp.einsum('bnikgd,bnjkd->bnkgij', qb, kk).astype(jnp.float32) * (SWA_HEAD_DIM ** -0.5)
    p = sink_softmax(s, mask[None, :, None, None], sinks.reshape(SWA_KV_HEADS, SWA_GROUP))
    o = jnp.einsum('bnkgij,bnjkd->bnikgd', p.astype(vv.dtype), vv).reshape(B, T, SWA_Q_HEADS * SWA_HEAD_DIM)
    return o @ w_o, k[:, -WINDOW:], v[:, -WINDOW:]

def swa_sample(h, pos, cache_k, cache_v, w_qkv, q_norm, k_norm, sinks, w_o):
    B, T, _ = h.shape
    L = cache_k.shape[1]
    q, k, v = swa_qkv(h, pos, w_qkv, q_norm, k_norm)
    kk = jnp.concatenate([cache_k.astype(k.dtype), k], axis=1)
    vv = jnp.concatenate([cache_v.astype(v.dtype), v], axis=1)
    kpos = PAST_LEN - L + jnp.arange(L + T)
    d = pos[:, None] - kpos[None, :]
    mask = (d >= 0) & (d < WINDOW)
    s = jnp.einsum('btkgd,bskd->bkgts', q, kk).astype(jnp.float32) * (SWA_HEAD_DIM ** -0.5)
    p = sink_softmax(s, mask[None, None, None], sinks.reshape(SWA_KV_HEADS, SWA_GROUP))
    o = jnp.einsum('bkgts,bskd->btkgd', p.astype(vv.dtype), vv).reshape(B, T, SWA_Q_HEADS * SWA_HEAD_DIM)
    return o @ w_o, kk[:, -L:], vv[:, -L:]

def sq_relu_mlp(h, w_up, w_down):
    a = jax.nn.relu(h @ w_up)
    return (a * a) @ w_down

def setup_inputs(seed: int = 0) -> dict:
    key = jax.random.key(seed)
    ks = jax.random.split(key, 16)
    f32 = jnp.float32
    nrm = lambda k, shape, scale: jax.random.normal(k, shape, f32) * scale
    L = min(WINDOW, PAST_LEN)
    ret_in = 2 * RET_HEADS * RET_QK_DIM + 2 * RET_HEADS * RET_V_DIM
    swa_in = (SWA_Q_HEADS + 2 * SWA_KV_HEADS) * SWA_HEAD_DIM
    return {
        "x_prompt": nrm(ks[0], (BATCH, SEQ, D_MODEL), 1.0),
        "x_sample": nrm(ks[1], (DEC_BATCH, DEC_SEQ, D_MODEL), 1.0),
        "state_ret": nrm(ks[2], (N_RET, DEC_BATCH, RET_HEADS, RET_QK_DIM, RET_V_DIM), 0.5),
        "cache_swa_k": nrm(ks[3], (N_SWA, DEC_BATCH, L, SWA_KV_HEADS, SWA_HEAD_DIM), 1.0),
        "cache_swa_v": nrm(ks[4], (N_SWA, DEC_BATCH, L, SWA_KV_HEADS, SWA_HEAD_DIM), 1.0),
        "norm_mix": 1.0 + nrm(ks[5], (DEPTH, D_MODEL), 0.1),
        "norm_ffn": 1.0 + nrm(ks[6], (DEPTH, D_MODEL), 0.1),
        "ret_w_in": nrm(ks[7], (N_RET, D_MODEL, ret_in), D_MODEL ** -0.5),
        "ret_w_out": nrm(ks[8], (N_RET, RET_HEADS * RET_V_DIM, D_MODEL), (RET_HEADS * RET_V_DIM) ** -0.5),
        "swa_w_qkv": nrm(ks[9], (N_SWA, D_MODEL, swa_in), D_MODEL ** -0.5),
        "swa_q_norm": 1.0 + nrm(ks[10], (N_SWA, SWA_HEAD_DIM), 0.1),
        "swa_k_norm": 1.0 + nrm(ks[11], (N_SWA, SWA_HEAD_DIM), 0.1),
        "swa_sinks": nrm(ks[12], (N_SWA, SWA_Q_HEADS), 1.0),
        "swa_w_o": nrm(ks[13], (N_SWA, SWA_Q_HEADS * SWA_HEAD_DIM, D_MODEL), (SWA_Q_HEADS * SWA_HEAD_DIM) ** -0.5),
        "ffn_w_up": nrm(ks[14], (DEPTH, D_MODEL, D_FF), D_MODEL ** -0.5),
        "ffn_w_down": nrm(ks[15], (DEPTH, D_FF, D_MODEL), D_FF ** -0.5),
    }

def reference(x_prompt, x_sample, state_ret, cache_swa_k, cache_swa_v, norm_mix, norm_ffn,
              ret_w_in, ret_w_out, swa_w_qkv, swa_q_norm, swa_k_norm, swa_sinks, swa_w_o,
              ffn_w_up, ffn_w_down):
    pos_p = jnp.arange(SEQ)
    pos_s = PAST_LEN + jnp.arange(DEC_SEQ)
    xp, xs = x_prompt, x_sample
    ret_p, ret_s, kp, vp, ksmp, vsmp = [], [], [], [], [], []
    for i in range(DEPTH):
        hp = rms_norm(xp, norm_mix[i])
        hs = rms_norm(xs, norm_mix[i])
        if i % 2 == 0:
            r = i // 2
            s0 = jnp.zeros((BATCH, RET_HEADS, RET_QK_DIM, RET_V_DIM), jnp.float32)
            op, sp = retention(hp, s0, pos_p, ret_w_in[r], ret_w_out[r])
            os_, ss = retention(hs, state_ret[r], pos_s, ret_w_in[r], ret_w_out[r])
            ret_p.append(sp)
            ret_s.append(ss)
        else:
            a = i // 2
            op, k1, v1 = swa_prompt(hp, pos_p, swa_w_qkv[a], swa_q_norm[a], swa_k_norm[a], swa_sinks[a], swa_w_o[a])
            os_, k2, v2 = swa_sample(hs, pos_s, cache_swa_k[a], cache_swa_v[a], swa_w_qkv[a], swa_q_norm[a],
                                     swa_k_norm[a], swa_sinks[a], swa_w_o[a])
            kp.append(k1)
            vp.append(v1)
            ksmp.append(k2)
            vsmp.append(v2)
        xp = xp + op.astype(xp.dtype)
        xs = xs + os_.astype(xs.dtype)
        xp = xp + sq_relu_mlp(rms_norm(xp, norm_ffn[i]), ffn_w_up[i], ffn_w_down[i]).astype(xp.dtype)
        xs = xs + sq_relu_mlp(rms_norm(xs, norm_ffn[i]), ffn_w_up[i], ffn_w_down[i]).astype(xs.dtype)
    return (xp, xs, jnp.stack(ret_p), jnp.stack(kp), jnp.stack(vp), jnp.stack(ret_s), jnp.stack(ksmp), jnp.stack(vsmp))


_drawn_inputs = setup_inputs


def setup_inputs(seed=0):
    import zlib

    import numpy as np

    out = dict(_drawn_inputs(seed))
    spreads = {}
    factors = {'swa_q_norm': 6.26, 'swa_sinks': 8.0}
    for name, (base, spread) in spreads.items():
        noise = np.random.default_rng([zlib.crc32(name.encode()), seed]).standard_normal(out[name].shape)
        drawn = base * np.exp(spread * noise) if base else spread * noise
        out[name] = __import__('jax').numpy.asarray(drawn.astype(out[name].dtype))
    for name, factor in factors.items():
        out[name] = (out[name] * factor).astype(out[name].dtype)
    return out
```

```python
import numpy as np
import concourse.bass as bass
from concourse import mybir
from contextlib import ExitStack

F32 = mybir.dt.float32
F32R = mybir.dt.float32r
ALU = mybir.AluOpType
ACT = mybir.ActivationFunctionType
AX = mybir.AxisListType

P = 128
D = 1024
SEQ = 1024
NB, NT = 8, 4
NS = NB * NT
TOK = SEQ + NS
TB, NTB = 352, 3
DT = D // P
RH, DK, DV = 4, 256, 512
CH = SEQ // P
PAST = 2048
WIN = 128
HD = 64
KVH = 4
NPAIR, GR = 2, 4
PH = 2 * GR
FFC = 8
EPS = 1e-6
NEG = -1e30
THETA = 10000.0

KG = 4
RING = 4
LEAD = 3
RET_SLABS = 12 * 2 + DT
FFN_SLABS = 4 * 2 + DT
SWA_SLABS = 6 * 2 + DT
FFN0_SLAB = RH * RET_SLABS
SWA_SLAB = FFN0_SLAB + FFC * FFN_SLABS
FFN1_SLAB = SWA_SLAB + NPAIR * SWA_SLABS
N_SLABS = FFN1_SLAB + FFC * FFN_SLABS

RET_MT, FFN_MT, SWA_MT = 12 + DT, 4 + DT, 6 + DT
FFN0_MT = RH * RET_MT
SWA_MT0 = FFN0_MT + FFC * FFN_MT
FFN1_MT = SWA_MT0 + NPAIR * SWA_MT

FFN0_A = RH * 4
SWA_A = FFN0_A + FFC * 4
FFN1_A = SWA_A + NPAIR * 4

C_ID, C_ONE, C_GAIN = 0, P, 2 * P
C_EPS = C_GAIN + 4 * DT
C_BM = C_EPS + 1
C_QN, C_KN = C_BM + NB, C_BM + NB + 1
C_SINK = C_KN + 1
C_SINKS = C_SINK + NPAIR * PH
C_N = C_SINKS + NPAIR
H_QDEC, H_KDEC, H_CDEC, H_QDS, H_KDS, H_CDS = range(6)
A_BO, A_MASK, A_N = 0, P, P + 2 * P
KEYS = WIN + NS


def trunk(nc, xT, weights, tables, attn_tables, consts, ret_masks, ret_decays, attn_consts, sample_mask, state_in, cache_k,
          cache_v, yT, state_p, kp_out, vp_out, state_s, ks_out, vs_out):
    with ExitStack() as ctx:
        base = (nc.sbuf_base + 31) // 32 * 32

        def at(name, offset, shape, dt):
            return nc.alloc_sbuf_tensor_at(name, shape, dt, offset=base + offset)

        TT = TOK * 4
        o_x, o_hhi, o_hlo = 0, DT * TT, 2 * DT * TT
        o_ahi = 3 * DT * TT
        o_alo = o_ahi + KG * TT
        o_wraw = o_alo + KG * TT
        o_whi = o_wraw + RING * 2048
        o_wlo = o_whi + RING * 2048
        o_rst = o_wlo + RING * 2048
        o_cst = o_rst + TT
        o_work = (o_cst + 4 * C_N + 31) // 32 * 32

        x = at("x", o_x, [P, DT, TOK], F32)
        hhi = at("hhi", o_hhi, [P, DT, TOK], F32R)
        hlo = at("hlo", o_hlo, [P, DT, TOK], F32R)
        ahi = at("ahi", o_ahi, [P, KG, TOK], F32R)
        alo = at("alo", o_alo, [P, KG, TOK], F32R)
        wraw = at("wraw", o_wraw, [P, RING, 512], F32)
        whi = at("whi", o_whi, [P, RING, 512], F32R)
        wlo = at("wlo", o_wlo, [P, RING, 512], F32R)
        rst = at("rst", o_rst, [P, TOK], F32)
        cst = at("cst", o_cst, [P, C_N], F32)
        ident = cst[:, C_ID:C_ID + P]
        ones = cst[:, C_ONE:C_ONE + P]
        eps = cst[:, C_EPS:C_EPS + 1]

        o_v = o_work + 4 * TT
        qk = at("qk", o_work, [P, 4, TOK], F32)
        v_tok = at("v_tok", o_v, [P, CH + 1, DV], F32)
        rope_tab = at("rope_tab", o_v, [P, 2, TOK], F32)
        q_sel = at("q_sel", o_v, [P, 2, NB, NS], F32)
        k_sel = at("k_sel", o_v + 2048, [P, NB, DK], F32)
        o_r = o_v + (CH + 1) * DV * 4
        s_ret = at("s_ret", o_r, [P, 2, DV], F32)
        sc_t = at("sc_t", o_r + 4096, [P, 2, P], F32)
        k_tok = at("k_tok", o_r + 5120, [P, 2, DK], F32)
        o_tok = at("o_tok", o_r + 7168, [P, DV], F32)
        hmask = at("hmask", o_r + 9216, [P, P + NS], F32)
        stat = at("stat", o_r + 9856, [P, 4], F32)
        hc = at("hc", o_r + 9888, [P, 6], F32)
        o_t = at("o_t", o_ahi, [P, 4, TOK], F32)
        tmp = at("tmp", o_alo, [P, 4, TOK], F32)
        s0 = at("s0", o_alo, [P, 4, 2, DV], F32)

        sq = at("sq", o_work, [P, 2, TOK], F32)
        ssum = at("ssum", o_work + 2 * TT, [P, TOK], F32)
        relu = at("relu", o_work + 4 * TT, [P, 2, TOK], F32)
        a2 = at("a2", o_work + 6 * TT, [P, 2, TOK], F32)

        q_a = at("q_a", o_work, [P, GR, TOK], F32)
        k_a = at("k_a", o_work + 4 * TT, [P, TOK], F32)
        o_a = o_work + 5 * TT
        v_a = at("v_a", o_a, [P, CH + 1, P], F32)
        oc = at("oc", o_a + 4608, [P, DV], F32)
        acst = at("acst", o_a + 6656, [P, A_N], F32)
        ast = at("ast", o_a + 6656 + 4 * A_N, [P, 80], F32)
        vt_a = at("vt_a", o_a + 6976 + 4 * A_N, [P, TOK], F32)
        z_a = at("z_a", o_ahi, [P, 2, TOK], F32)
        zz = at("zz", o_ahi + 2 * TT, [P, TOK], F32)
        zg = at("zg", o_ahi + 3 * TT, [P, TOK], F32)
        zr = at("zr", o_ahi + 4 * TT, [P, TOK], F32)
        nr = at("nr", o_ahi + 5 * TT, [P, TOK], F32)
        atab = at("atab", o_ahi + 6 * TT, [P, 2, TOK], F32)
        kc = at("kc", o_ahi, [P, NB, P], F32)
        vc = at("vc", o_ahi + 4096, [P, NB, P], F32)
        kct = at("kct", o_ahi + 8192, [P, NB, P], F32)
        sa = at("sa", o_ahi + 12288, [P, NB, KEYS], F32)
        q_bd = at("q_bd", o_ahi + 17408, [P, NB, NS], F32)
        pts = at("pts", o_ahi + 18432, [P, 2, NB, NS], F32)
        nk = at("nk", o_ahi + 32768, [P, 2, P], F32)
        p_a = at("p_a", o_ahi, [P, 2, PH, 2 * P], F32)
        pt_a = at("pt_a", o_ahi + 16384, [P, 2, 4, 4 * P], F32)
        bones = acst[:, A_BO:A_BO + P]

        ps = ctx.enter_context(nc.psum_tensor("ps", [P, 8, 512], F32))

        def sem(name):
            return ctx.enter_context(nc.semaphore(name))

        w_in = [sem(f"w_in{i}") for i in range(RING)]
        w_hi = sem("w_hi")
        w_lo = sem("w_lo")
        slab_used = sem("slab_used")
        mt_free = sem("mt_free")
        c_in = sem("c_in")
        x_in = [sem(f"x_in{k}") for k in range(DT)]
        tab_in = sem("tab_in")
        h_hi = sem("h_hi")
        h_lo = sem("h_lo")
        sq_done = sem("sq_done")
        sum_done = sem("sum_done")
        ssq_done = sem("ssq_done")
        rst_sq = sem("rst_sq")
        rst_done = sem("rst_done")
        a2_done = sem("a2_done")
        a_hi = sem("a_hi")
        a_lo = sem("a_lo")
        dve_seq = sem("dve_seq")
        v_turned = sem("v_turned")
        v_kept = sem("v_kept")
        sc_done = sem("sc_done")
        sc_kept = sem("sc_kept")
        kt_done = sem("kt_done")
        kt_kept = sem("kt_kept")
        st_done = sem("st_done")
        s_upd = sem("s_upd")
        o_done = sem("o_done")
        ss_done = sem("ss_done")
        rs_done = sem("rs_done")
        rr_done = sem("rr_done")
        o_kept = sem("o_kept")
        ot_done = sem("ot_done")
        ot_kept = sem("ot_kept")
        sp_out = sem("sp_out")
        sel_ready = sem("sel_ready")
        sts_done = sem("sts_done")
        s0_upd = sem("s0_upd")
        s0_in = [sem(f"s0_in{i}") for i in range(4)]
        s0_out = [sem(f"s0_out{i}") for i in range(4)]
        g_silu = sem("g_silu")
        g_of = sem("g_of")
        ac_in = sem("ac_in")
        zz_done = sem("zz_done")
        zg_done = sem("zg_done")
        zr_in = sem("zr_in")
        zs_done = sem("zs_done")
        hsum_done = sem("hsum_done")
        hroot_done = sem("hroot_done")
        qk_ready = sem("qk_ready")
        av_turned = sem("av_turned")
        av_kept = sem("av_kept")
        nk_done = sem("nk_done")
        nk_kept = sem("nk_kept")
        kc_in = sem("kc_in")
        kct_done = sem("kct_done")
        kct_kept = sem("kct_kept")
        qbd_ready = sem("qbd_ready")
        sas_done = sem("sas_done")
        sa_max = sem("sa_max")
        sa_exp = sem("sa_exp")
        sa_ready = sem("sa_ready")
        pts_done = sem("pts_done")
        pts_kept = sem("pts_kept")
        os_done = sem("os_done")
        os_kept = sem("os_kept")
        s_done = sem("s_done")
        s_kept = sem("s_kept")
        m_ready = sem("m_ready")
        p_done = sem("p_done")
        pt_done = sem("pt_done")
        pt_kept_v = sem("pt_kept_v")
        pt_kept_s = sem("pt_kept_s")
        pv_done = sem("pv_done")
        oc_kept = sem("oc_kept")
        oct_done = sem("oct_done")
        oct_kept = sem("oct_kept")
        swa_out = sem("swa_out")
        y_out = sem("y_out")

        block = ctx.enter_context(nc.Block())

        def bank_set(m):
            return ps[:, 3 * (m % 2):3 * (m % 2) + NTB, 0:TB]

        def blocks(tile):
            return tile.rearrange("p (b t) -> p b t", b=NTB)

        def turned(p, c):
            return p * (4 * CH - 2) + (0 if c == 0 else 4 * c - 2)

        def f32(ap):
            return ap.bitcast(F32)

        @block.sync
        def _(sp):
            def slabs(quad, a, b):
                for i in range(a, b):
                    if not (isinstance(quad, int) and quad == 0 and i < RING):
                        sp.wait_ge(w_lo, quad * 4 + (i - RING + 1))
                    sp.dma_start(wraw[:, i % RING, :], weights[quad * 4 + i]).then_inc(w_in[i % RING], 16)

            sp.dma_start(x[:, 0, :], xT[:, 0, :]).then_inc(x_in[0], 16)
            sp.dma_start(cst[:, :], consts).then_inc(c_in, 16)
            slabs(0, 0, RING)
            for k in range(1, DT):
                sp.dma_start(x[:, k, :], xT[:, k, :]).then_inc(x_in[k], 16)

            def store_state(h, b):
                sp.wait_ge(s0_upd, h * NB + (b + 1))
                sp.dma_start(state_s[b, h].rearrange("(j p) e -> p j e", j=2), s0[:, b % 4, :, :]
                             ).then_inc(s0_out[b % 4], 16)

            def load_state(h, b):
                if b >= 4:
                    sp.wait_ge(s0_out[b % 4], h * 32 + 16)
                sp.dma_start(s0[:, b % 4, :, :], state_in[b, h].rearrange("(j p) e -> p j e", j=2)
                             ).then_inc(s0_in[b % 4], 16)

            def ret_head(h, first):
                quad = h * (RET_SLABS // 4)
                if not first:
                    slabs(quad, 0, 4)
                    sp.wait_ge(ot_kept, h * (CH + 1))
                sp.dma_start(rope_tab[:, :, :], tables).then_inc(tab_in, 16)
                sp.dma_start(hmask[:, :], ret_masks[h]).then_inc(tab_in, 16)
                sp.dma_start(hc[:, :], ret_decays[h]).then_inc(tab_in, 16)
                slabs(quad, 4, 19)
                sp.wait_ge(v_turned, h * 9 + 9)
                for b in range(4):
                    load_state(h, b)
                sp.wait_ge(s_upd, h * CH + CH)
                sp.dma_start(state_p[h].rearrange("(j p) e -> p j e", j=2), s_ret[:, :, :]).then_inc(sp_out, 16)
                store_state(h, 0)
                store_state(h, 1)
                load_state(h, 4)
                store_state(h, 2)
                load_state(h, 5)
                store_state(h, 3)
                load_state(h, 6)
                load_state(h, 7)
                for b in range(4, NB):
                    store_state(h, b)
                slabs(quad, 19, RET_SLABS)

            ret_head(0, True)
            with sp.Fori(1, RH) as h:
                ret_head(h, False)

            with sp.Fori(FFN0_SLAB // 4, SWA_SLAB // 4) as quad:
                slabs(quad, 0, 4)

            sp.wait_ge(a_lo, SWA_A)
            sp.dma_start(acst[:, :], attn_consts).then_inc(ac_in, 16)
            for p in range(NPAIR):
                quad = (SWA_SLAB + p * SWA_SLABS) // 4
                slabs(quad, 0, 4)
                sp.wait_ge(slab_used, 4 * quad)
                sp.dma_start(atab[:, :, :], attn_tables).then_inc(tab_in, 16)
                slabs(quad, 4, 15)
                sp.wait_ge(qk_ready, 5 * (p + 1))
                feats = slice(2 * p * HD, (2 * p + 2) * HD)
                sp.dma_start(kc[:, :, :], cache_k[:, :, feats].rearrange("b k f -> k b f")).then_inc(kc_in, 16)
                sp.dma_start(vc[:, :, :], cache_v[:, :, feats].rearrange("b k f -> k b f")).then_inc(kc_in, 16)
                sp.dma_start(sa[0:NS, :, :], sample_mask).then_inc(kc_in, 16)
                if p == 0:
                    sp.dma_start(ks_out[:, 0:WIN - NT, :], cache_k[:, NT:WIN, :]).then_inc(swa_out, 16)
                    sp.dma_start(vs_out[:, 0:WIN - NT, :], cache_v[:, NT:WIN, :]).then_inc(swa_out, 16)
                sp.wait_ge(av_kept, 3 * (p + 1))
                sp.dma_start(vp_out[:, feats], v_a[:, CH - 1, :]).then_inc(swa_out, 16)
                for b in range(NB):
                    sp.dma_start(vs_out[b, WIN - NT:WIN, feats], v_a[NT * b:NT * b + NT, CH, :]
                                 ).then_inc(swa_out, 16)
                sp.wait_ge(nk_kept, 2 * (p + 1))
                sp.dma_start(kp_out[:, feats], nk[:, 0, :]).then_inc(swa_out, 16)
                for b in range(NB):
                    sp.dma_start(ks_out[b, WIN - NT:WIN, feats], nk[NT * b:NT * b + NT, 1, :]
                                 ).then_inc(swa_out, 16)
                slabs(quad, 15, SWA_SLABS)

            with sp.Fori(FFN1_SLAB // 4, N_SLABS // 4) as quad:
                slabs(quad, 0, 4)
            for m in range(DT):
                sp.wait_ge(mt_free, FFN1_MT + FFC * FFN_MT - DT + m + 1)
                sp.dma_start(yT[:, m, :], x[:, m, :]).then_inc(y_out, 16)
            sp.wait_ge(y_out, 16 * DT)
            sp.wait_ge(swa_out, 16 * (2 + NPAIR * (2 + 2 * NB)))
            sp.wait_ge(sp_out, 16 * RH)
            for i in range(4):
                sp.wait_ge(s0_out[i], 32 * RH)

        @block.gpsimd
        def _(pool):
            def sum_squares(phase):
                for k in range(DT):
                    n = phase * DT + k
                    pool.wait_ge(sq_done, n + 1)
                    if k == 0:
                        if phase:
                            pool.wait_ge(ssq_done, phase)
                        pool.tensor_copy(ssum[:, :], sq[:, 0, :]).then_inc(sum_done, 1)
                    else:
                        pool.wait_ge(sum_done, n)
                        pool.tensor_tensor(ssum[:, :], ssum[:, :], sq[:, k % 2, :], ALU.add).then_inc(sum_done, 1)

            sum_squares(0)
            sum_squares(1)
            sum_squares(2)
            for i in range(5 * NPAIR):
                if i % 5 == 0:
                    pool.wait_ge(tab_in, 48 * RH + 16 * (i // 5 + 1))
                pool.wait_ge(zr_in, 64 * (i + 1))
                pool.tensor_tensor(zr[:, :], zr[:, :], atab[:, 1, :], ALU.mult).then_inc(zs_done, 1)
            sum_squares(3)

        @block.scalar
        def _(act):
            def split(quad, a, b, last=N_SLABS):
                for i in range(a + LEAD, b + LEAD):
                    if isinstance(quad, int) and 4 * quad + i >= last:
                        continue
                    act.wait_ge(w_in[i % RING], 16 * (quad + i // RING + 1))
                    if not (isinstance(quad, int) and 4 * quad + i < RING):
                        act.wait_ge(slab_used, quad * 4 + (i - RING + 1))
                    act.copy(whi[:, i % RING, :], wraw[:, i % RING, :]).then_inc(w_hi, 1)

            def gain_x(k, phase):
                g = C_GAIN + phase * DT + k
                act.mul(hhi[:, k, :], x[:, k, :], cst[:, g:g + 1]).then_inc(h_hi, 1)
                n = phase * DT + k
                if n >= 2:
                    act.wait_ge(sum_done, n - 1)
                act.activation(sq[:, k % 2, :], x[:, k, :], ACT.Square).then_inc(sq_done, 1)

            def norm(phase):
                act.wait_ge(ssq_done, phase + 1)
                if phase:
                    act.wait_ge(rst_done, phase)
                act.activation(blocks(rst[:, :]), ps[:, 3:6, 0:TB], ACT.Sqrt, bias=eps, scale=1.0 / D
                               ).then_inc(rst_sq, 1)

            split(0, -LEAD, 0)
            act.wait_ge(c_in, 16)
            for k in range(DT):
                act.wait_ge(x_in[k], 16)
                gain_x(k, 0)

            def keep_v(h, e):
                for half in range(2):
                    act.wait_ge(v_turned, h * 9 + (2 * e + half + 1))
                    act.copy(v_tok[:, 4 * half:4 * half + 4, e * P:(e + 1) * P],
                             ps[:, 6 + half, :].rearrange("p (c f) -> p c f", c=4)).then_inc(v_kept, 1)

            def keep_o(h, c):
                rows = NS if c == CH else P
                act.wait_ge(ot_done, h * (CH + 1) + (c + 1))
                act.copy(o_t[:, :, c * P:c * P + rows],
                         ps[:, 4, :].rearrange("p (e t) -> p e t", e=4)[:, :, 0:rows]).then_inc(ot_kept, 1)

            def norm_o(h, c):
                i = h * (CH + 1) + c
                rows = NS if c == CH else P
                qdec = hc[0:rows, H_QDS:H_QDS + 1] if c == CH else hc[0:rows, H_QDEC:H_QDEC + 1]
                bank = 2 + c % 2
                act.wait_ge(o_done, i + 1)
                if not (isinstance(h, int) and i == 0):
                    act.wait_ge(ot_done, i)
                act.activation(o_tok[0:rows, :], ps[0:rows, bank, :], ACT.Square, scale=qdec,
                               accum_out=stat[0:rows, 0:1]).then_inc(ss_done, 1)
                act.wait_ge(ss_done, i + 1)
                act.activation(stat[0:rows, 1:2], stat[0:rows, 0:1], ACT.Sqrt, bias=eps[0:rows, :], scale=1.0 / DV
                               ).then_inc(rs_done, 1)
                if c:
                    keep_o(h, c - 1)
                act.wait_ge(rr_done, i + 1)
                act.mul(o_tok[0:rows, :], ps[0:rows, bank, :], stat[0:rows, 3:4]).then_inc(o_kept, 1)

            def ret_head(h, first, last):
                quad = h * (RET_SLABS // 4)
                mt = h * RET_MT
                split(quad, 0, 2)
                if first:
                    norm(0)
                split(quad, 2, 8)
                for e in range(4):
                    split(quad, 8 + 2 * e, 10 + 2 * e)
                    if e:
                        keep_v(h, e - 1)
                keep_v(h, 3)
                act.wait_ge(v_turned, h * 9 + 9)
                act.copy(v_tok[0:NS, CH, :], ps[0:NS, 4, :]).then_inc(v_kept, 1)
                for c in range(CH + 1):
                    norm_o(h, c)
                keep_o(h, CH)
                for m in range(4):
                    split(quad, 16 + 2 * m, 18 + 2 * m)
                    act.wait_ge(mt_free, mt + (8 + m + 1))
                    act.activation(qk[:, 2 + m % 2, :], qk[:, m % 2, :], ACT.Silu).then_inc(g_silu, 1)
                    act.wait_ge(g_of, h * 4 + (m + 1))
                    act.copy(ahi[:, m, :], qk[:, m % 2, :]).then_inc(a_hi, 1)
                for m in range(DT):
                    split(quad, 24 + m, 25 + m)
                    if last:
                        act.wait_ge(mt_free, mt + (12 + m + 1))
                        gain_x(m, 1)

            ret_head(0, True, False)
            with act.Fori(1, RH - 1) as h:
                ret_head(h, False, False)
            ret_head(RH - 1, False, True)

            def ffn(c, slab0, mt0, a0, up0, phase, next_phase):
                quad = c * (FFN_SLABS // 4) + slab0 // 4
                for m in range(4):
                    up = c * 4 + (up0 + m)
                    split(quad, 2 * m, 2 * m + 2)
                    if m == 0 and phase is not None:
                        norm(phase)
                    act.wait_ge(mt_free, c * FFN_MT + (mt0 + m + 1))
                    act.wait_ge(a_lo, c * 4 + (a0 + m - 1))
                    act.activation(a2[:, m % 2, :], relu[:, m % 2, :], ACT.Square).then_inc(a2_done, 1)
                    act.wait_ge(a2_done, up + 1)
                    act.copy(ahi[:, m, :], a2[:, m % 2, :]).then_inc(a_hi, 1)
                for m in range(DT):
                    split(quad, 8 + m, 9 + m)
                    if next_phase is not None:
                        act.wait_ge(mt_free, c * FFN_MT + (mt0 + 4 + m + 1))
                        gain_x(m, next_phase)

            def mlp(slab0, mt0, a0, up0, phase, next_phase):
                ffn(0, slab0, mt0, a0, up0, phase, None)
                with act.Fori(1, FFC - 1) as c:
                    ffn(c, slab0, mt0, a0, up0, None, None)
                ffn(FFC - 1, slab0, mt0, a0, up0, None, next_phase)

            mlp(FFN0_SLAB, FFN0_MT, FFN0_A, 0, 1, 2)

            def head_roots(p, m, t):
                i = 5 * p + m
                act.wait_ge(hsum_done, 3 * i + t + 1)
                if t == 0 and i:
                    act.wait_ge(qk_ready, i)
                act.activation(nr[:, t * TB:(t + 1) * TB], ps[:, 6 + t % 2, 0:TB], ACT.Sqrt, bias=eps,
                               scale=1.0 / HD).then_inc(hroot_done, 1)

            def gain_head(p, m):
                i = 5 * p + m
                gain = C_QN if m < 4 else C_KN
                act.wait_ge(mt_free, SWA_MT0 + p * SWA_MT + m + 1)
                act.activation(zz[:, :], z_a[:, m % 2, :], ACT.Square).then_inc(zz_done, 1)
                if i:
                    act.wait_ge(qk_ready, i)
                act.mul(zg[:, :], z_a[:, m % 2, :], cst[:, gain:gain + 1]).then_inc(zg_done, 1)
                act.wait_ge(zg_done, i + 1)
                for half in range(0, P, HD):
                    for a, b in ((0, HD // 2), (HD // 2, 0)):
                        act.dma_start(zr[half + a:half + a + HD // 2, :], zg[half + b:half + b + HD // 2, :]
                                      ).then_inc(zr_in, 16)

            def softmax_block(u, c):
                slot = u % 2
                lo = P if c == 0 else 0
                act.wait_ge(m_ready, u + 1)
                st = 32 + 24 * slot
                for j in range(PH):
                    act.activation(p_a[:, slot, j, lo:], p_a[:, slot, j, lo:], ACT.Exp,
                                   bias=ast[:, st + j:st + j + 1], accum_out=ast[:, st + 8 + j:st + 9 + j]
                                   ).then_inc(p_done, 1)
                act.activation(ast[:, st + 16:st + 24], ast[:, st + 16:st + 24], ACT.Exp).then_inc(p_done, 1)

            def keep_block(u, c, p):
                for g in (1, 3):
                    act.wait_ge(pt_done, turned(p, c) + (g // 2 if c == 0 else g) + 1)
                    if u - 2 >= 8 * p and g == 1:
                        act.wait_ge(pv_done, u - 1)
                    act.copy(pt_a[:, u % 2, g, :], ps[:, 5, :]).then_inc(pt_kept_s, 1)
                if c:
                    keep_out(u - 1, c - 1)

            def keep_out(u, c):
                act.wait_ge(oct_done, u + 1)
                act.copy(q_a[:, :, c * P:(c + 1) * P], ps[:, 7, :].rearrange("p (r t) -> p r t", r=GR)
                         ).then_inc(oct_kept, 1)

            def pair(p):
                quad = (SWA_SLAB + p * SWA_SLABS) // 4
                for m in range(6):
                    split(quad, 2 * m, 2 * m + 1)
                    if m == 0:
                        split(quad, 1, 2)
                        if p == 0:
                            norm(2)
                    else:
                        head_roots(p, m - 1, 0)
                        head_roots(p, m - 1, 1)
                        split(quad, 2 * m + 1, 2 * m + 2)
                        head_roots(p, m - 1, 2)
                    if m < 5:
                        gain_head(p, m)
                if p:
                    act.wait_ge(swa_out, 16 * (2 + p * (2 + 2 * NB)))
                for half in range(2):
                    act.wait_ge(av_turned, 3 * p + half + 1)
                    act.copy(v_a[:, 4 * half:4 * half + 4, :],
                             ps[:, 6 + half, :].rearrange("p (c f) -> p c f", c=4)).then_inc(av_kept, 1)
                act.wait_ge(av_turned, 3 * p + 3)
                act.copy(v_a[0:NS, CH, :], ps[0:NS, 4, 0:P]).then_inc(av_kept, 1)
                act.wait_ge(nk_done, p + 1)
                act.copy(nk[:, 0, :], ps[:, 5, 0:P]).then_inc(nk_kept, 1)
                act.copy(nk[0:NS, 1, :], ps[0:NS, 5, P:2 * P]).then_inc(nk_kept, 1)
                for half in range(2):
                    act.wait_ge(kct_done, 2 * p + half + 1)
                    act.copy(kct[:, 4 * half:4 * half + 4, :],
                             ps[:, 3 + half, :].rearrange("p (b f) -> p b f", b=4)).then_inc(kct_kept, 1)
                act.wait_ge(sa_max, p + 1)
                for b in range(NB):
                    act.activation(sa[0:NS, b, :], sa[0:NS, b, :], ACT.Exp, bias=ast[0:NS, 8 + b:9 + b],
                                   accum_out=ast[0:NS, 16 + b:17 + b]).then_inc(sa_exp, 1)
                act.activation(ast[0:NS, 24:32], ast[0:NS, 24:32], ACT.Exp).then_inc(sa_exp, 1)
                act.wait_ge(pts_done, 2 * (p + 1))
                act.copy(pts[:, 0, :, :], ps[:, 3, 0:NB * NS].rearrange("p (b n) -> p b n", b=NB)
                         ).then_inc(pts_kept, 1)
                act.copy(pts[0:NS, 1, :, :], ps[0:NS, 4, 0:NB * NS].rearrange("p (b n) -> p b n", b=NB)
                         ).then_inc(pts_kept, 1)
                for c in range(CH):
                    u = p * CH + c
                    softmax_block(u, c)
                    keep_block(u, c, p)
                keep_out(p * CH + CH - 1, CH - 1)
                for r in range(GR):
                    act.wait_ge(oct_kept, (p + 1) * CH)
                    act.wait_ge(os_kept, 2 * (p + 1))
                    act.copy(ahi[:, r, :], q_a[:, r, :]).then_inc(a_hi, 1)
                split(quad, 12, 12)
                for m in range(DT):
                    split(quad, 12 + m, 13 + m)
                    if p == NPAIR - 1:
                        act.wait_ge(mt_free, SWA_MT0 + p * SWA_MT + 6 + m + 1)
                        gain_x(m, 3)

            for p in range(NPAIR):
                pair(p)
            mlp(FFN1_SLAB, FFN1_MT, FFN1_A, FFC * 4, 3, None)

        @block.vector
        def _(dve):
            def split(quad, a, b, last=N_SLABS):
                for i in range(a + LEAD, b + LEAD):
                    if isinstance(quad, int) and 4 * quad + i >= last:
                        continue
                    dve.wait_ge(w_hi, quad * 4 + (i + 1))
                    dve.tensor_tensor(wlo[:, i % RING, :], wraw[:, i % RING, :], f32(whi[:, i % RING, :]),
                                      ALU.subtract).then_inc(w_lo, 1)

            def gain_x(k, phase):
                g = C_GAIN + phase * DT + k
                dve.wait_ge(h_hi, phase * DT + k + 1)
                dve.scalar_tensor_tensor(out=hlo[:, k, :], in0=x[:, k, :], scalar=cst[:, g:g + 1],
                                         in1=f32(hhi[:, k, :]), op0=ALU.mult, op1=ALU.subtract).then_inc(h_lo, 1)

            def norm(phase):
                dve.wait_ge(rst_sq, phase + 1)
                dve.reciprocal(rst[:, :], rst[:, :]).then_inc(rst_done, 1)
                dve.wait_ge(rst_done, phase + 1)

            def read_normed(m, slab_end, out):
                dve.wait_ge(slab_used, slab_end)
                dve.tensor_tensor(blocks(out), bank_set(m), blocks(rst[:, :]), ALU.mult).then_inc(mt_free, 1)

            def add_x(k, m, slab_end):
                dve.wait_ge(slab_used, slab_end)
                dve.tensor_tensor(blocks(x[:, k, :]), bank_set(m), blocks(x[:, k, :]), ALU.add).then_inc(mt_free, 1)

            split(0, -LEAD, 0)
            for k in range(DT):
                gain_x(k, 0)

            N_SEQ = 12 + CH + 1 + 1

            def rope(h, j, mt):
                cos, sin = rope_tab[:, 0, :], rope_tab[:, 1, :]
                if j == 0:
                    dve.wait_ge(tab_in, h * 48 + 48)
                dve.wait_ge(mt_free, mt + (2 * j + 2))
                dve.tensor_tensor(tmp[:, 2, :], tmp[:, 1, :], sin, ALU.mult).then_inc(dve_seq, 1)
                dve.tensor_tensor(tmp[:, 3, :], tmp[:, 0, :], sin, ALU.mult).then_inc(dve_seq, 1)
                dve.tensor_tensor(qk[:, 2 * j, :], tmp[:, 0, :], cos, ALU.mult).then_inc(dve_seq, 1)
                dve.tensor_tensor(qk[:, 2 * j + 1, :], tmp[:, 1, :], cos, ALU.mult).then_inc(dve_seq, 1)
                dve.wait_ge(dve_seq, h * N_SEQ + (6 * j + 4))
                dve.tensor_tensor(qk[:, 2 * j, :], qk[:, 2 * j, :], tmp[:, 2, :], ALU.subtract).then_inc(dve_seq, 1)
                dve.tensor_tensor(qk[:, 2 * j + 1, :], qk[:, 2 * j + 1, :], tmp[:, 3, :], ALU.add
                                  ).then_inc(dve_seq, 1)

            def mask_scores(h, c):
                i = h * (CH + 1) + c
                rows = NS if c == CH else P
                mask = hmask[0:rows, P:P + NS] if c == CH else hmask[:, 0:P]
                dve.wait_ge(sc_done, i + 1)
                if c >= 2:
                    dve.wait_ge(o_done, i - 1)
                dve.tensor_tensor(sc_t[0:rows, c % 2, 0:rows], ps[0:rows, 6 + c % 2, 0:rows], mask, ALU.mult).then_inc(sc_kept, 1)

            def decay_keys(h, c):
                i = h * (CH + 1) + c
                rows = NS if c == CH else P
                kdec = hc[0:rows, H_KDS:H_KDS + 1] if c == CH else hc[0:rows, H_KDEC:H_KDEC + 1]
                dve.wait_ge(kt_done, i + 1)
                if c >= 2 and c < CH:
                    dve.wait_ge(st_done, h * CH + (c - 1))
                if c == CH:
                    dve.wait_ge(st_done, h * CH + (CH - 1))
                dve.tensor_scalar(k_tok[0:rows, c % 2, :], ps[0:rows, 5, 0:DK], kdec, None, ALU.mult
                                  ).then_inc(kt_kept, 1)

            def update_state(h, c):
                dve.wait_ge(st_done, h * CH + (c + 1))
                if c == 0:
                    if not isinstance(h, int) or h:
                        dve.wait_ge(sp_out, h * 16)
                    dve.tensor_copy(s_ret[:, :, :], ps[:, 0:2, :]).then_inc(s_upd, 1)
                else:
                    dve.wait_ge(s_upd, h * CH + c)
                    dve.scalar_tensor_tensor(out=s_ret[:, :, :], in0=s_ret[:, :, :],
                                             scalar=hc[:, H_CDEC:H_CDEC + 1], in1=ps[:, 0:2, :],
                                             op0=ALU.mult, op1=ALU.add).then_inc(s_upd, 1)

            def inverse_rms(h, c):
                i = h * (CH + 1) + c
                rows = NS if c == CH else P
                qdec = hc[0:rows, H_QDS:H_QDS + 1] if c == CH else hc[0:rows, H_QDEC:H_QDEC + 1]
                dve.wait_ge(rs_done, i + 1)
                dve.reciprocal(stat[0:rows, 2:3], stat[0:rows, 1:2]).then_inc(dve_seq, 1)
                dve.wait_ge(dve_seq, h * N_SEQ + (12 + c + 1 if c < CH else N_SEQ))
                dve.tensor_tensor(stat[0:rows, 3:4], stat[0:rows, 2:3], qdec, ALU.mult).then_inc(rr_done, 1)

            def ret_head(h, first, last):
                quad = h * (RET_SLABS // 4)
                n = h * RET_SLABS
                mt = h * RET_MT
                for m in range(4):
                    split(quad, 2 * m, 2 * m + 2)
                    if first and m == 0:
                        norm(0)
                    read_normed(m, n + (2 * m + 2), tmp[:, m % 2, :])
                    if m % 2:
                        rope(h, m // 2, mt)
                for m in range(4, 8):
                    split(quad, 2 * m, 2 * m + 2)
                    read_normed(m, n + (2 * m + 2), tmp[:, m - 4, :])
                mask_scores(h, 0)
                decay_keys(h, 0)
                for c in range(CH):
                    update_state(h, c)
                    mask_scores(h, c + 1)
                    decay_keys(h, c + 1)
                    inverse_rms(h, c)
                dve.wait_ge(o_done, h * (CH + 1) + CH)
                dve.memset(q_sel[:, :, :, :], 0.0).then_inc(dve_seq, 1)
                dve.wait_ge(kt_kept, (h + 1) * (CH + 1))
                dve.tensor_tensor(k_sel[0:NS, :, :], k_tok[0:NS, 0, :].unsqueeze(1).to_broadcast([NS, NB, DK]),
                                  cst[0:NS, C_BM:C_BM + NB].unsqueeze(2).to_broadcast([NS, NB, DK]), ALU.mult
                                  ).then_inc(sel_ready, 1)
                dve.wait_ge(dve_seq, h * N_SEQ + (12 + CH + 1))
                for b in range(NB):
                    dve.tensor_copy(q_sel[:, :, b, NT * b:NT * b + NT], qk[:, 0:2, SEQ + NT * b:SEQ + NT * b + NT]
                                    ).then_inc(sel_ready, 1)
                for b in range(NB):
                    dve.wait_ge(sts_done, h * NB + (b + 1))
                    bank = 6 * (b % 2)
                    dve.scalar_tensor_tensor(out=s0[:, b % 4, :, :], in0=s0[:, b % 4, :, :],
                                             scalar=hc[:, H_CDS:H_CDS + 1], in1=ps[:, bank:bank + 2, :],
                                             op0=ALU.mult, op1=ALU.add).then_inc(s0_upd, 1)
                inverse_rms(h, CH)

                def gate(m):
                    dve.wait_ge(g_silu, h * 4 + (m + 1))
                    dve.wait_ge(ot_kept, (h + 1) * (CH + 1))
                    dve.tensor_tensor(qk[:, m % 2, :], qk[:, 2 + m % 2, :], o_t[:, m, :], ALU.mult).then_inc(g_of, 1)

                def gate_lo(m):
                    if m == 0:
                        for i in range(4):
                            dve.wait_ge(s0_out[i], h * 32 + 32)
                    dve.wait_ge(a_hi, h * 4 + (m + 1))
                    dve.tensor_tensor(alo[:, m, :], qk[:, m % 2, :], f32(ahi[:, m, :]), ALU.subtract
                                      ).then_inc(a_lo, 1)

                for m in range(4):
                    split(quad, 16 + 2 * m, 18 + 2 * m)
                    read_normed(8 + m, n + (18 + 2 * m), qk[:, m % 2, :])
                    gate(m)
                    gate_lo(m)
                for m in range(DT):
                    split(quad, 24 + m, 25 + m)
                    add_x(m, 12 + m, n + (25 + m))
                    if last and m:
                        gain_x(m - 1, 1)
                if last:
                    gain_x(DT - 1, 1)

            ret_head(0, True, False)
            with dve.Fori(1, RH - 1) as h:
                ret_head(h, False, False)
            ret_head(RH - 1, False, True)

            def ffn(c, slab0, mt0, a0, up0, phase, next_phase):
                quad = c * (FFN_SLABS // 4) + slab0 // 4
                n = c * FFN_SLABS + slab0

                def squares_lo(m):
                    dve.wait_ge(a_hi, c * 4 + (a0 + m + 1))
                    dve.tensor_tensor(alo[:, m, :], a2[:, m % 2, :], f32(ahi[:, m, :]), ALU.subtract
                                      ).then_inc(a_lo, 1)

                for m in range(4):
                    split(quad, 2 * m, 2 * m + 2)
                    if m == 0 and phase is not None:
                        norm(phase)
                    up = c * 4 + (up0 + m)
                    dve.wait_ge(slab_used, n + (2 * m + 2))
                    if not (isinstance(up, int) and up < 2):
                        dve.wait_ge(a2_done, up - 1)
                    dve.scalar_tensor_tensor(out=blocks(relu[:, m % 2, :]), in0=bank_set(m), scalar=0.0,
                                             in1=blocks(rst[:, :]), op0=ALU.max, op1=ALU.mult).then_inc(mt_free, 1)
                    if m:
                        squares_lo(m - 1)
                for m in range(DT):
                    split(quad, 8 + m, 9 + m)
                    if m == 0:
                        squares_lo(3)
                    add_x(m, 4 + m, n + (9 + m))
                    if next_phase is not None and m:
                        gain_x(m - 1, next_phase)
                if next_phase is not None:
                    gain_x(DT - 1, next_phase)

            def mlp(slab0, mt0, a0, up0, phase, next_phase):
                ffn(0, slab0, mt0, a0, up0, phase, None)
                with dve.Fori(1, FFC - 1) as c:
                    ffn(c, slab0, mt0, a0, up0, None, None)
                ffn(FFC - 1, slab0, mt0, a0, up0, None, next_phase)

            mlp(FFN0_SLAB, FFN0_MT, FFN0_A, 0, 1, 2)

            seq = [RH * N_SEQ]

            def link(ins):
                seq[0] += 1
                ins.then_inc(dve_seq, 1)
                dve.wait_ge(dve_seq, seq[0])

            def rope_head(p, m):
                i = 5 * p + m
                dve.wait_ge(hroot_done, 3 * i + 3)
                link(dve.reciprocal(nr[:, :], nr[:, :]))
                dve.wait_ge(zg_done, i + 1)
                if m == 0:
                    dve.wait_ge(tab_in, 48 * RH + 16 * (p + 1))
                link(dve.tensor_tensor(z_a[:, m % 2, :], zg[:, :], atab[:, 0, :], ALU.mult))
                dve.wait_ge(zs_done, i + 1)
                link(dve.tensor_tensor(z_a[:, m % 2, :], z_a[:, m % 2, :], zr[:, :], ALU.add))
                dve.tensor_tensor(q_a[:, m, :] if m < GR else k_a[:, :], z_a[:, m % 2, :], nr[:, :], ALU.mult
                                  ).then_inc(qk_ready, 1)

            def scale_scores(u, c, p):
                slot = u % 2
                lo = P if c == 0 else 0
                st = 32 + 24 * slot
                dve.wait_ge(s_done, u + 1)
                if c >= 2:
                    dve.wait_ge(pt_done, turned(p, c - 1))
                if c == 0:
                    dve.wait_ge(os_done, p + 1)
                    dve.wait_ge(swa_out, 16 * (2 + (p + 1) * (2 + 2 * NB)))
                scores = ps[:, 0:4, :].rearrange("p k (j n) -> p (k j) n", j=2)
                mask = acst[:, A_MASK + lo:A_MASK + 2 * P].unsqueeze(1).to_broadcast([P, PH, 2 * P - lo])
                dve.scalar_tensor_tensor(out=p_a[:, slot, :, lo:], in0=scores[:, :, lo:], scalar=HD ** -0.5,
                                         in1=mask, op0=ALU.mult, op1=ALU.add).then_inc(s_kept, 1)
                dve.wait_ge(s_kept, u + 1)
                link(dve.tensor_reduce(ast[:, 0:8], p_a[:, slot, :, lo:], AX.X, ALU.max))
                sink = cst[:, C_SINK + PH * p:C_SINK + PH * (p + 1)]
                link(dve.tensor_tensor(ast[:, 8:16], ast[:, 0:8], sink, ALU.max))
                link(dve.tensor_scalar(ast[:, st:st + 8], ast[:, 8:16], -1.0, None, ALU.mult))
                dve.tensor_tensor(ast[:, st + 16:st + 24], ast[:, st:st + 8], sink, ALU.add).then_inc(m_ready, 1)

            def keep_block(u, c, p):
                if c:
                    for g in (0, 2):
                        dve.wait_ge(pt_done, turned(p, c) + g + 1)
                        if c >= 2 and g == 0:
                            dve.wait_ge(pv_done, u - 1)
                        dve.tensor_copy(pt_a[:, u % 2, g, :], ps[:, 4, :]).then_inc(pt_kept_v, 1)
                st = 32 + 24 * (u % 2)
                dve.wait_ge(p_done, 9 * (u + 1))
                link(dve.tensor_tensor(ast[:, st + 8:st + 16], ast[:, st + 8:st + 16], ast[:, st + 16:st + 24], ALU.add))
                link(dve.reciprocal(ast[:, 24:32], ast[:, st + 8:st + 16]))
                dve.wait_ge(pv_done, u + 1)
                if u:
                    dve.wait_ge(oct_done, u)
                inv = ast[:, 24:32].rearrange("p (s r) -> p r s", s=2).unsqueeze(3).to_broadcast([P, GR, 2, HD])
                dve.tensor_tensor(oc[:, :].rearrange("p (r s d) -> p r s d", r=GR, s=2),
                                  ps[:, 6, :].rearrange("p (r s d) -> p r s d", r=GR, s=2), inv, ALU.mult
                                  ).then_inc(oc_kept, 1)

            def sample(p):
                link(dve.memset(q_bd[:, :, :], 0.0))
                for s in range(2):
                    part = slice(HD * s, HD * (s + 1))
                    dve.tensor_copy(q_bd[part, :, 16 * s:16 * s + 16].rearrange("p b (r t) -> p r b t", r=GR),
                                    q_a[part, :, SEQ:TOK].rearrange("p r (b t) -> p r b t", b=NB)
                                    ).then_inc(qbd_ready, 1)
                dve.wait_ge(kc_in, 48 * (p + 1))
                dve.wait_ge(sas_done, p + 1)
                for k in range(3):
                    nb = min(3, NB - 3 * k)
                    view = ps[0:NS, k, 0:nb * KEYS].rearrange("p (b n) -> p b n", b=nb)
                    ins = dve.scalar_tensor_tensor(out=sa[0:NS, 3 * k:3 * k + nb, :], in0=view, scalar=HD ** -0.5,
                                                   in1=sa[0:NS, 3 * k:3 * k + nb, :], op0=ALU.mult, op1=ALU.add)
                    link(ins)
                sink = cst[0:NS, C_SINKS + p:C_SINKS + p + 1]
                link(dve.tensor_reduce(ast[0:NS, 0:8], sa[0:NS, :, :], AX.X, ALU.max))
                link(dve.tensor_scalar(ast[0:NS, 8:16], ast[0:NS, 0:8], sink, -1.0, ALU.max, ALU.mult))
                dve.tensor_scalar(ast[0:NS, 24:32], ast[0:NS, 8:16], sink, None, ALU.add).then_inc(sa_max, 1)
                dve.wait_ge(sa_exp, 9 * (p + 1))
                link(dve.tensor_tensor(ast[0:NS, 16:24], ast[0:NS, 16:24], ast[0:NS, 24:32], ALU.add))
                link(dve.reciprocal(ast[0:NS, 0:8], ast[0:NS, 16:24]))
                dve.tensor_tensor(sa[0:NS, :, :], sa[0:NS, :, :],
                                  ast[0:NS, 0:8].unsqueeze(2).to_broadcast([NS, NB, KEYS]), ALU.mult
                                  ).then_inc(sa_ready, 1)
                dve.wait_ge(os_done, p + 1)
                for s in range(2):
                    part = slice(HD * s, HD * (s + 1))
                    view = ps[part, 5, 0:NB * NS].rearrange("p (b n) -> p b n", b=NB)[:, :, 16 * s:16 * s + 16]
                    dve.tensor_copy(q_a[part, :, SEQ:TOK].rearrange("p r (b t) -> p r b t", b=NB),
                                    view.rearrange("p b (r t) -> p r b t", r=GR)).then_inc(os_kept, 1)

            def pair(p):
                n = SWA_SLAB + p * SWA_SLABS
                quad = n // 4
                for m in range(6):
                    split(quad, 2 * m, 2 * m + 2)
                    if p == 0 and m == 0:
                        norm(2)
                    read_normed(m, n + 2 * m + 2, z_a[:, m % 2, :] if m < 5 else vt_a[:, :])
                    if m:
                        rope_head(p, m - 1)
                sample(p)
                scale_scores(p * CH, 0, p)
                for c in range(CH):
                    if c + 1 < CH:
                        scale_scores(p * CH + c + 1, c + 1, p)
                    keep_block(p * CH + c, c, p)
                for r in range(GR):
                    dve.wait_ge(a_hi, SWA_A + 4 * p + r + 1)
                    dve.tensor_tensor(alo[:, r, :], q_a[:, r, :], f32(ahi[:, r, :]), ALU.subtract).then_inc(a_lo, 1)
                for m in range(DT):
                    split(quad, 12 + m, 13 + m)
                    add_x(m, 6 + m, n + 13 + m)
                    if p == NPAIR - 1 and m:
                        gain_x(m - 1, 3)
                if p == NPAIR - 1:
                    gain_x(DT - 1, 3)

            dve.wait_ge(ac_in, 16)
            for p in range(NPAIR):
                pair(p)
            mlp(FFN1_SLAB, FFN1_MT, FFN1_A, FFC * 4, 3, None)

        @block.tensor
        def _(pe):
            def product(m, mt, quad, i0, n_slabs, hi, lo, k_ready=None, between=None):
                for s in range(n_slabs):
                    i = i0 + s
                    pe.wait_ge(w_lo, quad * 4 + (i + 1))
                    if s == 0 and not (isinstance(mt, int) and mt < 2):
                        pe.wait_ge(mt_free, mt - 1)
                    for k in range(KG):
                        if k_ready is not None:
                            pe.wait_ge(k_ready[0], k_ready[1] + (s * KG + k + 1))
                        w = slice(k * P, (k + 1) * P)
                        passes = ((whi, hi), (whi, lo), (wlo, hi))
                        for j, (a, b) in enumerate(passes):
                            for t in range(NTB):
                                mm = pe.matmul(ps[:, 3 * (m % 2) + t, 0:TB], a[:, i % RING, w],
                                               b[:, s * KG + k, t * TB:(t + 1) * TB],
                                               start=(s == 0 and k == 0 and j == 0),
                                               stop=(s == n_slabs - 1 and k == KG - 1 and j == 2))
                    mm.then_inc(slab_used, 1)
                    if between is not None:
                        between(s)

            def norm(phase, mt):
                pe.wait_ge(sum_done, (phase + 1) * DT)
                if phase:
                    pe.wait_ge(mt_free, mt - 1)
                for t in range(NTB):
                    mm = pe.matmul(ps[:, 3 + t, 0:TB], ones, ssum[:, t * TB:(t + 1) * TB], start=True, stop=True)
                mm.then_inc(ssq_done, 1)
                pe.wait_ge(rst_sq, phase + 1)

            def turn_v(h, e):
                pe.wait_ge(mt_free, h * RET_MT + (4 + e + 1))
                for half in range(2):
                    if e:
                        pe.wait_ge(v_kept, h * 9 + (2 * e + half - 1))
                    for c in range(4):
                        t = (4 * half + c) * P
                        mm = pe.transpose(ps[:, 6 + half, c * P:(c + 1) * P], tmp[:, e, t:t + P], ident)
                    mm.then_inc(v_turned, 1)

            def scores(h, c):
                i = h * (CH + 1) + c
                rows = NS if c == CH else P
                tok = slice(c * P, c * P + rows)
                if c < 2:
                    pe.wait_ge(v_kept, h * 9 + 8)
                else:
                    pe.wait_ge(sc_kept, i - 1)
                for j in range(2):
                    mm = pe.matmul(ps[0:rows, 6 + c % 2, 0:rows], qk[:, 2 + j, tok], qk[:, j, tok],
                                   start=(j == 0), stop=(j == 1))
                mm.then_inc(sc_done, 1)

            def turn_k(h, c):
                i = h * (CH + 1) + c
                rows = NS if c == CH else P
                if not (isinstance(h, int) and i == 0):
                    pe.wait_ge(kt_kept, i)
                for j in range(2):
                    mm = pe.transpose(ps[0:rows, 5, j * P:(j + 1) * P], qk[:, 2 + j, c * P:c * P + rows], ident)
                mm.then_inc(kt_done, 1)

            def turn_o(h, c):
                i = h * (CH + 1) + c
                pe.wait_ge(o_kept, i + 1)
                if c == 0:
                    pe.wait_ge(v_kept, h * 9 + 9)
                else:
                    pe.wait_ge(ot_kept, i)
                for e in range(4):
                    mm = pe.transpose(ps[:, 4, e * P:(e + 1) * P], o_tok[:, e * P:(e + 1) * P], ident)
                mm.then_inc(ot_done, 1)

            def chunk(h, c):
                i = h * (CH + 1) + c
                tok = slice(c * P, (c + 1) * P)
                bank = 2 + c % 2
                if c >= 2:
                    pe.wait_ge(o_kept, i - 1)
                if c:
                    pe.wait_ge(s_upd, h * CH + c)
                    for j in range(2):
                        pe.matmul(ps[:, bank, :], qk[:, j, tok], s_ret[:, j, :], start=(j == 0), stop=False)
                pe.wait_ge(kt_kept, i + 1)
                for j in range(2):
                    mm = pe.matmul(ps[:, j, :], k_tok[:, c % 2, j * P:(j + 1) * P], v_tok[:, c, :],
                                   start=True, stop=True)
                mm.then_inc(st_done, 1)
                scores(h, c + 1)
                turn_k(h, c + 1)
                pe.wait_ge(sc_kept, i + 1)
                pe.matmul(ps[:, bank, :], sc_t[:, c % 2, :], v_tok[:, c, :], start=(c == 0), stop=True
                          ).then_inc(o_done, 1)
                if c:
                    turn_o(h, c - 1)

            def sample_heads(h):
                i = h * (CH + 1) + CH
                pe.wait_ge(sel_ready, (h + 1) * (NB + 1))
                pe.wait_ge(o_kept, i - 1)
                pe.wait_ge(sc_kept, i + 1)
                for b in range(NB):
                    pe.wait_ge(s0_in[b % 4], h * 32 + 16 * (b // 4 + 1))
                    for j in range(2):
                        pe.matmul(ps[0:NS, 2, :], q_sel[:, j, b, :], s0[:, b % 4, j, :],
                                  start=(b == 0 and j == 0), stop=False)
                    bank = 6 * (b % 2)
                    if b == 0:
                        pe.wait_ge(s_upd, (h + 1) * CH)
                    elif b >= 2:
                        pe.wait_ge(s0_upd, h * NB + (b - 1))
                    for j in range(2):
                        mm = pe.matmul(ps[:, bank + j, :], k_sel[0:NS, b, j * P:(j + 1) * P], v_tok[0:NS, CH, :],
                                       start=True, stop=True)
                    mm.then_inc(sts_done, 1)
                pe.matmul(ps[0:NS, 2, :], sc_t[0:NS, 0, 0:NS], v_tok[0:NS, CH, :], start=False, stop=True
                          ).then_inc(o_done, 1)
                turn_o(h, CH)

            def ret_head(h, first):
                quad = h * (RET_SLABS // 4)
                mt = h * RET_MT
                for m in range(8):
                    product(m, mt + m, quad, 2 * m, 2, hhi, hlo, (h_lo, 0) if first and m == 0 else None)
                    if first and m == 0:
                        norm(0, 0)
                    if m > 4:
                        turn_v(h, m - 5)
                pe.wait_ge(mt_free, mt + 8)
                turn_v(h, 3)
                for e in range(4):
                    mm = pe.transpose(ps[0:NS, 4, e * P:(e + 1) * P], tmp[:, e, SEQ:TOK], ident)
                mm.then_inc(v_turned, 1)
                scores(h, 0)
                turn_k(h, 0)
                for c in range(CH):
                    chunk(h, c)
                turn_o(h, CH - 1)
                sample_heads(h)
                for m in range(8, 12):
                    if m == 8:
                        pe.wait_ge(s0_upd, (h + 1) * NB)
                        pe.wait_ge(ot_kept, (h + 1) * (CH + 1))
                    product(m, mt + m, quad, 2 * m, 2, hhi, hlo)
                for m in range(DT):
                    product(12 + m, mt + (12 + m), quad, 24 + m, 1, ahi, alo, (a_lo, h * 4) if m == 0 else None)

            ret_head(0, True)
            with pe.Fori(1, RH) as h:
                ret_head(h, False)

            def ffn(c, slab0, mt0, a0, phase):
                quad = c * (FFN_SLABS // 4) + slab0 // 4
                mt = c * FFN_MT + mt0
                for m in range(4):
                    first = m == 0 and phase is not None
                    product(m, mt + m, quad, 2 * m, 2, hhi, hlo, (h_lo, phase * DT) if first else None)
                    if first:
                        norm(phase, mt + 1)
                for m in range(DT):
                    product(4 + m, mt + (4 + m), quad, 8 + m, 1, ahi, alo, (a_lo, c * 4 + a0) if m == 0 else None)

            def mlp(slab0, mt0, a0, phase):
                ffn(0, slab0, mt0, a0, phase)
                with pe.Fori(1, FFC) as c:
                    ffn(c, slab0, mt0, a0, None)

            mlp(FFN0_SLAB, FFN0_MT, FFN0_A, 1)

            def head_sums(p, m):
                i = 5 * p + m

                def between(s):
                    pe.wait_ge(zz_done, i + 1)
                    for t in ((0, 1), (2,))[s]:
                        if t == 2:
                            pe.wait_ge(hroot_done, 3 * i + 1)
                        elif t == 0 and m:
                            pe.wait_ge(hroot_done, 3 * i)
                        pe.matmul(ps[:, 6 + t % 2, 0:TB], bones, zz[:, t * TB:(t + 1) * TB], start=True, stop=True
                                  ).then_inc(hsum_done, 1)
                return between

            def sample(p):
                for half in range(2):
                    if half == 0:
                        pe.wait_ge(kc_in, 48 * (p + 1))
                        pe.wait_ge(av_kept, 3 * (p + 1))
                    for b in range(4):
                        mm = pe.transpose(ps[:, 3 + half, b * P:(b + 1) * P], kc[:, 4 * half + b, :], ident)
                    mm.then_inc(kct_done, 1)
                pe.wait_ge(qbd_ready, 2 * (p + 1))
                for b in range(NB):
                    if b % 4 == 0:
                        pe.wait_ge(kct_kept, 2 * p + b // 4 + 1)
                    col = (b % 3) * KEYS
                    pe.matmul(ps[0:NS, b // 3, col:col + P], q_bd[:, b, :], kct[:, b, :], start=True, stop=True)
                    mm = pe.matmul(ps[0:NS, b // 3, col + P:col + KEYS], q_bd[:, b, :], k_a[:, SEQ:TOK],
                                   start=True, stop=True)
                mm.then_inc(sas_done, 1)
                pe.wait_ge(sa_ready, p + 1)
                for b in range(NB):
                    mm = pe.transpose(ps[:, 3, b * NS:(b + 1) * NS], sa[0:NS, b, 0:P], ident[0:NS, 0:NS])
                mm.then_inc(pts_done, 1)
                for b in range(NB):
                    mm = pe.transpose(ps[0:NS, 4, b * NS:(b + 1) * NS], sa[0:NS, b, P:KEYS], ident[0:NS, 0:NS])
                mm.then_inc(pts_done, 1)
                pe.wait_ge(pts_kept, 2 * (p + 1))
                pe.wait_ge(nk_kept, 2 * (p + 1))
                for b in range(NB):
                    out = ps[:, 5, b * NS:(b + 1) * NS]
                    pe.matmul(out, vc[:, b, :], pts[:, 0, b, :], start=True, stop=False)
                    mm = pe.matmul(out, v_a[0:NS, CH, :], pts[0:NS, 1, b, :], start=False, stop=True)
                mm.then_inc(os_done, 1)

            def block_scores(u, c):
                if c:
                    pe.wait_ge(s_kept, u)
                lo = P if c == 0 else 0
                keys = slice((c - 1) * P + lo, (c + 1) * P)
                for r in range(GR):
                    for s in range(2):
                        rows = slice(HD * s, HD * (s + 1))
                        col = (r % 2) * 2 * P
                        mm = pe.matmul(ps[:, 2 * s + r // 2, col + lo:col + 2 * P],
                                       q_a[rows, r, c * P:(c + 1) * P], k_a[rows, keys], start=True, stop=True)
                mm.then_inc(s_done, 1)

            def turn_out(u, c):
                pe.wait_ge(oc_kept, u + 1)
                if u:
                    pe.wait_ge(oct_kept, u)
                for r in range(GR):
                    mm = pe.transpose(ps[:, 7, r * P:(r + 1) * P], oc[:, r * P:(r + 1) * P], ident)
                mm.then_inc(oct_done, 1)

            def attend(u, c, p):
                pe.wait_ge(p_done, 9 * (u + 1))
                for g in range(4):
                    if g % 2 == 0:
                        if c == 0:
                            continue
                        if not (c == 1 and g == 0):
                            pe.wait_ge(pt_kept_v, 14 * p + 2 * (c - 1) + g // 2)
                    elif u or g == 3:
                        pe.wait_ge(pt_kept_s, 2 * u + g // 2)
                    for r in range(GR):
                        mm = pe.transpose(ps[:, 4 + g % 2, r * P:(r + 1) * P],
                                          p_a[:, u % 2, 4 * (g // 2) + r, (g % 2) * P:(g % 2 + 1) * P], ident)
                    mm.then_inc(pt_done, 1)
                if c:
                    pe.wait_ge(pt_kept_v, 14 * p + 2 * c)
                pe.wait_ge(pt_kept_s, 2 * u + 2)
                if u:
                    pe.wait_ge(oc_kept, u)
                for s in range(2):
                    for r in range(GR):
                        out = ps[:, 6, r * P + s * HD:r * P + (s + 1) * HD]
                        for k in range(1 if c == 0 else 0, 2):
                            mm = pe.matmul(out, pt_a[:, u % 2, 2 * s + k, r * P:(r + 1) * P],
                                           v_a[:, c - 1 + k, s * HD:(s + 1) * HD],
                                           start=(k == 0 or c == 0), stop=(k == 1))
                mm.then_inc(pv_done, 1)
                if c:
                    turn_out(u - 1, c - 1)

            def pair(p):
                n = SWA_SLAB + p * SWA_SLABS
                mt = SWA_MT0 + p * SWA_MT
                for m in range(6):
                    first = p == 0 and m == 0
                    product(m, mt + m, n // 4, 2 * m, 2, hhi, hlo, (h_lo, 2 * DT) if first else None,
                            head_sums(p, m - 1) if m else None)
                    if first:
                        norm(2, mt + 1)
                pe.wait_ge(mt_free, mt + 6)
                for half in range(2):
                    pe.wait_ge(hroot_done, 15 * (p + 1))
                    for c in range(4):
                        t = (4 * half + c) * P
                        mm = pe.transpose(ps[:, 6 + half, c * P:(c + 1) * P], vt_a[:, t:t + P], ident)
                    mm.then_inc(av_turned, 1)
                pe.transpose(ps[0:NS, 4, 0:P], vt_a[:, SEQ:TOK], ident).then_inc(av_turned, 1)
                pe.wait_ge(qk_ready, 5 * (p + 1))
                pe.transpose(ps[:, 5, 0:P], k_a[:, SEQ - P:SEQ], ident)
                pe.transpose(ps[0:NS, 5, P:2 * P], k_a[:, SEQ:TOK], ident).then_inc(nk_done, 1)
                sample(p)
                pe.wait_ge(sa_max, p + 1)
                block_scores(p * CH, 0)
                for c in range(CH):
                    if c + 1 < CH:
                        block_scores(p * CH + c + 1, c + 1)
                    attend(p * CH + c, c, p)
                turn_out(p * CH + CH - 1, CH - 1)
                for m in range(DT):
                    if m == 0:
                        pe.wait_ge(os_kept, 2 * (p + 1))
                    product(6 + m, mt + 6 + m, n // 4, 12 + m, 1, ahi, alo, (a_lo, SWA_A + 4 * p) if m == 0 else None)

            pe.wait_ge(ac_in, 16)
            for p in range(NPAIR):
                pair(p)
            mlp(FFN1_SLAB, FFN1_MT, FFN1_A, 3)


def _slab(w, rows, cols):
    return w[rows][:, cols].reshape(KG, P, P).transpose(1, 0, 2).reshape(P, KG * P)


def _weights(inputs):
    w_in, w_out = inputs["ret_w_in"][0], inputs["ret_w_out"][0]
    w_qkv, w_o = inputs["swa_w_qkv"][0], inputs["swa_w_o"][0]
    half = [np.arange(0, D // 2), np.arange(D // 2, D)]
    tile = [np.arange(m * P, (m + 1) * P) for m in range(DT)]
    slabs = []
    for h in range(RH):
        starts = [h * DK, h * DK + P, D + h * DK, D + h * DK + P]
        starts += [2 * D + h * DV + m * P for m in range(4)] + [4 * D + h * DV + m * P for m in range(4)]
        slabs += [_slab(w_in, rows, np.arange(s, s + P)) for s in starts for rows in half]
        slabs += [_slab(w_out, np.arange(h * DV, (h + 1) * DV), cols) for cols in tile]

    def ffn(layer):
        up, down = inputs["ffn_w_up"][layer], inputs["ffn_w_down"][layer]
        for c in range(FFC):
            yield from (_slab(up, rows, np.arange(c * 512 + m * P, c * 512 + (m + 1) * P))
                        for m in range(4) for rows in half)
            yield from (_slab(down, np.arange(c * 512, (c + 1) * 512), cols) for cols in tile)

    slabs += ffn(0)
    for p in range(NPAIR):
        heads = [np.concatenate([np.arange((GR * (2 * p + s) + r) * HD, (GR * (2 * p + s) + r + 1) * HD)
                                 for s in range(2)]) for r in range(GR)]
        kv = [D + KVH * HD * j + np.arange(2 * p * HD, (2 * p + 2) * HD) for j in range(2)]
        slabs += [_slab(w_qkv, rows, cols) for cols in heads + kv for rows in half]
        slabs += [_slab(w_o, np.concatenate(heads), cols) for cols in tile]
    slabs += ffn(1)
    return np.stack(slabs)


def _rope(width):
    half = width // 2
    inv = np.float32(THETA) ** (-np.arange(half, dtype=np.float32) / np.float32(half))
    pos = np.concatenate([np.arange(SEQ), np.tile(PAST + np.arange(NT), NB)]).astype(np.float32)
    ang = (inv[:, None] * pos[None, :]).astype(np.float32).astype(np.float64)
    return np.cos(ang).astype(np.float32), np.sin(ang).astype(np.float32)


def _constants():
    lg = np.log1p(-np.exp2(-5.0 - np.arange(RH)))
    i = np.arange(P)
    t, seq = np.arange(NS) % NT, np.arange(NS) // NT
    cols = np.zeros((P, C_N), np.float32)
    cols[:, C_ID:C_ID + P] = np.eye(P)
    cols[:, C_ONE:C_ONE + P] = 1.0
    cols[:, C_EPS] = EPS
    scale = DK ** -0.5
    decays = np.zeros((RH, P, 6), np.float32)
    decays[:, :, H_QDEC] = np.exp(lg[:, None] * (i + 1))
    decays[:, :, H_KDEC] = np.exp(lg[:, None] * (P - 1 - i)) * scale
    decays[:, :, H_CDEC] = np.exp(lg * P)[:, None]
    decays[:, :NS, H_QDS] = np.exp(lg[:, None] * (t + 1))
    decays[:, :NS, H_KDS] = np.exp(lg[:, None] * (NT - 1 - t)) * scale
    decays[:, :, H_CDS] = np.exp(lg * NT)[:, None]
    cols[:NS, C_BM:C_BM + NB] = seq[:, None] == np.arange(NB)
    masks = np.zeros((RH, P, P + NS), np.float32)
    for h in range(RH):
        masks[h, :, :P] = np.where(i[None, :] >= i[:, None], np.exp(-(i + 1.0) * lg[h])[:, None] * scale, 0.0)
        own = (seq[:, None] == seq[None, :]) & (t[None, :] >= t[:, None])
        masks[h, :NS, P:] = np.where(own, np.exp(-(t + 1.0) * lg[h])[:, None] * scale, 0.0)
    attn = np.zeros((P, A_N), np.float32)
    attn[:, A_BO:A_BO + P] = (i[:, None] // HD) == (i[None, :] // HD)
    d = i[:, None] + P - np.arange(2 * P)[None, :]
    attn[:, A_MASK:] = np.where((d >= 0) & (d < WIN), 0.0, NEG)
    tq = np.arange(NS) % NT
    s_mask = np.full((NS, NB, KEYS), NEG, np.float32)
    d = tq[:, None] + WIN - np.arange(WIN)[None, :]
    s_mask[:, :, :WIN] = np.where((d >= 0) & (d < WIN), 0.0, NEG)[:, None, :]
    for b in range(NB):
        for j in range(NT):
            s_mask[tq >= j, b, WIN + NT * b + j] = 0.0
    cos, sin = _rope(DK)
    tables = np.stack([cos, sin], axis=1)
    cos, sin = _rope(HD)
    attn_tables = np.stack([np.concatenate([cos] * 4), np.concatenate([-sin, sin] * 2)], axis=1)
    return cols, masks, decays, attn, s_mask, tables, attn_tables


def kernel(**inputs):
    import concourse.bacc as _bacc
    from concourse.bass_utils import run_bass_kernel_spmd as _run

    inputs = {k: np.asarray(v) for k, v in inputs.items()}
    cols, masks, decays, attn, s_mask, tables, attn_tables = _constants()
    gains = [inputs["norm_mix"][0], inputs["norm_ffn"][0], inputs["norm_mix"][1], inputs["norm_ffn"][1]]
    for phase, g in enumerate(gains):
        cols[:, C_GAIN + phase * DT:C_GAIN + (phase + 1) * DT] = g.reshape(DT, P).T
    cols[:, C_QN] = np.concatenate([inputs["swa_q_norm"][0]] * 2)
    cols[:, C_KN] = np.concatenate([inputs["swa_k_norm"][0]] * 2)
    sinks = inputs["swa_sinks"][0]
    cols[:, C_SINK:C_SINK + NPAIR * PH] = sinks[None, :]
    for p in range(NPAIR):
        cols[:NS, C_SINKS + p] = np.repeat(sinks[PH * p:PH * (p + 1)], NT)
    xs = np.concatenate([inputs["x_prompt"][0], inputs["x_sample"].reshape(NS, D)])
    data = {
        "xT": xs.T.reshape(DT, P, TOK).transpose(1, 0, 2), "weights": _weights(inputs), "tables": tables,
        "attn_tables": attn_tables, "consts": cols, "ret_masks": masks, "ret_decays": decays, "attn_consts": attn, "sample_mask": s_mask,
        "state_in": inputs["state_ret"][0], "cache_k": inputs["cache_swa_k"][0].reshape(NB, WIN, KVH * HD),
        "cache_v": inputs["cache_swa_v"][0].reshape(NB, WIN, KVH * HD),
    }
    outs = {
        "yT": (P, DT, TOK), "state_p": (RH, DK, DV), "kp_out": (WIN, KVH * HD), "vp_out": (WIN, KVH * HD),
        "state_s": (NB, RH, DK, DV), "ks_out": (NB, WIN, KVH * HD), "vs_out": (NB, WIN, KVH * HD),
    }
    nc = _bacc.Bacc("TRN2", target_bir_lowering=False, num_devices=1)
    arrays, args = {}, []
    for name, a in data.items():
        a = np.ascontiguousarray(a)
        arrays[f"in_{name}"] = a
        args.append(nc.dram_tensor(f"in_{name}", a.shape, mybir.dt.from_np(a.dtype), kind="ExternalInput").ap())
    for name, shape in outs.items():
        args.append(nc.dram_tensor(f"out_{name}", shape, F32, kind="ExternalOutput").ap())
    trunk(nc, *args)
    r = _run(nc, [arrays], core_ids=[0]).results[0]
    got = {name: np.asarray(r[f"out_{name}"]) for name in outs}
    y = got["yT"].transpose(1, 0, 2).reshape(D, TOK).T
    return (y[:SEQ].reshape(1, SEQ, D), y[SEQ:].reshape(NB, NT, D), got["state_p"].reshape(1, 1, RH, DK, DV),
            got["kp_out"].reshape(1, 1, WIN, KVH, HD), got["vp_out"].reshape(1, 1, WIN, KVH, HD),
            got["state_s"].reshape(1, NB, RH, DK, DV), got["ks_out"].reshape(1, NB, WIN, KVH, HD),
            got["vs_out"].reshape(1, NB, WIN, KVH, HD))
```

```python
import numpy as np
import concourse.bass as bass
from concourse import mybir
from contextlib import ExitStack

F32 = mybir.dt.float32
F32R = mybir.dt.float32r
ALU = mybir.AluOpType
ACT = mybir.ActivationFunctionType
AX = mybir.AxisListType

P = 128
D = 1024
SEQ = 1024
NB, NT = 8, 4
NS = NB * NT
TOK = SEQ + NS
TB, NTB = 352, 3
DT = D // P
RH, DK, DV = 4, 256, 512
CH = SEQ // P
PAST = 2048
WIN = 128
HD = 64
KVH = 4
NPAIR, GR = 2, 4
PH = 2 * GR
FFC = 8
EPS = 1e-6
NEG = -1e30
THETA = 10000.0

KG = 4
RING = 4
LEAD = 3
RET_SLABS = 12 * 2 + DT
FFN_SLABS = 4 * 2 + DT
SWA_SLABS = 6 * 2 + DT
FFN0_SLAB = RH * RET_SLABS
SWA_SLAB = FFN0_SLAB + FFC * FFN_SLABS
FFN1_SLAB = SWA_SLAB + NPAIR * SWA_SLABS
N_SLABS = FFN1_SLAB + FFC * FFN_SLABS

RET_MT, FFN_MT, SWA_MT = 12 + DT, 4 + DT, 6 + DT
FFN0_MT = RH * RET_MT
SWA_MT0 = FFN0_MT + FFC * FFN_MT
FFN1_MT = SWA_MT0 + NPAIR * SWA_MT

FFN0_A = RH * 4
SWA_A = FFN0_A + FFC * 4
FFN1_A = SWA_A + NPAIR * 4

C_ID, C_ONE, C_GAIN = 0, P, 2 * P
C_EPS = C_GAIN + 4 * DT
C_BM = C_EPS + 1
C_QN, C_KN, C_QX, C_KX = (C_BM + NB + i for i in range(4))
C_SINK = C_KX + 1
C_SINKS = C_SINK + NPAIR * PH
C_N = C_SINKS + NPAIR
H_QDEC, H_KDEC, H_CDEC, H_QDS, H_KDS, H_CDS = range(6)
A_BO, A_MASK, A_N = 0, P, P + 2 * P
KEYS = WIN + NS


def trunk(nc, xT, weights, tables, attn_tables, consts, ret_masks, ret_decays, attn_consts, sample_mask,
          state_in, cache_k, cache_v, yT, state_p, kp_out, vp_out, state_s, ks_out, vs_out):
    with ExitStack() as ctx:
        base = (nc.sbuf_base + 31) // 32 * 32

        def at(name, offset, shape, dt):
            return nc.alloc_sbuf_tensor_at(name, shape, dt, offset=base + offset)

        TT = TOK * 4
        o_x, o_hhi, o_hlo = 0, DT * TT, 2 * DT * TT
        o_ahi = 3 * DT * TT
        o_alo = o_ahi + KG * TT
        o_wraw = o_alo + KG * TT
        o_whi = o_wraw + RING * 2048
        o_wlo = o_whi + RING * 2048
        o_rst = o_wlo + RING * 2048
        o_cst = o_rst + TT
        o_work = (o_cst + 4 * C_N + 31) // 32 * 32

        x = at("x", o_x, [P, DT, TOK], F32)
        hhi = at("hhi", o_hhi, [P, DT, TOK], F32R)
        hlo = at("hlo", o_hlo, [P, DT, TOK], F32R)
        ahi = at("ahi", o_ahi, [P, KG, TOK], F32R)
        alo = at("alo", o_alo, [P, KG, TOK], F32R)
        wraw = at("wraw", o_wraw, [P, RING, 512], F32)
        whi = at("whi", o_whi, [P, RING, 512], F32R)
        wlo = at("wlo", o_wlo, [P, RING, 512], F32R)
        rst = at("rst", o_rst, [P, TOK], F32)
        cst = at("cst", o_cst, [P, C_N], F32)
        ident = cst[:, C_ID:C_ID + P]
        ones = cst[:, C_ONE:C_ONE + P]
        eps = cst[:, C_EPS:C_EPS + 1]

        o_v = o_work + 4 * TT
        qk = at("qk", o_work, [P, 4, TOK], F32)
        v_tok = at("v_tok", o_v, [P, CH, DV], F32)
        v_smp = at("v_smp", o_v + CH * DV * 4, [P, DV], F32R)
        rope_tab = at("rope_tab", o_v, [P, 2, TOK], F32)
        q_sel = at("q_sel", o_v, [P, 2, NB, NS], F32)
        k_sel = at("k_sel", o_v + 2048, [P, NB, DK], F32R)
        o_r = o_v + (CH + 1) * DV * 4
        s_ret = at("s_ret", o_r, [P, 2, DV], F32)
        sc_t = at("sc_t", o_r + 4096, [P, 2, P], F32)
        k_tok = at("k_tok", o_r + 5120, [P, 2, DK], F32)
        o_tok = at("o_tok", o_r + 7168, [P, DV], F32)
        hmask = at("hmask", o_r + 9216, [P, P + NS], F32)
        stat = at("stat", o_r + 9856, [P, 4], F32)
        hc = at("hc", o_r + 9888, [P, 6], F32)
        k_smp = at("k_smp", o_r + 9920, [P, DK], F32R)
        sc_smp = at("sc_smp", o_r + 10944, [P, NS], F32R)
        k4 = at("k4", o_r + 11072, [P, 2, 4, NS], F32)
        v4 = at("v4", o_ahi, [P, 4, 4, NS], F32)
        o_t = at("o_t", o_ahi, [P, 4, TOK], F32)
        tmp = at("tmp", o_alo, [P, 4, TOK], F32)
        s0 = at("s0", o_alo, [P, 4, 2, DV], F32)

        sq = at("sq", o_work, [P, 2, TOK], F32)
        ssum = at("ssum", o_work + 2 * TT, [P, TOK], F32)
        relu = at("relu", o_work + 4 * TT, [P, 2, TOK], F32)
        a2 = at("a2", o_work + 6 * TT, [P, 2, TOK], F32)

        q_a = at("q_a", o_work, [P, GR, TOK], F32)
        k_z = at("k_z", o_work + 4 * TT, [P, 2, TOK], F32)
        o_a = o_work + 6 * TT
        v_a = at("v_a", o_a, [P, CH + 1, P], F32)
        acst = at("acst", o_a + 4608, [P, A_N], F32)
        ast = at("ast", o_a + 4608 + 4 * A_N, [P, 96], F32)
        o_b = o_a + 4992 + 4 * A_N
        kc = at("kc", o_b, [P, NB, P], F32)
        vc = at("vc", o_b + 4096, [P, NB, P], F32)
        nk = at("nk", o_b + 8192, [P, 2, P], F32)
        vt_a = at("vt_a", o_b + 9216, [P, TOK], F32)
        z_a = at("z_a", o_ahi, [P, 2, TOK], F32)
        zz = at("zz", o_ahi + 2 * TT, [P, TOK], F32)
        zr = at("zr", o_ahi + 3 * TT, [P, 2, TOK], F32)
        nr = at("nr", o_ahi + 5 * TT, [P, TOK], F32)
        atab = at("atab", o_ahi + 6 * TT, [P, 2, TOK], F32)
        p_a = at("p_a", o_ahi, [P, 4, GR, 2 * P], F32)
        pt_a = at("pt_a", o_ahi + 16384, [P, 2, 2, GR * P], F32)
        sa = at("sa", o_ahi + 24576, [P, NB, KEYS], F32)
        q_bd = at("q_bd", o_ahi + 29696, [P, NB, NS], F32)
        pts = at("pts", o_ahi + 30720, [P, 2, NB, NS], F32)
        bones = acst[:, A_BO:A_BO + P]

        ps = ctx.enter_context(nc.psum_tensor("ps", [P, 8, 512], F32))

        def sem(name):
            return ctx.enter_context(nc.semaphore(name))

        w_in = [sem(f"w_in{i}") for i in range(RING)]
        w_hi = sem("w_hi")
        w_lo = sem("w_lo")
        slab_used = sem("slab_used")
        mt_free = sem("mt_free")
        c_in = sem("c_in")
        x_in = [sem(f"x_in{k}") for k in range(DT)]
        tab_in = sem("tab_in")
        h_hi = sem("h_hi")
        h_lo = sem("h_lo")
        sq_done = sem("sq_done")
        sum_done = sem("sum_done")
        ssq_done = sem("ssq_done")
        rst_sq = sem("rst_sq")
        rst_done = sem("rst_done")
        a2_done = sem("a2_done")
        a_hi = sem("a_hi")
        a_lo = sem("a_lo")
        dve_seq = sem("dve_seq")
        v_turned = sem("v_turned")
        v_kept = sem("v_kept")
        four_ready = sem("four_ready")
        vs_ready = sem("vs_ready")
        sc_done = sem("sc_done")
        sc_kept = sem("sc_kept")
        kt_done = sem("kt_done")
        kt_kept = sem("kt_kept")
        st_done = sem("st_done")
        s_upd = sem("s_upd")
        o_done = sem("o_done")
        ss_done = sem("ss_done")
        rs_done = sem("rs_done")
        rr_done = sem("rr_done")
        o_kept = sem("o_kept")
        ot_done = sem("ot_done")
        ot_kept = sem("ot_kept")
        sp_out = sem("sp_out")
        sel_ready = sem("sel_ready")
        sts_done = sem("sts_done")
        s0_upd = sem("s0_upd")
        s0_in = [sem(f"s0_in{i}") for i in range(4)]
        s0_out = [sem(f"s0_out{i}") for i in range(4)]
        g_silu = sem("g_silu")
        g_of = sem("g_of")
        ac_in = sem("ac_in")
        zz_done = sem("zz_done")
        zr_in = [sem(f"zr_in{i}") for i in range(2)]
        zs_done = sem("zs_done")
        hsum_done = sem("hsum_done")
        hroot_done = sem("hroot_done")
        kz_zero = sem("kz_zero")
        qk_ready = sem("qk_ready")
        av_turned = sem("av_turned")
        av_kept = sem("av_kept")
        nk_done = sem("nk_done")
        nk_kept = sem("nk_kept")
        kc_in = sem("kc_in")
        sm_in = sem("sm_in")
        kct_done = sem("kct_done")
        kct_kept = sem("kct_kept")
        qbd_ready = sem("qbd_ready")
        sas_done = sem("sas_done")
        sas_kept = sem("sas_kept")
        sa_max = sem("sa_max")
        sa_exp = sem("sa_exp")
        sa_ready = sem("sa_ready")
        pts_done = sem("pts_done")
        pts_kept = sem("pts_kept")
        os_done = sem("os_done")
        os_kept = sem("os_kept")
        s_done = sem("s_done")
        s_kept = sem("s_kept")
        m_ready = sem("m_ready")
        p_done = sem("p_done")
        den_ready = sem("den_ready")
        pn_done = sem("pn_done")
        pt_done = sem("pt_done")
        pt0_kept = sem("pt0_kept")
        pt1_kept = sem("pt1_kept")
        pv_done = sem("pv_done")
        out_kept = sem("out_kept")
        swa_out = sem("swa_out")
        y_out = sem("y_out")

        block = ctx.enter_context(nc.Block())

        def bank_set(m):
            return ps[:, 3 * (m % 2):3 * (m % 2) + NTB, 0:TB]

        def blocks(tile):
            return tile.rearrange("p (b t) -> p b t", b=NTB)

        HU = 2 * CH

        def turned(p, k):
            return p * (2 * HU - 2) + (k if k < 2 else 2 * k - 2)

        def f32(ap):
            return ap.bitcast(F32)

        @block.sync
        def _(sp):
            def slabs(quad, a, b):
                for i in range(a, b):
                    if not (isinstance(quad, int) and quad == 0 and i < RING):
                        sp.wait_ge(w_lo, quad * 4 + (i - RING + 1))
                    sp.dma_start(wraw[:, i % RING, :], weights[quad * 4 + i]).then_inc(w_in[i % RING], 16)

            sp.dma_start(x[:, 0, :], xT[:, 0, :]).then_inc(x_in[0], 16)
            sp.dma_start(cst[:, :], consts).then_inc(c_in, 16)
            slabs(0, 0, RING)
            for k in range(1, DT):
                sp.dma_start(x[:, k, :], xT[:, k, :]).then_inc(x_in[k], 16)

            def store_state(h, b):
                sp.wait_ge(s0_upd, h * NB + (b + 1))
                sp.dma_start(state_s[b, h].rearrange("(j p) e -> p j e", j=2), s0[:, b % 4, :, :]
                             ).then_inc(s0_out[b % 4], 16)

            def load_state(h, b):
                if b >= 4:
                    sp.wait_ge(s0_out[b % 4], h * 32 + 16)
                sp.dma_start(s0[:, b % 4, :, :], state_in[b, h].rearrange("(j p) e -> p j e", j=2)
                             ).then_inc(s0_in[b % 4], 16)

            def ret_head(h, first):
                quad = h * (RET_SLABS // 4)
                if not first:
                    slabs(quad, 0, 4)
                    sp.wait_ge(ot_kept, h * (CH + 1))
                sp.dma_start(rope_tab[:, :, :], tables).then_inc(tab_in, 16)
                sp.dma_start(hmask[:, :], ret_masks[h]).then_inc(tab_in, 16)
                sp.dma_start(hc[:, :], ret_decays[h]).then_inc(tab_in, 16)
                slabs(quad, 4, 19)
                sp.wait_ge(v_turned, h * 9 + 9)
                for b in range(4):
                    load_state(h, b)
                sp.wait_ge(s_upd, h * CH + CH)
                sp.dma_start(state_p[h].rearrange("(j p) e -> p j e", j=2), s_ret[:, :, :]).then_inc(sp_out, 16)
                store_state(h, 0)
                store_state(h, 1)
                load_state(h, 4)
                store_state(h, 2)
                load_state(h, 5)
                store_state(h, 3)
                load_state(h, 6)
                load_state(h, 7)
                for b in range(4, NB):
                    store_state(h, b)
                slabs(quad, 19, RET_SLABS)

            ret_head(0, True)
            with sp.Fori(1, RH) as h:
                ret_head(h, False)

            with sp.Fori(FFN0_SLAB // 4, SWA_SLAB // 4) as quad:
                slabs(quad, 0, 4)

            sp.wait_ge(a_lo, SWA_A)
            sp.dma_start(acst[:, :], attn_consts).then_inc(ac_in, 16)
            for p in range(NPAIR):
                quad = (SWA_SLAB + p * SWA_SLABS) // 4
                slabs(quad, 0, 4)
                sp.wait_ge(slab_used, 4 * quad)
                sp.dma_start(atab[:, :, :], attn_tables).then_inc(tab_in, 16)
                feats = slice(2 * p * HD, (2 * p + 2) * HD)
                if p:
                    sp.wait_ge(os_done, p)
                sp.dma_start(kc[:, :, :], cache_k[:, :, feats].rearrange("b k f -> k b f")).then_inc(kc_in, 16)
                sp.dma_start(vc[:, :, :], cache_v[:, :, feats].rearrange("b k f -> k b f")).then_inc(kc_in, 16)
                slabs(quad, 4, 15)
                sp.wait_ge(qk_ready, 6 * (p + 1))
                sp.dma_start(sa[0:NS, :, :], sample_mask).then_inc(sm_in, 16)
                if p == 0:
                    sp.dma_start(ks_out[:, 0:WIN - NT, :], cache_k[:, NT:WIN, :]).then_inc(swa_out, 16)
                    sp.dma_start(vs_out[:, 0:WIN - NT, :], cache_v[:, NT:WIN, :]).then_inc(swa_out, 16)
                slabs(quad, 15, 19)
                sp.wait_ge(av_kept, 3 * (p + 1))
                sp.dma_start(vp_out[:, feats], v_a[:, CH - 1, :]).then_inc(swa_out, 16)
                for b in range(NB):
                    sp.dma_start(vs_out[b, WIN - NT:WIN, feats], v_a[NT * b:NT * b + NT, CH, :]
                                 ).then_inc(swa_out, 16)
                sp.wait_ge(nk_kept, 4 * (p + 1))
                sp.dma_start(kp_out[:, feats], nk[:, 0, :]).then_inc(swa_out, 16)
                for b in range(NB):
                    sp.dma_start(ks_out[b, WIN - NT:WIN, feats], nk[NT * b:NT * b + NT, 1, :]
                                 ).then_inc(swa_out, 16)
                slabs(quad, 19, SWA_SLABS)

            with sp.Fori(FFN1_SLAB // 4, N_SLABS // 4) as quad:
                slabs(quad, 0, 4)
            for m in range(DT):
                sp.wait_ge(mt_free, FFN1_MT + FFC * FFN_MT - DT + m + 1)
                sp.dma_start(yT[:, m, :], x[:, m, :]).then_inc(y_out, 16)
            sp.wait_ge(y_out, 16 * DT)
            sp.wait_ge(swa_out, 16 * (2 + NPAIR * (2 + 2 * NB)))
            sp.wait_ge(sp_out, 16 * RH)
            for i in range(4):
                sp.wait_ge(s0_out[i], 32 * RH)

        @block.gpsimd
        def _(pool):
            def sum_squares(phase):
                for k in range(DT):
                    n = phase * DT + k
                    pool.wait_ge(sq_done, n + 1)
                    if k == 0:
                        if phase:
                            pool.wait_ge(ssq_done, phase)
                        pool.tensor_copy(ssum[:, :], sq[:, 0, :]).then_inc(sum_done, 1)
                    else:
                        pool.wait_ge(sum_done, n)
                        pool.tensor_tensor(ssum[:, :], ssum[:, :], sq[:, k % 2, :], ALU.add).then_inc(sum_done, 1)

            sum_squares(0)
            sum_squares(1)
            sum_squares(2)
            for p in range(NPAIR):
                for m in range(5):
                    if m == 0:
                        pool.wait_ge(tab_in, 48 * RH + 16 * (p + 1))
                    pool.wait_ge(zr_in[m % 2], 64 * ((3 - m % 2) * p + m // 2 + 1))
                    pool.tensor_tensor(zr[:, m % 2, :], zr[:, m % 2, :], atab[:, 1, :], ALU.mult
                                       ).then_inc(zs_done, 1)
                for k in range(HU):
                    u = p * HU + k
                    lo = P if k < 2 else 0
                    pool.wait_ge(den_ready, u + 1)
                    inv = ast[:, 32 + 16 * (u % 4) + 12:32 + 16 * (u % 4) + 16]
                    pool.tensor_tensor(p_a[:, u % 4, :, lo:], p_a[:, u % 4, :, lo:],
                                       inv.unsqueeze(2).to_broadcast([P, GR, 2 * P - lo]), ALU.mult
                                       ).then_inc(pn_done, 1)
            sum_squares(3)

        @block.scalar
        def _(act):
            def split(quad, a, b, last=N_SLABS):
                for i in range(a + LEAD, b + LEAD):
                    if isinstance(quad, int) and 4 * quad + i >= last:
                        continue
                    act.wait_ge(w_in[i % RING], 16 * (quad + i // RING + 1))
                    if not (isinstance(quad, int) and 4 * quad + i < RING):
                        act.wait_ge(slab_used, quad * 4 + (i - RING + 1))
                    act.copy(whi[:, i % RING, :], wraw[:, i % RING, :]).then_inc(w_hi, 1)

            def gain_x(k, phase):
                g = C_GAIN + phase * DT + k
                act.mul(hhi[:, k, :], x[:, k, :], cst[:, g:g + 1]).then_inc(h_hi, 1)
                n = phase * DT + k
                if n >= 2:
                    act.wait_ge(sum_done, n - 1)
                act.activation(sq[:, k % 2, :], x[:, k, :], ACT.Square).then_inc(sq_done, 1)

            def norm(phase):
                act.wait_ge(ssq_done, phase + 1)
                if phase:
                    act.wait_ge(rst_done, phase)
                act.activation(blocks(rst[:, :]), ps[:, 3:6, 0:TB], ACT.Sqrt, bias=eps, scale=1.0 / D
                               ).then_inc(rst_sq, 1)

            split(0, -LEAD, 0)
            act.wait_ge(c_in, 16)
            for k in range(DT):
                act.wait_ge(x_in[k], 16)
                gain_x(k, 0)

            def keep_v(h, e):
                for half in range(2):
                    act.wait_ge(v_turned, h * 9 + (2 * e + half + 1))
                    act.copy(v_tok[:, 4 * half:4 * half + 4, e * P:(e + 1) * P],
                             ps[:, 6 + half, :].rearrange("p (c f) -> p c f", c=4)).then_inc(v_kept, 1)

            def keep_o(h, c):
                rows = NS if c == CH else P
                act.wait_ge(ot_done, h * (CH + 1) + (c + 1))
                act.copy(o_t[:, :, c * P:c * P + rows],
                         ps[:, 4, :].rearrange("p (e t) -> p e t", e=4)[:, :, 0:rows]).then_inc(ot_kept, 1)

            def norm_o(h, c):
                i = h * (CH + 1) + c
                rows = NS if c == CH else P
                qdec = hc[0:rows, H_QDS:H_QDS + 1] if c == CH else hc[0:rows, H_QDEC:H_QDEC + 1]
                bank = 2 + c % 2
                act.wait_ge(o_done, i + 1)
                if not (isinstance(h, int) and i == 0):
                    act.wait_ge(ot_done, i)
                act.activation(o_tok[0:rows, :], ps[0:rows, bank, :], ACT.Square, scale=qdec,
                               accum_out=stat[0:rows, 0:1]).then_inc(ss_done, 1)
                act.wait_ge(ss_done, i + 1)
                act.activation(stat[0:rows, 1:2], stat[0:rows, 0:1], ACT.Sqrt, bias=eps[0:rows, :], scale=1.0 / DV
                               ).then_inc(rs_done, 1)
                if c:
                    keep_o(h, c - 1)
                act.wait_ge(rr_done, i + 1)
                act.mul(o_tok[0:rows, :], ps[0:rows, bank, :], stat[0:rows, 3:4]).then_inc(o_kept, 1)

            def ret_head(h, first, last):
                quad = h * (RET_SLABS // 4)
                mt = h * RET_MT
                split(quad, 0, 2)
                if first:
                    norm(0)
                split(quad, 2, 8)
                for e in range(4):
                    split(quad, 8 + 2 * e, 10 + 2 * e)
                    if e:
                        keep_v(h, e - 1)
                keep_v(h, 3)
                act.wait_ge(v_turned, h * 9 + 9)
                act.copy(v_smp[:, :], ps[:, 4, :]).then_inc(v_kept, 1)
                for c in range(CH + 1):
                    norm_o(h, c)
                keep_o(h, CH)
                for m in range(4):
                    split(quad, 16 + 2 * m, 18 + 2 * m)
                    act.wait_ge(mt_free, mt + (8 + m + 1))
                    act.activation(qk[:, 2 + m % 2, :], qk[:, m % 2, :], ACT.Silu).then_inc(g_silu, 1)
                    act.wait_ge(g_of, h * 4 + (m + 1))
                    act.copy(ahi[:, m, :], qk[:, m % 2, :]).then_inc(a_hi, 1)
                for m in range(DT):
                    split(quad, 24 + m, 25 + m)
                    if last:
                        act.wait_ge(mt_free, mt + (12 + m + 1))
                        gain_x(m, 1)

            ret_head(0, True, False)
            with act.Fori(1, RH - 1) as h:
                ret_head(h, False, False)
            ret_head(RH - 1, False, True)

            def ffn(c, slab0, mt0, a0, up0, phase, next_phase):
                quad = c * (FFN_SLABS // 4) + slab0 // 4
                for m in range(4):
                    up = c * 4 + (up0 + m)
                    split(quad, 2 * m, 2 * m + 2)
                    if m == 0 and phase is not None:
                        norm(phase)
                    act.wait_ge(mt_free, c * FFN_MT + (mt0 + m + 1))
                    act.wait_ge(a_lo, c * 4 + (a0 + m - 1))
                    act.activation(a2[:, m % 2, :], relu[:, m % 2, :], ACT.Square).then_inc(a2_done, 1)
                    act.wait_ge(a2_done, up + 1)
                    act.copy(ahi[:, m, :], a2[:, m % 2, :]).then_inc(a_hi, 1)
                for m in range(DT):
                    split(quad, 8 + m, 9 + m)
                    if next_phase is not None:
                        act.wait_ge(mt_free, c * FFN_MT + (mt0 + 4 + m + 1))
                        gain_x(m, next_phase)

            def mlp(slab0, mt0, a0, up0, phase, next_phase):
                ffn(0, slab0, mt0, a0, up0, phase, None)
                with act.Fori(1, FFC - 1) as c:
                    ffn(c, slab0, mt0, a0, up0, None, None)
                ffn(FFC - 1, slab0, mt0, a0, up0, None, next_phase)

            mlp(FFN0_SLAB, FFN0_MT, FFN0_A, 0, 1, 2)

            def head_roots(p, m, t):
                i = 5 * p + m
                act.wait_ge(hsum_done, 3 * i + t + 1)
                if t == 0 and i:
                    act.wait_ge(qk_ready, 6 * p + m if m else 6 * p)
                act.activation(nr[:, t * TB:(t + 1) * TB], ps[:, 6 + t % 2, 0:TB], ACT.Sqrt, bias=eps,
                               scale=1.0 / HD).then_inc(hroot_done, 1)

            def square_head(p, m):
                act.wait_ge(mt_free, SWA_MT0 + p * SWA_MT + m + 1)
                for half in range(0, P, HD):
                    for a, b in ((0, HD // 2), (HD // 2, 0)):
                        act.dma_start(zr[half + a:half + a + HD // 2, m % 2, :],
                                      z_a[half + b:half + b + HD // 2, m % 2, :]).then_inc(zr_in[m % 2], 16)
                act.activation(zz[:, :], z_a[:, m % 2, :], ACT.Square).then_inc(zz_done, 1)

            def exponentials(u, k):
                slot, lo = u % 4, P if k < 2 else 0
                st = 32 + 16 * slot
                act.wait_ge(m_ready, u + 1)
                for j in range(GR):
                    act.activation(p_a[:, slot, j, lo:], p_a[:, slot, j, lo:], ACT.Exp,
                                   bias=ast[:, st + j:st + j + 1], accum_out=ast[:, st + 4 + j:st + 5 + j]
                                   ).then_inc(p_done, 1)
                act.activation(ast[:, st + 8:st + 12], ast[:, st + 8:st + 12], ACT.Exp).then_inc(p_done, 1)

            def keep_out(u, k):
                rows = slice(HD * (k % 2), HD * (k % 2 + 1))
                c = k // 2
                act.wait_ge(pv_done, u + 1)
                act.copy(q_a[rows, :, c * P:(c + 1) * P],
                         ps[rows, 6 + k % 2, :].rearrange("p (r t) -> p r t", r=GR)).then_inc(out_kept, 1)

            def pair(p):
                quad = (SWA_SLAB + p * SWA_SLABS) // 4
                for m in range(6):
                    split(quad, 2 * m, 2 * m + 1)
                    if m == 0:
                        split(quad, 1, 2)
                        if p == 0:
                            norm(2)
                    else:
                        head_roots(p, m - 1, 0)
                        head_roots(p, m - 1, 1)
                        split(quad, 2 * m + 1, 2 * m + 2)
                        head_roots(p, m - 1, 2)
                    if m == 1:
                        for half in range(2):
                            act.wait_ge(kct_done, 2 * p + half + 1)
                            act.copy(kc[:, 4 * half:4 * half + 4, :],
                                     ps[:, 6 + half, :].rearrange("p (b f) -> p b f", b=4)).then_inc(kct_kept, 1)
                    if m < 5:
                        square_head(p, m)
                if p:
                    act.wait_ge(swa_out, 16 * (2 + p * (2 + 2 * NB)))
                for half in range(2):
                    act.wait_ge(av_turned, 3 * p + half + 1)
                    act.copy(v_a[:, 4 * half:4 * half + 4, :],
                             ps[:, 6 + half, :].rearrange("p (c f) -> p c f", c=4)).then_inc(av_kept, 1)
                act.wait_ge(av_turned, 3 * p + 3)
                act.copy(v_a[0:NS, CH, :], ps[0:NS, 4, 0:P]).then_inc(av_kept, 1)
                act.wait_ge(nk_done, p + 1)
                for s in range(2):
                    col, f = s * P + s * HD, slice(s * HD, (s + 1) * HD)
                    act.copy(nk[:, 0, f], ps[:, 5, col:col + HD]).then_inc(nk_kept, 1)
                    act.copy(nk[0:NS, 1, f], ps[0:NS, 5, 2 * P + col:2 * P + col + HD]).then_inc(nk_kept, 1)
                act.wait_ge(sa_max, p + 1)
                for b in range(NB):
                    act.activation(sa[0:NS, b, :], sa[0:NS, b, :], ACT.Exp, bias=ast[0:NS, 8 + b:9 + b],
                                   accum_out=ast[0:NS, 16 + b:17 + b]).then_inc(sa_exp, 1)
                act.activation(ast[0:NS, 24:32], ast[0:NS, 24:32], ACT.Exp).then_inc(sa_exp, 1)
                exponentials(p * HU, 0)
                for k in range(HU):
                    u = p * HU + k
                    if k >= 2:
                        keep_out(u - 2, k - 2)
                    if k + 1 < HU:
                        exponentials(u + 1, k + 1)
                    act.wait_ge(pt_done, turned(p, k + 1))
                    if k >= 2:
                        act.wait_ge(pv_done, u - 1)
                    act.copy(pt_a[:, u % 2, 1, :], ps[:, 5, :]).then_inc(pt1_kept, 1)
                    if k == 0:
                        act.wait_ge(pts_done, p + 1)
                        act.copy(pts[:, 0, :, :], ps[:, 7, 0:NB * NS].rearrange("p (b n) -> p b n", b=NB)
                                 ).then_inc(pts_kept, 1)
                        act.copy(pts[0:NS, 1, :, :], ps[0:NS, 7, NB * NS:].rearrange("p (b n) -> p b n", b=NB)
                                 ).then_inc(pts_kept, 1)
                keep_out((p + 1) * HU - 2, HU - 2)
                keep_out((p + 1) * HU - 1, HU - 1)
                act.wait_ge(out_kept, HU * (p + 1))
                act.wait_ge(os_kept, 2 * (p + 1))
                for r in range(GR):
                    act.copy(ahi[:, r, :], q_a[:, r, :]).then_inc(a_hi, 1)
                for m in range(DT):
                    split(quad, 12 + m, 13 + m)
                    if p == NPAIR - 1:
                        act.wait_ge(mt_free, SWA_MT0 + p * SWA_MT + 6 + m + 1)
                        gain_x(m, 3)

            for p in range(NPAIR):
                pair(p)
            mlp(FFN1_SLAB, FFN1_MT, FFN1_A, FFC * 4, 3, None)

        @block.vector
        def _(dve):
            def split(quad, a, b, last=N_SLABS):
                for i in range(a + LEAD, b + LEAD):
                    if isinstance(quad, int) and 4 * quad + i >= last:
                        continue
                    dve.wait_ge(w_hi, quad * 4 + (i + 1))
                    dve.tensor_tensor(wlo[:, i % RING, :], wraw[:, i % RING, :], f32(whi[:, i % RING, :]),
                                      ALU.subtract).then_inc(w_lo, 1)

            def gain_x(k, phase):
                g = C_GAIN + phase * DT + k
                dve.wait_ge(h_hi, phase * DT + k + 1)
                dve.scalar_tensor_tensor(out=hlo[:, k, :], in0=x[:, k, :], scalar=cst[:, g:g + 1],
                                         in1=f32(hhi[:, k, :]), op0=ALU.mult, op1=ALU.subtract).then_inc(h_lo, 1)

            def norm(phase):
                dve.wait_ge(rst_sq, phase + 1)
                dve.reciprocal(rst[:, :], rst[:, :]).then_inc(rst_done, 1)
                dve.wait_ge(rst_done, phase + 1)

            def read_normed(m, slab_end, out):
                dve.wait_ge(slab_used, slab_end)
                dve.tensor_tensor(blocks(out), bank_set(m), blocks(rst[:, :]), ALU.mult).then_inc(mt_free, 1)

            def add_x(k, m, slab_end):
                dve.wait_ge(slab_used, slab_end)
                dve.tensor_tensor(blocks(x[:, k, :]), bank_set(m), blocks(x[:, k, :]), ALU.add).then_inc(mt_free, 1)

            split(0, -LEAD, 0)
            for k in range(DT):
                gain_x(k, 0)

            N_SEQ = 12 + (CH + 1) + 1 + 3 + 2
            seq = [0]

            def link(h, ins):
                seq[0] += 1
                ins.then_inc(dve_seq, 1)
                dve.wait_ge(dve_seq, h * N_SEQ + seq[0])

            def rope(h, j, mt):
                cos, sin = rope_tab[:, 0, :], rope_tab[:, 1, :]
                if j == 0:
                    dve.wait_ge(tab_in, h * 48 + 48)
                dve.wait_ge(mt_free, mt + (2 * j + 2))
                dve.tensor_tensor(tmp[:, 2, :], tmp[:, 1, :], sin, ALU.mult).then_inc(dve_seq, 1)
                dve.tensor_tensor(tmp[:, 3, :], tmp[:, 0, :], sin, ALU.mult).then_inc(dve_seq, 1)
                dve.tensor_tensor(qk[:, 2 * j, :], tmp[:, 0, :], cos, ALU.mult).then_inc(dve_seq, 1)
                seq[0] += 3
                link(h, dve.tensor_tensor(qk[:, 2 * j + 1, :], tmp[:, 1, :], cos, ALU.mult))
                dve.tensor_tensor(qk[:, 2 * j, :], qk[:, 2 * j, :], tmp[:, 2, :], ALU.subtract).then_inc(dve_seq, 1)
                dve.tensor_tensor(qk[:, 2 * j + 1, :], qk[:, 2 * j + 1, :], tmp[:, 3, :], ALU.add
                                  ).then_inc(dve_seq, 1)
                seq[0] += 2

            def mask_scores(h, c):
                i = h * (CH + 1) + c
                rows = NS if c == CH else P
                dve.wait_ge(sc_done, i + 1)
                if c >= 2:
                    dve.wait_ge(o_done, i - 1)
                dve.tensor_tensor(sc_t[:, c % 2, 0:rows], ps[:, 6 + c % 2, 0:rows],
                                  hmask[:, P:P + NS] if c == CH else hmask[:, 0:P], ALU.mult).then_inc(sc_kept, 1)

            def decay_keys(h, c):
                i = h * (CH + 1) + c
                kdec = hc[:, H_KDS:H_KDS + 1] if c == CH else hc[:, H_KDEC:H_KDEC + 1]
                dve.wait_ge(kt_done, i + 1)
                if c >= 2:
                    dve.wait_ge(st_done, h * CH + (c - 1))
                dve.tensor_scalar(k_tok[:, c % 2, :], ps[:, 5, 0:DK], kdec, None, ALU.mult).then_inc(kt_kept, 1)

            def stack(h, whole, parts, low):
                link(h, dve.tensor_copy(parts, whole))
                for k, rows in enumerate(low):
                    ins = dve.tensor_tensor(parts[rows, :], whole[rows, :], f32(parts[rows, :]), ALU.subtract)
                    if k + 1 < len(low):
                        ins.then_inc(dve_seq, 1)
                        seq[0] += 1
                return ins

            def update_state(h, c):
                dve.wait_ge(st_done, h * CH + (c + 1))
                if c == 0:
                    if not isinstance(h, int) or h:
                        dve.wait_ge(sp_out, h * 16)
                    dve.tensor_copy(s_ret[:, :, :], ps[:, 0:2, :]).then_inc(s_upd, 1)
                else:
                    dve.wait_ge(s_upd, h * CH + c)
                    dve.scalar_tensor_tensor(out=s_ret[:, :, :], in0=s_ret[:, :, :],
                                             scalar=hc[:, H_CDEC:H_CDEC + 1], in1=ps[:, 0:2, :],
                                             op0=ALU.mult, op1=ALU.add).then_inc(s_upd, 1)

            def inverse_rms(h, c):
                i = h * (CH + 1) + c
                rows = NS if c == CH else P
                qdec = hc[0:rows, H_QDS:H_QDS + 1] if c == CH else hc[0:rows, H_QDEC:H_QDEC + 1]
                dve.wait_ge(rs_done, i + 1)
                link(h, dve.reciprocal(stat[0:rows, 2:3], stat[0:rows, 1:2]))
                dve.tensor_tensor(stat[0:rows, 3:4], stat[0:rows, 2:3], qdec, ALU.mult).then_inc(rr_done, 1)

            def ret_head(h, first, last):
                quad = h * (RET_SLABS // 4)
                n = h * RET_SLABS
                mt = h * RET_MT
                seq[0] = 0
                for m in range(4):
                    split(quad, 2 * m, 2 * m + 2)
                    if first and m == 0:
                        norm(0)
                    read_normed(m, n + (2 * m + 2), tmp[:, m % 2, :])
                    if m % 2:
                        rope(h, m // 2, mt)
                for m in range(4, 8):
                    split(quad, 2 * m, 2 * m + 2)
                    read_normed(m, n + (2 * m + 2), tmp[:, m - 4, :])
                dve.wait_ge(dve_seq, h * N_SEQ + seq[0])
                dve.tensor_copy(k4[:, :, :, :], qk[:, 2:4, SEQ:TOK].unsqueeze(2).to_broadcast([P, 2, 4, NS])
                                ).then_inc(four_ready, 1)
                dve.wait_ge(mt_free, mt + 8)
                dve.tensor_copy(v4[:, :, :, :], tmp[:, :, SEQ:TOK].unsqueeze(2).to_broadcast([P, 4, 4, NS])
                                ).then_inc(four_ready, 1)
                dve.wait_ge(v_kept, h * 9 + 9)
                low = slice(64, 128)
                dve.tensor_tensor(v_smp[low, :], ps[low, 4, :], f32(v_smp[low, :]), ALU.subtract).then_inc(vs_ready, 1)
                mask_scores(h, 0)
                decay_keys(h, 0)
                for c in range(CH):
                    update_state(h, c)
                    mask_scores(h, c + 1)
                    decay_keys(h, c + 1)
                    inverse_rms(h, c)
                dve.wait_ge(o_done, h * (CH + 1) + CH)
                ins = dve.memset(q_sel[:, :, :, :], 0.0)
                dve.wait_ge(kt_kept, (h + 1) * (CH + 1))
                link(h, ins)
                for b in range(NB):
                    dve.tensor_copy(q_sel[:, :, b, NT * b:NT * b + NT], qk[:, 0:2, SEQ + NT * b:SEQ + NT * b + NT]
                                    ).then_inc(sel_ready, 1)
                odd = (slice(32, 64), slice(96, 128))
                link(h, stack(h, k_tok[:, 0, :], k_smp[:, :], odd))
                dve.tensor_tensor(k_sel[:, :, :], f32(k_smp[:, :]).unsqueeze(1).to_broadcast([P, NB, DK]),
                                  cst[:, C_BM:C_BM + NB].unsqueeze(2).to_broadcast([P, NB, DK]), ALU.mult
                                  ).then_inc(sel_ready, 1)
                dve.wait_ge(sc_kept, (h + 1) * (CH + 1))
                stack(h, sc_t[:, 0, 0:NS], sc_smp[:, :], odd).then_inc(sel_ready, 1)
                for b in range(NB):
                    dve.wait_ge(sts_done, h * NB + (b + 1))
                    bank = 6 * (b % 2)
                    dve.scalar_tensor_tensor(out=s0[:, b % 4, :, :], in0=s0[:, b % 4, :, :],
                                             scalar=hc[:, H_CDS:H_CDS + 1], in1=ps[:, bank:bank + 2, :],
                                             op0=ALU.mult, op1=ALU.add).then_inc(s0_upd, 1)
                inverse_rms(h, CH)
                assert seq[0] == N_SEQ

                def gate(m):
                    dve.wait_ge(g_silu, h * 4 + (m + 1))
                    dve.wait_ge(ot_kept, (h + 1) * (CH + 1))
                    dve.tensor_tensor(qk[:, m % 2, :], qk[:, 2 + m % 2, :], o_t[:, m, :], ALU.mult).then_inc(g_of, 1)

                def gate_lo(m):
                    if m == 0:
                        for i in range(4):
                            dve.wait_ge(s0_out[i], h * 32 + 32)
                    dve.wait_ge(a_hi, h * 4 + (m + 1))
                    dve.tensor_tensor(alo[:, m, :], qk[:, m % 2, :], f32(ahi[:, m, :]), ALU.subtract
                                      ).then_inc(a_lo, 1)

                for m in range(4):
                    split(quad, 16 + 2 * m, 18 + 2 * m)
                    read_normed(8 + m, n + (18 + 2 * m), qk[:, m % 2, :])
                    gate(m)
                    gate_lo(m)
                for m in range(DT):
                    split(quad, 24 + m, 25 + m)
                    add_x(m, 12 + m, n + (25 + m))
                    if last and m:
                        gain_x(m - 1, 1)
                if last:
                    gain_x(DT - 1, 1)

            ret_head(0, True, False)
            with dve.Fori(1, RH - 1) as h:
                ret_head(h, False, False)
            ret_head(RH - 1, False, True)

            def ffn(c, slab0, mt0, a0, up0, phase, next_phase):
                quad = c * (FFN_SLABS // 4) + slab0 // 4
                n = c * FFN_SLABS + slab0

                def squares_lo(m):
                    dve.wait_ge(a_hi, c * 4 + (a0 + m + 1))
                    dve.tensor_tensor(alo[:, m, :], a2[:, m % 2, :], f32(ahi[:, m, :]), ALU.subtract
                                      ).then_inc(a_lo, 1)

                for m in range(4):
                    split(quad, 2 * m, 2 * m + 2)
                    if m == 0 and phase is not None:
                        norm(phase)
                    up = c * 4 + (up0 + m)
                    dve.wait_ge(slab_used, n + (2 * m + 2))
                    if not (isinstance(up, int) and up < 2):
                        dve.wait_ge(a2_done, up - 1)
                    dve.scalar_tensor_tensor(out=blocks(relu[:, m % 2, :]), in0=bank_set(m), scalar=0.0,
                                             in1=blocks(rst[:, :]), op0=ALU.max, op1=ALU.mult).then_inc(mt_free, 1)
                    if m:
                        squares_lo(m - 1)
                for m in range(DT):
                    split(quad, 8 + m, 9 + m)
                    if m == 0:
                        squares_lo(3)
                    add_x(m, 4 + m, n + (9 + m))
                    if next_phase is not None and m:
                        gain_x(m - 1, next_phase)
                if next_phase is not None:
                    gain_x(DT - 1, next_phase)

            def mlp(slab0, mt0, a0, up0, phase, next_phase):
                ffn(0, slab0, mt0, a0, up0, phase, None)
                with dve.Fori(1, FFC - 1) as c:
                    ffn(c, slab0, mt0, a0, up0, None, None)
                ffn(FFC - 1, slab0, mt0, a0, up0, None, next_phase)

            mlp(FFN0_SLAB, FFN0_MT, FFN0_A, 0, 1, 2)

            total = [RH * N_SEQ]

            def chain(ins):
                total[0] += 1
                ins.then_inc(dve_seq, 1)
                dve.wait_ge(dve_seq, total[0])

            def rope_head(p, m):
                i = 5 * p + m
                z = z_a[:, m % 2, :]
                gain, gain_x = (C_QN, C_QX) if m < GR else (C_KN, C_KX)
                dve.wait_ge(hroot_done, 3 * i + 3)
                dve.reciprocal(nr[:, :], nr[:, :]).then_inc(dve_seq, 1)
                total[0] += 1
                dve.wait_ge(zz_done, i + 1)
                dve.wait_ge(zs_done, i + 1)
                if m == 0:
                    dve.wait_ge(tab_in, 48 * RH + 16 * (p + 1))
                chain(dve.scalar_tensor_tensor(out=z, in0=z, scalar=cst[:, gain:gain + 1], in1=atab[:, 0, :],
                                               op0=ALU.mult, op1=ALU.mult))
                chain(dve.scalar_tensor_tensor(out=z, in0=zr[:, m % 2, :], scalar=cst[:, gain_x:gain_x + 1], in1=z,
                                               op0=ALU.mult, op1=ALU.add))
                if m < GR:
                    dve.tensor_tensor(q_a[:, m, :], z, nr[:, :], ALU.mult).then_inc(qk_ready, 1)
                else:
                    for s in range(2):
                        part = slice(HD * s, HD * (s + 1))
                        dve.tensor_tensor(k_z[part, s, :], z[part, :], nr[part, :], ALU.mult).then_inc(qk_ready, 1)

            def scale_scores(p, k):
                u = p * HU + k
                slot, lo = u % 4, P if k < 2 else 0
                st = 32 + 16 * slot
                dve.wait_ge(s_done, u + 1)
                if k >= 4:
                    dve.wait_ge(pt_done, turned(p, k - 3))
                scores = ps[:, 2 * (k % 2):2 * (k % 2) + 2, :].rearrange("p b (j n) -> p (b j) n", j=2)
                mask = acst[:, A_MASK + lo:A_MASK + 2 * P].unsqueeze(1).to_broadcast([P, GR, 2 * P - lo])
                dve.scalar_tensor_tensor(out=p_a[:, slot, :, lo:], in0=scores[:, :, lo:], scalar=HD ** -0.5,
                                         in1=mask, op0=ALU.mult, op1=ALU.add).then_inc(s_kept, 1)
                dve.wait_ge(s_kept, u + 1)
                sink = cst[:, C_SINK + PH * p + GR * (k % 2):C_SINK + PH * p + GR * (k % 2) + GR]
                chain(dve.tensor_reduce(ast[:, st + 12:st + 16], p_a[:, slot, :, lo:], AX.X, ALU.max))
                chain(dve.tensor_tensor(ast[:, st + 4:st + 8], ast[:, st + 12:st + 16], sink, ALU.max))
                chain(dve.tensor_scalar(ast[:, st:st + 4], ast[:, st + 4:st + 8], -1.0, None, ALU.mult))
                dve.tensor_tensor(ast[:, st + 8:st + 12], ast[:, st:st + 4], sink, ALU.add).then_inc(m_ready, 1)

            def denominators(p, k):
                u = p * HU + k
                st = 32 + 16 * (u % 4)
                dve.wait_ge(p_done, 5 * (u + 1))
                chain(dve.tensor_tensor(ast[:, st + 4:st + 8], ast[:, st + 4:st + 8], ast[:, st + 8:st + 12], ALU.add))
                dve.reciprocal(ast[:, st + 12:st + 16], ast[:, st + 4:st + 8]).then_inc(den_ready, 1)

            def sample_scores(p):
                chain(dve.memset(q_bd[:, :, :], 0.0))
                dve.wait_ge(qk_ready, 6 * p + 4)
                for s in range(2):
                    part = slice(HD * s, HD * (s + 1))
                    dve.tensor_copy(q_bd[part, :, 16 * s:16 * s + 16].rearrange("p b (r t) -> p r b t", r=GR),
                                    q_a[part, :, SEQ:TOK].rearrange("p r (b t) -> p r b t", b=NB)
                                    ).then_inc(qbd_ready, 1)
                dve.wait_ge(sm_in, 16 * (p + 1))
                dve.wait_ge(sas_done, p + 1)
                for k in range(3):
                    nb = min(3, NB - 3 * k)
                    view = ps[0:NS, k, 0:nb * KEYS].rearrange("p (b n) -> p b n", b=nb)
                    dve.scalar_tensor_tensor(out=sa[0:NS, 3 * k:3 * k + nb, :], in0=view, scalar=HD ** -0.5,
                                             in1=sa[0:NS, 3 * k:3 * k + nb, :], op0=ALU.mult, op1=ALU.add
                                             ).then_inc(sas_kept, 1)
                dve.wait_ge(sas_kept, 3 * (p + 1))
                sink = cst[0:NS, C_SINKS + p:C_SINKS + p + 1]
                chain(dve.tensor_reduce(ast[0:NS, 0:8], sa[0:NS, :, :], AX.X, ALU.max))
                chain(dve.tensor_scalar(ast[0:NS, 8:16], ast[0:NS, 0:8], sink, -1.0, ALU.max, ALU.mult))
                dve.tensor_scalar(ast[0:NS, 24:32], ast[0:NS, 8:16], sink, None, ALU.add).then_inc(sa_max, 1)

            def sample_probs(p):
                dve.wait_ge(sa_exp, 9 * (p + 1))
                chain(dve.tensor_tensor(ast[0:NS, 16:24], ast[0:NS, 16:24], ast[0:NS, 24:32], ALU.add))
                chain(dve.reciprocal(ast[0:NS, 0:8], ast[0:NS, 16:24]))
                dve.tensor_tensor(sa[0:NS, :, :], sa[0:NS, :, :],
                                  ast[0:NS, 0:8].unsqueeze(2).to_broadcast([NS, NB, KEYS]), ALU.mult
                                  ).then_inc(sa_ready, 1)

            def sample_out(p):
                dve.wait_ge(os_done, p + 1)
                for s in range(2):
                    part = slice(HD * s, HD * (s + 1))
                    view = ps[part, 7, 0:NB * NS].rearrange("p (b n) -> p b n", b=NB)[:, :, 16 * s:16 * s + 16]
                    dve.tensor_copy(q_a[part, :, SEQ:TOK].rearrange("p r (b t) -> p r b t", b=NB),
                                    view.rearrange("p b (r t) -> p r b t", r=GR)).then_inc(os_kept, 1)

            def pair(p):
                n = SWA_SLAB + p * SWA_SLABS
                quad = n // 4
                for m in range(6):
                    split(quad, 2 * m, 2 * m + 2)
                    if p == 0 and m == 0:
                        norm(2)
                        for s in range(2):
                            dve.memset(k_z[HD * (1 - s):HD * (2 - s), s, :], 0.0).then_inc(kz_zero, 1)
                    read_normed(m, n + 2 * m + 2, z_a[:, m % 2, :] if m < 5 else vt_a[:, :])
                    if m:
                        rope_head(p, m - 1)
                sample_scores(p)
                scale_scores(p, 0)
                sample_probs(p)
                scale_scores(p, 1)
                denominators(p, 0)
                for k in range(HU):
                    u = p * HU + k
                    if k + 1 < HU:
                        denominators(p, k + 1)
                    if k + 2 < HU:
                        scale_scores(p, k + 2)
                    if k >= 2:
                        dve.wait_ge(pt_done, turned(p, k) + 1)
                        dve.wait_ge(pv_done, u - 1)
                        dve.tensor_copy(pt_a[:, u % 2, 0, :], ps[:, 4, :]).then_inc(pt0_kept, 1)
                    if k == 1:
                        sample_out(p)
                for r in range(GR):
                    dve.wait_ge(a_hi, SWA_A + 4 * p + r + 1)
                    dve.tensor_tensor(alo[:, r, :], q_a[:, r, :], f32(ahi[:, r, :]), ALU.subtract).then_inc(a_lo, 1)
                for m in range(DT):
                    split(quad, 12 + m, 13 + m)
                    add_x(m, 6 + m, n + 13 + m)
                    if p == NPAIR - 1 and m:
                        gain_x(m - 1, 3)
                if p == NPAIR - 1:
                    gain_x(DT - 1, 3)

            dve.wait_ge(ac_in, 16)
            for p in range(NPAIR):
                pair(p)
            mlp(FFN1_SLAB, FFN1_MT, FFN1_A, FFC * 4, 3, None)

        @block.tensor
        def _(pe):
            def passes(m, slot, s, k, hi, lo, first, last):
                w = slice(k * P, (k + 1) * P)
                for j, (a, b) in enumerate(((whi, hi), (whi, lo), (wlo, hi))):
                    for t in range(NTB):
                        mm = pe.matmul(ps[:, 3 * (m % 2) + t, 0:TB], a[:, slot, w],
                                       b[:, s * KG + k, t * TB:(t + 1) * TB],
                                       start=(first and j == 0), stop=(last and j == 2))
                return mm

            def product(m, mt, quad, i0, n_slabs, hi, lo, k_ready=None, between=None):
                for s in range(n_slabs):
                    i = i0 + s
                    pe.wait_ge(w_lo, quad * 4 + (i + 1))
                    if s == 0 and not (isinstance(mt, int) and mt < 2):
                        pe.wait_ge(mt_free, mt - 1)
                    for k in range(KG):
                        if k_ready is not None:
                            pe.wait_ge(k_ready[0], k_ready[1] + (s * KG + k + 1))
                        mm = passes(m, i % RING, s, k, hi, lo, s == 0 and k == 0, s == n_slabs - 1 and k == KG - 1)
                    mm.then_inc(slab_used, 1)
                    if between is not None:
                        between(s)

            def products(m, mt, quad, i0, a0):
                for j in range(2):
                    pe.wait_ge(w_lo, quad * 4 + (i0 + j + 1))
                    pe.wait_ge(mt_free, mt + (j - 1))
                    for k in range(KG - 1):
                        if j == 0:
                            pe.wait_ge(a_lo, a0 + (k + 1))
                        passes(m + j, (i0 + j) % RING, 0, k, ahi, alo, k == 0, False)
                pe.wait_ge(a_lo, a0 + KG)
                for j in range(2):
                    passes(m + j, (i0 + j) % RING, 0, KG - 1, ahi, alo, False, True).then_inc(slab_used, 1)
                for j in range(2, DT):
                    product(m + j, mt + j, quad, i0 + j, 1, ahi, alo)

            def norm(phase, mt):
                pe.wait_ge(sum_done, (phase + 1) * DT)
                if phase:
                    pe.wait_ge(mt_free, mt - 1)
                for t in range(NTB):
                    mm = pe.matmul(ps[:, 3 + t, 0:TB], ones, ssum[:, t * TB:(t + 1) * TB], start=True, stop=True)
                mm.then_inc(ssq_done, 1)
                pe.wait_ge(rst_sq, phase + 1)

            def turn_v(h, e):
                pe.wait_ge(mt_free, h * RET_MT + (4 + e + 1))
                for half in range(2):
                    if e:
                        pe.wait_ge(v_kept, h * 9 + (2 * e + half - 1))
                    for c in range(4):
                        t = (4 * half + c) * P
                        mm = pe.transpose(ps[:, 6 + half, c * P:(c + 1) * P], tmp[:, e, t:t + P], ident)
                    mm.then_inc(v_turned, 1)

            def scores(h, c):
                i = h * (CH + 1) + c
                rows = NS if c == CH else P
                tok = slice(c * P, c * P + rows)
                if c < 2:
                    pe.wait_ge(v_kept, h * 9 + 8)
                else:
                    pe.wait_ge(sc_kept, i - 1)
                for j in range(2):
                    keys = k4[:, j, :, :].rearrange("p r t -> p (r t)") if c == CH else qk[:, 2 + j, tok]
                    mm = pe.matmul(ps[:, 6 + c % 2, 0:rows], keys, qk[:, j, tok], start=(j == 0), stop=(j == 1))
                mm.then_inc(sc_done, 1)

            def turn_k(h, c):
                i = h * (CH + 1) + c
                if not (isinstance(h, int) and i == 0):
                    pe.wait_ge(kt_kept, i)
                for j in range(2):
                    keys = k4[:, j, :, :].rearrange("p r t -> p (r t)") if c == CH else qk[:, 2 + j, c * P:(c + 1) * P]
                    mm = pe.transpose(ps[:, 5, j * P:(j + 1) * P], keys, ident)
                mm.then_inc(kt_done, 1)

            def turn_o(h, c):
                i = h * (CH + 1) + c
                pe.wait_ge(o_kept, i + 1)
                if c == 0:
                    pe.wait_ge(vs_ready, h + 1)
                else:
                    pe.wait_ge(ot_kept, i)
                for e in range(4):
                    mm = pe.transpose(ps[:, 4, e * P:(e + 1) * P], o_tok[:, e * P:(e + 1) * P], ident)
                mm.then_inc(ot_done, 1)

            def chunk(h, c):
                i = h * (CH + 1) + c
                tok = slice(c * P, (c + 1) * P)
                bank = 2 + c % 2
                if c >= 2:
                    pe.wait_ge(o_kept, i - 1)
                if c:
                    pe.wait_ge(s_upd, h * CH + c)
                    for j in range(2):
                        pe.matmul(ps[:, bank, :], qk[:, j, tok], s_ret[:, j, :], start=(j == 0), stop=False)
                pe.wait_ge(kt_kept, i + 1)
                for j in range(2):
                    mm = pe.matmul(ps[:, j, :], k_tok[:, c % 2, j * P:(j + 1) * P], v_tok[:, c, :],
                                   start=True, stop=True)
                mm.then_inc(st_done, 1)
                scores(h, c + 1)
                turn_k(h, c + 1)
                pe.wait_ge(sc_kept, i + 1)
                pe.matmul(ps[:, bank, :], sc_t[:, c % 2, :], v_tok[:, c, :], start=(c == 0), stop=True
                          ).then_inc(o_done, 1)
                if c:
                    turn_o(h, c - 1)

            def sample_heads(h):
                i = h * (CH + 1) + CH
                pe.wait_ge(sel_ready, (h + 1) * (NB + 2))
                pe.wait_ge(o_kept, i - 1)
                pe.wait_ge(sc_kept, i + 1)
                for b in range(NB):
                    pe.wait_ge(s0_in[b % 4], h * 32 + 16 * (b // 4 + 1))
                    for j in range(2):
                        pe.matmul(ps[0:NS, 2, :], q_sel[:, j, b, :], s0[:, b % 4, j, :],
                                  start=(b == 0 and j == 0), stop=False)
                    bank = 6 * (b % 2)
                    if b == 0:
                        pe.wait_ge(s_upd, (h + 1) * CH)
                    elif b >= 2:
                        pe.wait_ge(s0_upd, h * NB + (b - 1))
                    for j in range(2):
                        mm = pe.matmul(ps[:, bank + j, :], k_sel[:, b, j * P:(j + 1) * P], v_smp[:, :],
                                       start=True, stop=True)
                    mm.then_inc(sts_done, 1)
                pe.matmul(ps[0:NS, 2, :], sc_smp[:, :], v_smp[:, :], start=False, stop=True
                          ).then_inc(o_done, 1)
                turn_o(h, CH)

            def ret_head(h, first):
                quad = h * (RET_SLABS // 4)
                mt = h * RET_MT
                for m in range(8):
                    product(m, mt + m, quad, 2 * m, 2, hhi, hlo, (h_lo, 0) if first and m == 0 else None)
                    if first and m == 0:
                        norm(0, 0)
                    if m > 4:
                        turn_v(h, m - 5)
                pe.wait_ge(mt_free, mt + 8)
                turn_v(h, 3)
                pe.wait_ge(four_ready, 2 * (h + 1))
                for e in range(4):
                    mm = pe.transpose(ps[:, 4, e * P:(e + 1) * P], v4[:, e, :, :].rearrange("p r t -> p (r t)"), ident)
                mm.then_inc(v_turned, 1)
                scores(h, 0)
                turn_k(h, 0)
                for c in range(CH):
                    chunk(h, c)
                turn_o(h, CH - 1)
                sample_heads(h)
                for m in range(8, 12):
                    if m == 8:
                        pe.wait_ge(s0_upd, (h + 1) * NB)
                        pe.wait_ge(ot_kept, (h + 1) * (CH + 1))
                    product(m, mt + m, quad, 2 * m, 2, hhi, hlo)
                products(12, mt + 12, quad, 24, h * 4)

            ret_head(0, True)
            with pe.Fori(1, RH) as h:
                ret_head(h, False)

            def ffn(c, slab0, mt0, a0, phase):
                quad = c * (FFN_SLABS // 4) + slab0 // 4
                mt = c * FFN_MT + mt0
                for m in range(4):
                    first = m == 0 and phase is not None
                    product(m, mt + m, quad, 2 * m, 2, hhi, hlo, (h_lo, phase * DT) if first else None)
                    if first:
                        norm(phase, mt + 1)
                products(4, mt + 4, quad, 8, c * 4 + a0)

            def mlp(slab0, mt0, a0, phase):
                ffn(0, slab0, mt0, a0, phase)
                with pe.Fori(1, FFC) as c:
                    ffn(c, slab0, mt0, a0, None)

            mlp(FFN0_SLAB, FFN0_MT, FFN0_A, 1)

            def head_sums(p, m):
                i = 5 * p + m

                def between(s):
                    pe.wait_ge(zz_done, i + 1)
                    for t in ((0, 1), (2,))[s]:
                        if t == 2:
                            pe.wait_ge(hroot_done, 3 * i + 1)
                        elif t == 0 and m:
                            pe.wait_ge(hroot_done, 3 * i)
                            pe.wait_ge(kct_kept, 2 * (p + 1))
                        pe.matmul(ps[:, 6 + t % 2, 0:TB], bones, zz[:, t * TB:(t + 1) * TB], start=True, stop=True
                                  ).then_inc(hsum_done, 1)
                return between

            def turn_cache(p):
                pe.wait_ge(kc_in, 32 * (p + 1))
                for half in range(2):
                    for b in range(4):
                        mm = pe.transpose(ps[:, 6 + half, b * P:(b + 1) * P], kc[:, 4 * half + b, :], ident)
                    mm.then_inc(kct_done, 1)

            def sample_scores(p):
                pe.wait_ge(qbd_ready, 2 * (p + 1))
                pe.wait_ge(kct_kept, 2 * (p + 1))
                for b in range(NB):
                    col = (b % 3) * KEYS
                    pe.matmul(ps[0:NS, b // 3, col:col + P], q_bd[:, b, :], kc[:, b, :], start=True, stop=True)
                    for s in range(2):
                        mm = pe.matmul(ps[0:NS, b // 3, col + P:col + KEYS], q_bd[:, b, :], k_z[:, s, SEQ:TOK],
                                       start=(s == 0), stop=(s == 1))
                mm.then_inc(sas_done, 1)

            def sample_turn(p):
                pe.wait_ge(sa_ready, p + 1)
                for b in range(NB):
                    pe.transpose(ps[:, 7, b * NS:(b + 1) * NS], sa[0:NS, b, 0:P], ident[0:NS, 0:NS])
                for b in range(NB, 2 * NB):
                    mm = pe.transpose(ps[0:NS, 7, b * NS:(b + 1) * NS], sa[0:NS, b - NB, P:KEYS],
                                      ident[0:NS, 0:NS])
                mm.then_inc(pts_done, 1)

            def sample_out(p):
                pe.wait_ge(pts_kept, 2 * (p + 1))
                for b in range(NB):
                    out = ps[:, 7, b * NS:(b + 1) * NS]
                    pe.matmul(out, vc[:, b, :], pts[:, 0, b, :], start=True, stop=False)
                    mm = pe.matmul(out, v_a[0:NS, CH, :], pts[0:NS, 1, b, :], start=False, stop=True)
                mm.then_inc(os_done, 1)

            def block_scores(p, k):
                u, c, s = p * HU + k, k // 2, k % 2
                if k >= 2:
                    pe.wait_ge(s_kept, u - 1)
                lo = P if c == 0 else 0
                keys = slice((c - 1) * P + lo, (c + 1) * P)
                for r in range(GR):
                    col = (r % 2) * 2 * P
                    mm = pe.matmul(ps[:, 2 * s + r // 2, col + lo:col + 2 * P], q_a[:, r, c * P:(c + 1) * P],
                                   k_z[:, s, keys], start=True, stop=True)
                mm.then_inc(s_done, 1)

            def turn_probs(p, k):
                u = p * HU + k
                pe.wait_ge(pn_done, u + 1)
                for t in range(0 if k >= 2 else 1, 2):
                    if t == 0 and k > 2:
                        pe.wait_ge(pt0_kept, p * (HU - 2) + k - 2)
                    if t == 1 and k:
                        pe.wait_ge(pt1_kept, u)
                    for r in range(GR):
                        mm = pe.transpose(ps[:, 4 + t, r * P:(r + 1) * P], p_a[:, u % 4, r, t * P:(t + 1) * P], ident)
                    mm.then_inc(pt_done, 1)

            def block_out(p, k):
                u, c, s = p * HU + k, k // 2, k % 2
                pe.wait_ge(pt1_kept, u + 1)
                if k >= 2:
                    pe.wait_ge(pt0_kept, p * (HU - 2) + k - 1)
                    pe.wait_ge(out_kept, u - 1)
                elif k == 1:
                    pe.wait_ge(os_kept, 2 * (p + 1))
                for t in range(0 if c else 1, 2):
                    mm = pe.matmul(ps[:, 6 + s, :], v_a[:, c - 1 + t, :], pt_a[:, u % 2, t, :],
                                   start=(t == 0 or c == 0), stop=(t == 1))
                mm.then_inc(pv_done, 1)

            def pair(p):
                n = SWA_SLAB + p * SWA_SLABS
                mt = SWA_MT0 + p * SWA_MT
                for m in range(6):
                    first = p == 0 and m == 0
                    product(m, mt + m, n // 4, 2 * m, 2, hhi, hlo, (h_lo, 2 * DT) if first else None,
                            head_sums(p, m - 1) if m else None)
                    if first:
                        norm(2, mt + 1)
                    if m == 1:
                        pe.wait_ge(hroot_done, 15 * p + 3)
                        turn_cache(p)
                pe.wait_ge(mt_free, mt + 6)
                pe.wait_ge(hroot_done, 15 * (p + 1))
                for half in range(2):
                    for c in range(4):
                        t = (4 * half + c) * P
                        mm = pe.transpose(ps[:, 6 + half, c * P:(c + 1) * P], vt_a[:, t:t + P], ident)
                    mm.then_inc(av_turned, 1)
                pe.transpose(ps[0:NS, 4, 0:P], vt_a[:, SEQ:TOK], ident).then_inc(av_turned, 1)
                pe.wait_ge(qk_ready, 6 * (p + 1))
                for s in range(2):
                    pe.transpose(ps[:, 5, s * P:(s + 1) * P], k_z[:, s, SEQ - P:SEQ], ident)
                    mm = pe.transpose(ps[0:NS, 5, (2 + s) * P:(3 + s) * P], k_z[:, s, SEQ:TOK], ident)
                mm.then_inc(nk_done, 1)
                sample_scores(p)
                pe.wait_ge(sas_kept, 3 * (p + 1))
                block_scores(p, 0)
                block_scores(p, 1)
                for k in range(HU):
                    if k + 2 < HU:
                        block_scores(p, k + 2)
                    if k == 0:
                        pe.wait_ge(nk_kept, 4 * (p + 1))
                        pe.wait_ge(av_kept, 3 * (p + 1))
                    turn_probs(p, k)
                    if k == 0:
                        sample_turn(p)
                    elif k == 1:
                        sample_out(p)
                    if k:
                        block_out(p, k - 1)
                block_out(p, HU - 1)
                products(6, mt + 6, n // 4, 12, SWA_A + 4 * p)

            pe.wait_ge(ac_in, 16)
            for p in range(NPAIR):
                pair(p)
            mlp(FFN1_SLAB, FFN1_MT, FFN1_A, 3)


def _slab(w, rows, cols):
    return w[rows][:, cols].reshape(KG, P, P).transpose(1, 0, 2).reshape(P, KG * P)


def _weights(inputs):
    w_in, w_out = inputs["ret_w_in"][0], inputs["ret_w_out"][0]
    w_qkv, w_o = inputs["swa_w_qkv"][0], inputs["swa_w_o"][0]
    half = [np.arange(0, D // 2), np.arange(D // 2, D)]
    tile = [np.arange(m * P, (m + 1) * P) for m in range(DT)]
    slabs = []
    for h in range(RH):
        starts = [h * DK, h * DK + P, D + h * DK, D + h * DK + P]
        starts += [2 * D + h * DV + m * P for m in range(4)] + [4 * D + h * DV + m * P for m in range(4)]
        slabs += [_slab(w_in, rows, np.arange(s, s + P)) for s in starts for rows in half]
        slabs += [_slab(w_out, np.arange(h * DV, (h + 1) * DV), cols) for cols in tile]

    def ffn(layer):
        up, down = inputs["ffn_w_up"][layer], inputs["ffn_w_down"][layer]
        for c in range(FFC):
            yield from (_slab(up, rows, np.arange(c * 512 + m * P, c * 512 + (m + 1) * P))
                        for m in range(4) for rows in half)
            yield from (_slab(down, np.arange(c * 512, (c + 1) * 512), cols) for cols in tile)

    slabs += ffn(0)
    for p in range(NPAIR):
        heads = [np.concatenate([np.arange((GR * (2 * p + s) + r) * HD, (GR * (2 * p + s) + r + 1) * HD)
                                 for s in range(2)]) for r in range(GR)]
        kv = [D + KVH * HD * j + np.arange(2 * p * HD, (2 * p + 2) * HD) for j in range(2)]
        slabs += [_slab(w_qkv, rows, cols) for cols in heads + kv for rows in half]
        slabs += [_slab(w_o, np.concatenate(heads), cols) for cols in tile]
    slabs += ffn(1)
    return np.stack(slabs)


def _rope(width):
    half = width // 2
    inv = np.float32(THETA) ** (-np.arange(half, dtype=np.float32) / np.float32(half))
    pos = np.concatenate([np.arange(SEQ), np.tile(PAST + np.arange(NT), NB)]).astype(np.float32)
    ang = (inv[:, None] * pos[None, :]).astype(np.float32).astype(np.float64)
    return np.cos(ang).astype(np.float32), np.sin(ang).astype(np.float32)


def _constants():
    lg = np.log1p(-np.exp2(-5.0 - np.arange(RH)))
    i = np.arange(P)
    t, seq = np.arange(NS) % NT, np.arange(NS) // NT
    t4 = np.tile(t, 4)
    cols = np.zeros((P, C_N), np.float32)
    cols[:, C_ID:C_ID + P] = np.eye(P)
    cols[:, C_ONE:C_ONE + P] = 1.0
    cols[:, C_EPS] = EPS
    scale = DK ** -0.5
    decays = np.zeros((RH, P, 6), np.float32)
    decays[:, :, H_QDEC] = np.exp(lg[:, None] * (i + 1))
    decays[:, :, H_KDEC] = np.exp(lg[:, None] * (P - 1 - i)) * scale
    decays[:, :, H_CDEC] = np.exp(lg * P)[:, None]
    decays[:, :NS, H_QDS] = np.exp(lg[:, None] * (t + 1))
    decays[:, :, H_KDS] = np.exp(lg[:, None] * (NT - 1 - t4)) * scale
    decays[:, :, H_CDS] = np.exp(lg * NT)[:, None]
    cols[:, C_BM:C_BM + NB] = np.tile(seq, 4)[:, None] == np.arange(NB)
    masks = np.zeros((RH, P, P + NS), np.float32)
    for h in range(RH):
        masks[h, :, :P] = np.where(i[None, :] >= i[:, None], np.exp(-(i + 1.0) * lg[h])[:, None] * scale, 0.0)
        own = (seq[:, None] == seq[None, :]) & (t[None, :] >= t[:, None])
        masks[h, :, P:] = np.tile(np.where(own, np.exp(-(t + 1.0) * lg[h])[:, None] * scale, 0.0), (4, 1))
    attn = np.zeros((P, A_N), np.float32)
    attn[:, A_BO:A_BO + P] = (i[:, None] // HD) == (i[None, :] // HD)
    d = i[:, None] + P - np.arange(2 * P)[None, :]
    attn[:, A_MASK:] = np.where((d >= 0) & (d < WIN), 0.0, NEG)
    tq = np.arange(NS) % NT
    s_mask = np.full((NS, NB, KEYS), NEG, np.float32)
    d = tq[:, None] + WIN - np.arange(WIN)[None, :]
    s_mask[:, :, :WIN] = np.where((d >= 0) & (d < WIN), 0.0, NEG)[:, None, :]
    for b in range(NB):
        for j in range(NT):
            s_mask[tq >= j, b, WIN + NT * b + j] = 0.0
    cos, sin = _rope(DK)
    tables = np.stack([cos, sin], axis=1)
    cos, sin = _rope(HD)
    attn_tables = np.stack([np.concatenate([cos] * 4), np.concatenate([-sin, sin] * 2)], axis=1)
    return cols, masks, decays, attn, s_mask, tables, attn_tables


def kernel(**inputs):
    import concourse.bacc as _bacc
    from concourse.bass_utils import run_bass_kernel_spmd as _run

    inputs = {k: np.asarray(v) for k, v in inputs.items()}
    cols, masks, decays, attn, s_mask, tables, attn_tables = _constants()
    gains = [inputs["norm_mix"][0], inputs["norm_ffn"][0], inputs["norm_mix"][1], inputs["norm_ffn"][1]]
    for phase, g in enumerate(gains):
        cols[:, C_GAIN + phase * DT:C_GAIN + (phase + 1) * DT] = g.reshape(DT, P).T
    for plain, exchanged, g in ((C_QN, C_QX, inputs["swa_q_norm"][0]), (C_KN, C_KX, inputs["swa_k_norm"][0])):
        cols[:, plain] = np.concatenate([g, g])
        cols[:, exchanged] = np.concatenate([g[HD // 2:], g[:HD // 2]] * 2)
    sinks = inputs["swa_sinks"][0]
    cols[:, C_SINK:C_SINK + NPAIR * PH] = sinks[None, :]
    for p in range(NPAIR):
        cols[:NS, C_SINKS + p] = np.repeat(sinks[PH * p:PH * (p + 1)], NT)
    xs = np.concatenate([inputs["x_prompt"][0], inputs["x_sample"].reshape(NS, D)])
    data = {
        "xT": xs.T.reshape(DT, P, TOK).transpose(1, 0, 2), "weights": _weights(inputs), "tables": tables,
        "attn_tables": attn_tables, "consts": cols, "ret_masks": masks, "ret_decays": decays,
        "attn_consts": attn, "sample_mask": s_mask,
        "state_in": inputs["state_ret"][0], "cache_k": inputs["cache_swa_k"][0].reshape(NB, WIN, KVH * HD),
        "cache_v": inputs["cache_swa_v"][0].reshape(NB, WIN, KVH * HD),
    }
    outs = {
        "yT": (P, DT, TOK), "state_p": (RH, DK, DV), "kp_out": (WIN, KVH * HD), "vp_out": (WIN, KVH * HD),
        "state_s": (NB, RH, DK, DV), "ks_out": (NB, WIN, KVH * HD), "vs_out": (NB, WIN, KVH * HD),
    }
    nc = _bacc.Bacc("TRN2", target_bir_lowering=False, num_devices=1)
    arrays, args = {}, []
    for name, a in data.items():
        a = np.ascontiguousarray(a)
        arrays[f"in_{name}"] = a
        args.append(nc.dram_tensor(f"in_{name}", a.shape, mybir.dt.from_np(a.dtype), kind="ExternalInput").ap())
    for name, shape in outs.items():
        args.append(nc.dram_tensor(f"out_{name}", shape, F32, kind="ExternalOutput").ap())
    trunk(nc, *args)
    r = _run(nc, [arrays], core_ids=[0]).results[0]
    got = {name: np.asarray(r[f"out_{name}"]) for name in outs}
    y = got["yT"].transpose(1, 0, 2).reshape(D, TOK).T
    return (y[:SEQ].reshape(1, SEQ, D), y[SEQ:].reshape(NB, NT, D), got["state_p"].reshape(1, 1, RH, DK, DV),
            got["kp_out"].reshape(1, 1, WIN, KVH, HD), got["vp_out"].reshape(1, 1, WIN, KVH, HD),
            got["state_s"].reshape(1, NB, RH, DK, DV), got["ks_out"].reshape(1, NB, WIN, KVH, HD),
            got["vs_out"].reshape(1, NB, WIN, KVH, HD))
```

```python
import numpy as np
import concourse.bass as bass
from concourse import mybir
from contextlib import ExitStack

F32 = mybir.dt.float32
F32R = mybir.dt.float32r
ALU = mybir.AluOpType
ACT = mybir.ActivationFunctionType
AX = mybir.AxisListType

P = 128
D = 1024
SEQ = 1024
NB, NT = 8, 4
NS = NB * NT
TOK = SEQ + NS
TB, NTB = 352, 3
DT = D // P
RH, DK, DV = 4, 256, 512
CH = SEQ // P
PAST = 2048
WIN = 128
HD = 64
KVH = 4
NPAIR, GR = 2, 4
PH = 2 * GR
FFC = 8
EPS = 1e-6
NEG = -1e30
THETA = 10000.0

KG = 4
RING = 4
S0_RING = 3
S0_USES = [len(range(i, NB, S0_RING)) for i in range(S0_RING)]
LEAD = 3
RET_SLABS = 12 * 2 + DT
FFN_SLABS = 4 * 2 + DT
SWA_SLABS = 6 * 2 + DT
FFN0_SLAB = RH * RET_SLABS
SWA_SLAB = FFN0_SLAB + FFC * FFN_SLABS
FFN1_SLAB = SWA_SLAB + NPAIR * SWA_SLABS
N_SLABS = FFN1_SLAB + FFC * FFN_SLABS

RET_MT, FFN_MT, SWA_MT = 12 + DT, 4 + DT, 6 + DT
FFN0_MT = RH * RET_MT
SWA_MT0 = FFN0_MT + FFC * FFN_MT
FFN1_MT = SWA_MT0 + NPAIR * SWA_MT

FFN0_A = RH * 4
SWA_A = FFN0_A + FFC * 4
FFN1_A = SWA_A + NPAIR * 4

C_ID, C_ONE, C_GAIN = 0, P, 2 * P
C_EPS = C_GAIN + 4 * DT
C_BM = C_EPS + 1
C_QN, C_KN, C_QX, C_KX = (C_BM + NB + i for i in range(4))
C_SINK = C_KX + 1
C_SINKS = C_SINK + NPAIR * PH
C_N = C_SINKS + NPAIR
H_QDEC, H_KDEC, H_CDEC, H_QDS, H_KDS, H_CDS = range(6)
A_MASK, A_SEL, A_N = 0, 2 * P, 2 * P + 8
KEYS = WIN + NS


def trunk(nc, xT, weights, tables, attn_tables, consts, ret_masks, ret_decays, attn_consts, sample_mask,
          state_in, cache_k, cache_v, yT, state_p, kp_out, vp_out, state_s, ks_out, vs_out):
    with ExitStack() as ctx:
        base = (nc.sbuf_base + 31) // 32 * 32

        def at(name, offset, shape, dt):
            return nc.alloc_sbuf_tensor_at(name, shape, dt, offset=base + offset)

        TT = TOK * 4
        o_x, o_hhi, o_hlo = 0, DT * TT, 2 * DT * TT
        o_ahi = 3 * DT * TT
        o_alo = o_ahi + KG * TT
        o_wraw = o_alo + KG * TT
        o_whi = o_wraw + RING * 2048
        o_wlo = o_whi + RING * 2048
        o_rst = o_wlo + RING * 2048
        o_cst = o_rst + TT
        o_work = (o_cst + 4 * C_N + 31) // 32 * 32

        x = at("x", o_x, [P, DT, TOK], F32)
        hhi = at("hhi", o_hhi, [P, DT, TOK], F32R)
        hlo = at("hlo", o_hlo, [P, DT, TOK], F32R)
        ahi = at("ahi", o_ahi, [P, KG, TOK], F32R)
        alo = at("alo", o_alo, [P, KG, TOK], F32R)
        wraw = at("wraw", o_wraw, [P, RING, 512], F32)
        whi = at("whi", o_whi, [P, RING, 512], F32R)
        wlo = at("wlo", o_wlo, [P, RING, 512], F32R)
        rst = at("rst", o_rst, [P, TOK], F32)
        cst = at("cst", o_cst, [P, C_N], F32)
        ident = cst[:, C_ID:C_ID + P]
        ones = cst[:, C_ONE:C_ONE + P]
        eps = cst[:, C_EPS:C_EPS + 1]

        o_v = o_work + 4 * TT
        qk = at("qk", o_work, [P, 4, TOK], F32)
        v_tok = at("v_tok", o_v, [P, CH, DV], F32)
        v_smp = at("v_smp", o_v + CH * DV * 4, [P, DV], F32R)
        rope_tab = at("rope_tab", o_v, [P, 2, TOK], F32)
        o_r = o_v + (CH + 1) * DV * 4
        s_ret = at("s_ret", o_r, [P, 2, DV], F32)
        sc_t = at("sc_t", o_r + 4096, [P, 2, P], F32)
        k_tok = at("k_tok", o_r + 5120, [P, 2, DK], F32)
        o_tok = at("o_tok", o_r + 7168, [P, DV], F32)
        hmask = at("hmask", o_r + 9216, [P, P + NS], F32)
        stat = at("stat", o_r + 9856, [P, 4], F32)
        inv = at("inv", o_r + 12096, [P, 2, 18], F32)
        wide = at("wide", o_work + 6 * TT, [P, 18, HD], F32)
        hc = at("hc", o_r + 9888, [P, 6], F32)
        k_smp = at("k_smp", o_r + 9920, [P, DK], F32R)
        sc_smp = at("sc_smp", o_r + 10944, [P, NS], F32R)
        k4 = at("k4", o_r + 11072, [P, 2, 4, NS], F32)
        v4 = at("v4", o_ahi, [P, 4, 4, NS], F32)
        o_t = at("o_t", o_ahi, [P, 4, TOK], F32)
        tmp = at("tmp", o_alo, [P, 4, TOK], F32)
        s0 = at("s0", o_alo, [P, S0_RING, 2, DV], F32)
        k_sel = at("k_sel", o_alo + S0_RING * 4096, [P, 2, DK], F32R)
        q_sel = at("q_sel", o_alo + S0_RING * 4096 + 2048, [P, 2, 2, NS], F32)

        sq = at("sq", o_work, [P, 2, TOK], F32)
        ssum = at("ssum", o_work + 2 * TT, [P, TOK], F32)
        relu = at("relu", o_work + 4 * TT, [P, 2, TOK], F32)
        a2 = at("a2", o_work + 6 * TT, [P, 2, TOK], F32)

        q_a = at("q_a", o_work, [P, GR, TOK], F32)
        k_z = at("k_z", o_work + 4 * TT, [P, 2, TOK], F32)
        o_a = o_work + 6 * TT
        v_a = at("v_a", o_a, [P, CH + 1, P], F32)
        acst = at("acst", o_a + 4608, [P, A_N], F32)
        ast = at("ast", o_a + 4608 + 4 * A_N, [P, 96], F32)
        o_b = o_a + 4992 + 4 * A_N
        kc = at("kc", o_b, [P, NB, P], F32)
        vc = at("vc", o_b + 4096, [P, NB, P], F32)
        nk = at("nk", o_b + 8192, [P, 2, P], F32)
        vt_a = at("vt_a", o_b + 9216, [P, TOK], F32)
        z_a = at("z_a", o_ahi, [P, 2, TOK], F32)
        zz = at("zz", o_ahi + 2 * TT, [P, TOK], F32)
        zr = at("zr", o_ahi + 3 * TT, [P, 2, TOK], F32)
        atab = at("atab", o_ahi + 6 * TT, [P, 2, TOK], F32)
        p_a = at("p_a", o_ahi, [P, 4, GR, 2 * P], F32)
        pt_a = at("pt_a", o_ahi + 16384, [P, 2, 2, GR * P], F32)
        sa = at("sa", o_ahi + 24576, [P, NB, KEYS], F32)
        q_bd = at("q_bd", o_ahi + 29696, [P, NB, NS], F32)
        pts = at("pts", o_ahi + 30720, [P, 2, NB, NS], F32)
        head_sel = acst[:, A_SEL:A_SEL + 2]

        ps = ctx.enter_context(nc.psum_tensor("ps", [P, 8, 512], F32))

        def sem(name):
            return ctx.enter_context(nc.semaphore(name))

        w_in = [sem(f"w_in{i}") for i in range(RING)]
        w_hi = sem("w_hi")
        w_lo = sem("w_lo")
        slab_used = sem("slab_used")
        mt_free = sem("mt_free")
        c_in = sem("c_in")
        x_in = [sem(f"x_in{k}") for k in range(DT)]
        tab_in = sem("tab_in")
        h_hi = sem("h_hi")
        h_lo = sem("h_lo")
        sq_done = sem("sq_done")
        sum_done = sem("sum_done")
        msum_done = sem("msum_done")
        root_done = sem("root_done")
        inv_done = sem("inv_done")
        wide_done = sem("wide_done")
        spread_done = sem("spread_done")
        rst_done = sem("rst_done")
        zq_done = sem("zq_done")
        a2_done = sem("a2_done")
        a_hi = sem("a_hi")
        a_lo = sem("a_lo")
        dve_seq = sem("dve_seq")
        v_turned = sem("v_turned")
        v_kept = sem("v_kept")
        four_ready = sem("four_ready")
        vs_ready = sem("vs_ready")
        sc_kept = sem("sc_kept")
        kt_done = sem("kt_done")
        kt_kept = sem("kt_kept")
        st_done = sem("st_done")
        s_upd = sem("s_upd")
        o_done = sem("o_done")
        ss_done = sem("ss_done")
        rs_done = sem("rs_done")
        rr_done = sem("rr_done")
        o_kept = sem("o_kept")
        ot_done = sem("ot_done")
        ot_kept = sem("ot_kept")
        sp_out = sem("sp_out")
        sel_ready = sem("sel_ready")
        sts_done = sem("sts_done")
        s0_upd = sem("s0_upd")
        s0_in = [sem(f"s0_in{i}") for i in range(S0_RING)]
        s0_out = [sem(f"s0_out{i}") for i in range(S0_RING)]
        g_silu = sem("g_silu")
        g_of = sem("g_of")
        ac_in = sem("ac_in")
        zz_done = sem("zz_done")
        zr_in = [sem(f"zr_in{i}") for i in range(2)]
        zs_done = sem("zs_done")
        kz_zero = sem("kz_zero")
        av_turned = sem("av_turned")
        av_kept = sem("av_kept")
        nk_done = sem("nk_done")
        nk_kept = sem("nk_kept")
        kc_in = sem("kc_in")
        sm_in = sem("sm_in")
        kct_done = sem("kct_done")
        kct_kept = sem("kct_kept")
        qbd_ready = sem("qbd_ready")
        sas_done = sem("sas_done")
        sas_kept = sem("sas_kept")
        sa_max = sem("sa_max")
        sa_exp = sem("sa_exp")
        sa_ready = sem("sa_ready")
        pts_done = sem("pts_done")
        pts_kept = sem("pts_kept")
        os_done = sem("os_done")
        os_kept = sem("os_kept")
        s_done = sem("s_done")
        s_kept = sem("s_kept")
        m_ready = sem("m_ready")
        p_done = sem("p_done")
        den_ready = sem("den_ready")
        pn_done = sem("pn_done")
        pt_done = sem("pt_done")
        pt0_kept = sem("pt0_kept")
        pt1_kept = sem("pt1_kept")
        pv_done = sem("pv_done")
        out_kept = sem("out_kept")
        swa_out = sem("swa_out")
        y_out = sem("y_out")

        block = ctx.enter_context(nc.Block())

        def bank_set(m):
            return ps[:, 3 * (m % 2):3 * (m % 2) + NTB, 0:TB]

        def blocks(tile):
            return tile.rearrange("p (b t) -> p b t", b=NTB)

        HU = 2 * CH

        def turned(p, k):
            return p * (2 * HU - 2) + (k if k < 2 else 2 * k - 2)

        def f32(ap):
            return ap.bitcast(F32)

        def s0_count(h, b):
            return h * (16 * S0_USES[b % S0_RING]) + 16 * (b // S0_RING)

        PARTS = ((6, slice(0, SEQ // 2)), (7, slice(SEQ // 2, SEQ)), (6, slice(SEQ, TOK)))

        def norm_use(phase):
            return phase if phase < 3 else phase + 5 * NPAIR

        def tile_use(p, m):
            return 3 + 5 * p + m

        def score_bank(c):
            return 7 if c == CH else 5 + (c + 1) % 2

        def wide_part(part):
            bank, tok = PARTS[part]
            return ps[:, bank, P - NS:P] if part == 2 else ps[:, bank, :]

        def kept_before(p):
            return 18 * p

        @block.sync
        def _(sp):
            def slabs(quad, a, b):
                for i in range(a, b):
                    if not (isinstance(quad, int) and quad == 0 and i < RING):
                        sp.wait_ge(w_lo, quad * 4 + (i - RING + 1))
                    sp.dma_start(wraw[:, i % RING, :], weights[quad * 4 + i]).then_inc(w_in[i % RING], 16)

            sp.dma_start(x[:, 0, :], xT[:, 0, :]).then_inc(x_in[0], 16)
            sp.dma_start(cst[:, :], consts).then_inc(c_in, 16)
            for k in range(1, DT):
                if k <= RING:
                    slabs(0, k - 1, k)
                sp.dma_start(x[:, k, :], xT[:, k, :]).then_inc(x_in[k], 16)

            def store_state(h, b):
                sp.wait_ge(s0_upd, h * NB + (b + 1))
                sp.dma_start(state_s[b, h].rearrange("(j p) e -> p j e", j=2), s0[:, b % S0_RING, :, :]
                             ).then_inc(s0_out[b % S0_RING], 16)

            def load_state(h, b):
                if b >= S0_RING:
                    sp.wait_ge(s0_out[b % S0_RING], s0_count(h, b))
                sp.dma_start(s0[:, b % S0_RING, :, :], state_in[b, h].rearrange("(j p) e -> p j e", j=2)
                             ).then_inc(s0_in[b % S0_RING], 16)

            def ret_head(h, first):
                quad = h * (RET_SLABS // 4)
                if not first:
                    slabs(quad, 0, 4)
                    sp.wait_ge(ot_kept, h * (CH + 1))
                sp.dma_start(rope_tab[:, :, :], tables).then_inc(tab_in, 16)
                sp.dma_start(hmask[:, :], ret_masks[h]).then_inc(tab_in, 16)
                sp.dma_start(hc[:, :], ret_decays[h]).then_inc(tab_in, 16)
                slabs(quad, 4, 19)
                sp.wait_ge(v_turned, h * 9 + 9)
                for b in range(S0_RING):
                    load_state(h, b)
                for b in range(NB):
                    if b == NB - 1:
                        sp.wait_ge(s_upd, h * CH + CH)
                        sp.dma_start(state_p[h].rearrange("(j p) e -> p j e", j=2), s_ret[:, :, :]
                                     ).then_inc(sp_out, 16)
                    store_state(h, b)
                    if b + S0_RING < NB:
                        load_state(h, b + S0_RING)
                slabs(quad, 19, RET_SLABS)

            ret_head(0, True)
            with sp.Fori(1, RH) as h:
                ret_head(h, False)

            with sp.Fori(FFN0_SLAB // 4, SWA_SLAB // 4) as quad:
                slabs(quad, 0, 4)

            sp.wait_ge(a_lo, SWA_A)
            sp.dma_start(acst[:, :], attn_consts).then_inc(ac_in, 16)
            for p in range(NPAIR):
                quad = (SWA_SLAB + p * SWA_SLABS) // 4
                slabs(quad, 0, 4)
                sp.wait_ge(slab_used, 4 * quad)
                sp.dma_start(atab[:, :, :], attn_tables).then_inc(tab_in, 16)
                feats = slice(2 * p * HD, (2 * p + 2) * HD)
                if p:
                    sp.wait_ge(os_done, p)
                sp.dma_start(kc[:, :, :], cache_k[:, :, feats].rearrange("b k f -> k b f")).then_inc(kc_in, 16)
                sp.dma_start(vc[:, :, :], cache_v[:, :, feats].rearrange("b k f -> k b f")).then_inc(kc_in, 16)
                slabs(quad, 4, 15)
                sp.wait_ge(zq_done, kept_before(p + 1))
                sp.dma_start(sa[0:NS, :, :], sample_mask).then_inc(sm_in, 16)
                if p == 0:
                    sp.dma_start(ks_out[:, 0:WIN - NT, :], cache_k[:, NT:WIN, :]).then_inc(swa_out, 16)
                    sp.dma_start(vs_out[:, 0:WIN - NT, :], cache_v[:, NT:WIN, :]).then_inc(swa_out, 16)
                slabs(quad, 15, 19)
                sp.wait_ge(av_kept, 3 * (p + 1))
                sp.dma_start(vp_out[:, feats], v_a[:, CH - 1, :]).then_inc(swa_out, 16)
                for b in range(NB):
                    sp.dma_start(vs_out[b, WIN - NT:WIN, feats], v_a[NT * b:NT * b + NT, CH, :]
                                 ).then_inc(swa_out, 16)
                sp.wait_ge(nk_kept, 4 * (p + 1))
                sp.dma_start(kp_out[:, feats], nk[:, 0, :]).then_inc(swa_out, 16)
                for b in range(NB):
                    sp.dma_start(ks_out[b, WIN - NT:WIN, feats], nk[NT * b:NT * b + NT, 1, :]
                                 ).then_inc(swa_out, 16)
                slabs(quad, 19, SWA_SLABS)

            with sp.Fori(FFN1_SLAB // 4, N_SLABS // 4) as quad:
                slabs(quad, 0, 4)
            for m in range(DT):
                sp.wait_ge(mt_free, FFN1_MT + FFC * FFN_MT - DT + m + 1)
                sp.dma_start(yT[:, m, :], x[:, m, :]).then_inc(y_out, 16)
            sp.wait_ge(y_out, 16 * DT)
            sp.wait_ge(swa_out, 16 * (2 + NPAIR * (2 + 2 * NB)))
            sp.wait_ge(sp_out, 16 * RH)
            for i in range(S0_RING):
                sp.wait_ge(s0_out[i], s0_count(RH, i))

        @block.gpsimd
        def _(pool):
            def sum_squares(phase):
                for k in range(DT):
                    n = phase * DT + k
                    pool.wait_ge(sq_done, n + 1)
                    if k == 0:
                        if phase:
                            pool.wait_ge(msum_done, norm_use(phase - 1) + 1)
                        pool.tensor_copy(ssum[:, :], sq[:, 0, :]).then_inc(sum_done, 1)
                    else:
                        pool.wait_ge(sum_done, n)
                        pool.tensor_tensor(ssum[:, :], ssum[:, :], sq[:, k % 2, :], ALU.add).then_inc(sum_done, 1)

            sum_squares(0)
            sum_squares(1)
            sum_squares(2)
            for p in range(NPAIR):
                for m in range(5):
                    if m == 0:
                        pool.wait_ge(tab_in, 48 * RH + 16 * (p + 1))
                    pool.wait_ge(zr_in[m % 2], 64 * ((3 - m % 2) * p + m // 2 + 1))
                    pool.tensor_tensor(zr[:, m % 2, :], zr[:, m % 2, :], atab[:, 1, :], ALU.mult
                                       ).then_inc(zs_done, 1)
                for k in range(HU):
                    u = p * HU + k
                    lo = P if k < 2 else 0
                    pool.wait_ge(den_ready, u + 1)
                    inv = ast[:, 32 + 16 * (u % 4) + 12:32 + 16 * (u % 4) + 16]
                    pool.tensor_tensor(p_a[:, u % 4, :, lo:], p_a[:, u % 4, :, lo:],
                                       inv.unsqueeze(2).to_broadcast([P, GR, 2 * P - lo]), ALU.mult
                                       ).then_inc(pn_done, 1)
            sum_squares(3)

        @block.scalar
        def _(act):
            def split(quad, a, b):
                for i in range(a + LEAD, b + LEAD):
                    if isinstance(quad, int) and 4 * quad + i >= N_SLABS:
                        continue
                    act.wait_ge(w_in[i % RING], 16 * (quad + i // RING + 1))
                    if not (isinstance(quad, int) and 4 * quad + i < RING):
                        act.wait_ge(slab_used, quad * 4 + (i - RING + 1))
                    act.copy(whi[:, i % RING, :], wraw[:, i % RING, :]).then_inc(w_hi, 1)

            def gain_x(k, phase):
                g = C_GAIN + phase * DT + k
                act.mul(hhi[:, k, :], x[:, k, :], cst[:, g:g + 1]).then_inc(h_hi, 1)
                n = phase * DT + k
                if n >= 2:
                    act.wait_ge(sum_done, n - 1)
                act.activation(sq[:, k % 2, :], x[:, k, :], ACT.Square).then_inc(sq_done, 1)

            def roots(i, width):
                act.wait_ge(msum_done, i + 1)
                act.activation(inv[:, 0, :], ps[:, 7, 0:18], ACT.Sqrt, bias=eps, scale=1.0 / width
                               ).then_inc(root_done, 1)

            split(0, -LEAD, -LEAD + 1)
            act.wait_ge(c_in, 16)
            for k in range(DT):
                act.wait_ge(x_in[k], 16)
                gain_x(k, 0)
                if k < 3:
                    split(0, -LEAD + 1 + k, -LEAD + 2 + k)

            def keep_v(h, e):
                for half in range(2):
                    act.wait_ge(v_turned, h * 9 + (2 * e + half + 1))
                    act.copy(v_tok[:, 4 * half:4 * half + 4, e * P:(e + 1) * P],
                             ps[:, 6 + half, :].rearrange("p (c f) -> p c f", c=4)).then_inc(v_kept, 1)

            def keep_o(h, c):
                rows = NS if c == CH else P
                act.wait_ge(ot_done, h * (CH + 1) + (c + 1))
                act.copy(o_t[:, :, c * P:c * P + rows],
                         ps[:, 4, :].rearrange("p (e t) -> p e t", e=4)[:, :, 0:rows]).then_inc(ot_kept, 1)

            def norm_o(h, c):
                i = h * (CH + 1) + c
                rows = NS if c == CH else P
                qdec = hc[0:rows, H_QDS:H_QDS + 1] if c == CH else hc[0:rows, H_QDEC:H_QDEC + 1]
                bank = 7 if c == CH else 2 + c % 2
                act.wait_ge(o_done, i + 1)
                if not (isinstance(h, int) and i == 0):
                    act.wait_ge(ot_done, i)
                act.activation(o_tok[0:rows, :], ps[0:rows, bank, :], ACT.Square, scale=qdec,
                               accum_out=stat[0:rows, 0:1]).then_inc(ss_done, 1)
                act.wait_ge(ss_done, i + 1)
                act.activation(stat[0:rows, 1:2], stat[0:rows, 0:1], ACT.Sqrt, bias=eps[0:rows, :], scale=1.0 / DV
                               ).then_inc(rs_done, 1)
                if c:
                    keep_o(h, c - 1)
                act.wait_ge(rr_done, i + 1)
                act.mul(o_tok[0:rows, :], ps[0:rows, bank, :], stat[0:rows, 3:4]).then_inc(o_kept, 1)

            def ret_head(h, first, last):
                quad = h * (RET_SLABS // 4)
                mt = h * RET_MT
                split(quad, 1 if first else 0, 2)
                if first:
                    roots(norm_use(0), D)
                split(quad, 2, 8)
                for e in range(4):
                    split(quad, 8 + 2 * e, 10 + 2 * e)
                    if e:
                        keep_v(h, e - 1)
                keep_v(h, 3)
                act.wait_ge(v_turned, h * 9 + 9)
                act.copy(v_smp[:, :], ps[:, 4, :]).then_inc(v_kept, 1)
                for c in range(CH + 1):
                    norm_o(h, c)
                keep_o(h, CH)
                for m in range(4):
                    split(quad, 16 + 2 * m, 18 + 2 * m)
                    act.wait_ge(mt_free, mt + (8 + m + 1))
                    act.activation(qk[:, 2 + m % 2, :], qk[:, m % 2, :], ACT.Silu).then_inc(g_silu, 1)
                    act.wait_ge(g_of, h * 4 + (m + 1))
                    act.copy(ahi[:, m, :], qk[:, m % 2, :]).then_inc(a_hi, 1)
                for m in range(DT):
                    split(quad, 24 + m, 25 + m)
                    if last:
                        act.wait_ge(mt_free, mt + (12 + m + 1))
                        gain_x(m, 1)

            ret_head(0, True, False)
            with act.Fori(1, RH - 1) as h:
                ret_head(h, False, False)
            ret_head(RH - 1, False, True)

            def ffn(c, slab0, mt0, a0, up0, phase, next_phase):
                quad = c * (FFN_SLABS // 4) + slab0 // 4
                for m in range(4):
                    up = c * 4 + (up0 + m)
                    split(quad, 2 * m, 2 * m + 2)
                    if m == 0 and phase is not None:
                        roots(norm_use(phase), D)
                    act.wait_ge(mt_free, c * FFN_MT + (mt0 + m + 1))
                    act.wait_ge(a_lo, c * 4 + (a0 + m - 1))
                    act.activation(a2[:, m % 2, :], relu[:, m % 2, :], ACT.Square).then_inc(a2_done, 1)
                    act.wait_ge(a2_done, up + 1)
                    act.copy(ahi[:, m, :], a2[:, m % 2, :]).then_inc(a_hi, 1)
                for m in range(DT):
                    split(quad, 8 + m, 9 + m)
                    if next_phase is not None:
                        act.wait_ge(mt_free, c * FFN_MT + (mt0 + 4 + m + 1))
                        gain_x(m, next_phase)

            def mlp(slab0, mt0, a0, up0, phase, next_phase):
                ffn(0, slab0, mt0, a0, up0, phase, None)
                with act.Fori(1, FFC - 1) as c:
                    ffn(c, slab0, mt0, a0, up0, None, None)
                ffn(FFC - 1, slab0, mt0, a0, up0, None, next_phase)

            mlp(FFN0_SLAB, FFN0_MT, FFN0_A, 0, 1, 2)

            def square_head(p, m):
                act.wait_ge(mt_free, SWA_MT0 + p * SWA_MT + m + 1)
                for half in range(0, P, HD):
                    for a, b in ((0, HD // 2), (HD // 2, 0)):
                        act.dma_start(zr[half + a:half + a + HD // 2, m % 2, :],
                                      z_a[half + b:half + b + HD // 2, m % 2, :]).then_inc(zr_in[m % 2], 16)
                act.activation(zz[:, :], z_a[:, m % 2, :], ACT.Square).then_inc(zz_done, 1)

            def exponentials(u, k):
                slot, lo = u % 4, P if k < 2 else 0
                st = 32 + 16 * slot
                act.wait_ge(m_ready, u + 1)
                for j in range(GR):
                    act.activation(p_a[:, slot, j, lo:], p_a[:, slot, j, lo:], ACT.Exp,
                                   bias=ast[:, st + j:st + j + 1], accum_out=ast[:, st + 4 + j:st + 5 + j]
                                   ).then_inc(p_done, 1)
                act.activation(ast[:, st + 8:st + 12], ast[:, st + 8:st + 12], ACT.Exp).then_inc(p_done, 1)

            def keep_out(u, k):
                rows = slice(HD * (k % 2), HD * (k % 2 + 1))
                c = k // 2
                act.wait_ge(pv_done, u + 1)
                act.copy(q_a[rows, :, c * P:(c + 1) * P],
                         ps[rows, 6 + k % 2, :].rearrange("p (r t) -> p r t", r=GR)).then_inc(out_kept, 1)

            def pair(p):
                quad = (SWA_SLAB + p * SWA_SLABS) // 4
                for m in range(6):
                    split(quad, 2 * m, 2 * m + 1)
                    if m > 1:
                        roots(tile_use(p, m - 1), HD)
                    elif m == 1 and p:
                        roots(tile_use(p, 0), HD)
                    split(quad, 2 * m + 1, 2 * m + 2)
                    if m == 0:
                        for half in range(2):
                            act.wait_ge(kct_done, 2 * p + half + 1)
                            act.copy(kc[:, 4 * half:4 * half + 4, :],
                                     ps[:, 6 + half, :].rearrange("p (b f) -> p b f", b=4)).then_inc(kct_kept, 1)
                        if p == 0:
                            roots(norm_use(2), D)
                    elif m == 1 and p == 0:
                        roots(tile_use(0, 0), HD)
                    if m < 5:
                        square_head(p, m)
                if p:
                    act.wait_ge(swa_out, 16 * (2 + p * (2 + 2 * NB)))
                for half in range(2):
                    act.wait_ge(av_turned, 3 * p + half + 1)
                    act.copy(v_a[:, 4 * half:4 * half + 4, :],
                             ps[:, half, :].rearrange("p (c f) -> p c f", c=4)).then_inc(av_kept, 1)
                act.wait_ge(av_turned, 3 * p + 3)
                act.copy(v_a[0:NS, CH, :], ps[0:NS, 2, 0:P]).then_inc(av_kept, 1)
                act.wait_ge(nk_done, p + 1)
                for s in range(2):
                    col, f = s * P + s * HD, slice(s * HD, (s + 1) * HD)
                    act.copy(nk[:, 0, f], ps[:, 7, col:col + HD]).then_inc(nk_kept, 1)
                    act.copy(nk[0:NS, 1, f], ps[0:NS, 7, 2 * P + col:2 * P + col + HD]).then_inc(nk_kept, 1)
                exponentials(p * HU, 0)
                exponentials(p * HU + 1, 1)
                for k in range(HU):
                    u = p * HU + k
                    if k >= 2:
                        keep_out(u - 2, k - 2)
                    if 0 < k < HU - 2:
                        exponentials(u + 2, k + 2)
                    act.wait_ge(pt_done, turned(p, k + 1))
                    if k >= 2:
                        act.wait_ge(pv_done, u - 1)
                    act.copy(pt_a[:, u % 2, 1, :], ps[:, 5, :]).then_inc(pt1_kept, 1)
                    if k == 0:
                        exponentials(u + 2, 2)
                        act.wait_ge(sa_max, p + 1)
                        for b in range(NB):
                            act.activation(sa[0:NS, b, :], sa[0:NS, b, :], ACT.Exp, bias=ast[0:NS, 8 + b:9 + b],
                                           accum_out=ast[0:NS, 16 + b:17 + b]).then_inc(sa_exp, 1)
                        act.activation(ast[0:NS, 24:32], ast[0:NS, 24:32], ACT.Exp).then_inc(sa_exp, 1)
                    elif k == 2:
                        act.wait_ge(pts_done, p + 1)
                        act.copy(pts[:, 0, :, :], ps[:, 7, 0:NB * NS].rearrange("p (b n) -> p b n", b=NB)
                                 ).then_inc(pts_kept, 1)
                        act.copy(pts[0:NS, 1, :, :], ps[0:NS, 7, NB * NS:].rearrange("p (b n) -> p b n", b=NB)
                                 ).then_inc(pts_kept, 1)
                keep_out((p + 1) * HU - 2, HU - 2)
                keep_out((p + 1) * HU - 1, HU - 1)
                act.wait_ge(out_kept, HU * (p + 1))
                act.wait_ge(os_kept, 2 * (p + 1))
                for r in range(GR):
                    act.copy(ahi[:, r, :], q_a[:, r, :]).then_inc(a_hi, 1)
                for m in range(DT):
                    split(quad, 12 + m, 13 + m)
                    if p == NPAIR - 1:
                        act.wait_ge(mt_free, SWA_MT0 + p * SWA_MT + 6 + m + 1)
                        gain_x(m, 3)

            for p in range(NPAIR):
                pair(p)
            mlp(FFN1_SLAB, FFN1_MT, FFN1_A, FFC * 4, 3, None)

        @block.vector
        def _(dve):
            def split(quad, a, b):
                for i in range(a + LEAD, b + LEAD):
                    if isinstance(quad, int) and 4 * quad + i >= N_SLABS:
                        continue
                    dve.wait_ge(w_hi, quad * 4 + (i + 1))
                    dve.tensor_tensor(wlo[:, i % RING, :], wraw[:, i % RING, :], f32(whi[:, i % RING, :]),
                                      ALU.subtract).then_inc(w_lo, 1)

            def gain_x(k, phase):
                g = C_GAIN + phase * DT + k
                dve.wait_ge(h_hi, phase * DT + k + 1)
                dve.scalar_tensor_tensor(out=hlo[:, k, :], in0=x[:, k, :], scalar=cst[:, g:g + 1],
                                         in1=f32(hhi[:, k, :]), op0=ALU.mult, op1=ALU.subtract).then_inc(h_lo, 1)

            def inverses(i):
                dve.wait_ge(root_done, i + 1)
                dve.reciprocal(inv[:, 1, :], inv[:, 0, :]).then_inc(inv_done, 1)
                if i:
                    dve.wait_ge(spread_done, 3 * i)
                dve.wait_ge(inv_done, i + 1)
                dve.tensor_copy(wide[:, :, :], inv[:, 1, :].unsqueeze(2).to_broadcast([P, 18, HD])
                                ).then_inc(wide_done, 1)

            def norm(phase):
                i = norm_use(phase)
                inverses(i)
                for part, (bank, tok) in enumerate(PARTS):
                    dve.wait_ge(spread_done, 3 * i + part + 1)
                    dve.tensor_copy(rst[:, tok], wide_part(part)).then_inc(rst_done, 1)
                dve.wait_ge(rst_done, 3 * (phase + 1))

            def read_normed(m, slab_end, out):
                dve.wait_ge(slab_used, slab_end)
                dve.tensor_tensor(blocks(out), bank_set(m), blocks(rst[:, :]), ALU.mult).then_inc(mt_free, 1)

            def add_x(k, m, slab_end):
                dve.wait_ge(slab_used, slab_end)
                dve.tensor_tensor(blocks(x[:, k, :]), bank_set(m), blocks(x[:, k, :]), ALU.add).then_inc(mt_free, 1)

            split(0, -LEAD, -LEAD + 1)
            for k in range(DT):
                gain_x(k, 0)
                if k < 3:
                    split(0, -LEAD + 1 + k, -LEAD + 2 + k)

            N_SEQ = 12 + (CH + 1) + 3 + 2 + NB
            seq = [0]

            def link(h, ins):
                seq[0] += 1
                ins.then_inc(dve_seq, 1)
                dve.wait_ge(dve_seq, h * N_SEQ + seq[0])

            def rope(h, j, mt):
                cos, sin = rope_tab[:, 0, :], rope_tab[:, 1, :]
                if j == 0:
                    dve.wait_ge(tab_in, h * 48 + 48)
                dve.wait_ge(mt_free, mt + (2 * j + 2))
                dve.tensor_tensor(tmp[:, 2, :], tmp[:, 1, :], sin, ALU.mult).then_inc(dve_seq, 1)
                dve.tensor_tensor(tmp[:, 3, :], tmp[:, 0, :], sin, ALU.mult).then_inc(dve_seq, 1)
                dve.tensor_tensor(qk[:, 2 * j, :], tmp[:, 0, :], cos, ALU.mult).then_inc(dve_seq, 1)
                seq[0] += 3
                link(h, dve.tensor_tensor(qk[:, 2 * j + 1, :], tmp[:, 1, :], cos, ALU.mult))
                dve.tensor_tensor(qk[:, 2 * j, :], qk[:, 2 * j, :], tmp[:, 2, :], ALU.subtract).then_inc(dve_seq, 1)
                dve.tensor_tensor(qk[:, 2 * j + 1, :], qk[:, 2 * j + 1, :], tmp[:, 3, :], ALU.add
                                  ).then_inc(dve_seq, 1)
                seq[0] += 2

            def mask_scores(h, c):
                n = h * (CH + 1) + (1 if c == CH else c + 2)
                rows = NS if c == CH else P
                dve.wait_ge(kt_done, n)
                if 2 <= c < CH:
                    dve.wait_ge(o_done, h * (CH + 1) + (c - 1))
                dve.tensor_tensor(sc_t[:, c % 2, 0:rows], ps[:, score_bank(c), DK:DK + rows],
                                  hmask[:, P:P + NS] if c == CH else hmask[:, 0:P], ALU.mult).then_inc(sc_kept, 1)

            def decay_keys(h, c):
                n = h * (CH + 1) + (1 if c == CH else c + 2)
                kdec = hc[:, H_KDS:H_KDS + 1] if c == CH else hc[:, H_KDEC:H_KDEC + 1]
                dve.wait_ge(kt_done, n)
                if 2 <= c < CH:
                    dve.wait_ge(st_done, h * CH + (c - 1))
                dve.tensor_scalar(k_tok[:, c % 2, :], ps[:, score_bank(c), 0:DK], kdec, None, ALU.mult
                                  ).then_inc(kt_kept, 1)

            def select(h, b):
                dve.tensor_scalar(k_sel[:, b % 2, :], f32(k_smp[:, :]), cst[:, C_BM + b:C_BM + b + 1], None, ALU.mult
                                  ).then_inc(sel_ready, 1)
                link(h, dve.memset(q_sel[:, b % 2, :, :], 0.0))
                dve.tensor_copy(q_sel[:, b % 2, :, NT * b:NT * b + NT], qk[:, 0:2, SEQ + NT * b:SEQ + NT * b + NT]
                                ).then_inc(sel_ready, 1)

            def update_sample(h, b):
                dve.wait_ge(sts_done, h * NB + (b + 1))
                dve.scalar_tensor_tensor(out=s0[:, b % S0_RING, :, :], in0=s0[:, b % S0_RING, :, :],
                                         scalar=hc[:, H_CDS:H_CDS + 1], in1=ps[:, 0:2, :],
                                         op0=ALU.mult, op1=ALU.add).then_inc(s0_upd, 1)

            def stack(h, whole, parts, low):
                link(h, dve.tensor_copy(parts, whole))
                for k, rows in enumerate(low):
                    ins = dve.tensor_tensor(parts[rows, :], whole[rows, :], f32(parts[rows, :]), ALU.subtract)
                    if k + 1 < len(low):
                        ins.then_inc(dve_seq, 1)
                        seq[0] += 1
                return ins

            def update_state(h, c):
                dve.wait_ge(st_done, h * CH + (c + 1))
                if c == 0:
                    if not isinstance(h, int) or h:
                        dve.wait_ge(sp_out, h * 16)
                    dve.tensor_copy(s_ret[:, :, :], ps[:, 0:2, :]).then_inc(s_upd, 1)
                else:
                    dve.wait_ge(s_upd, h * CH + c)
                    dve.scalar_tensor_tensor(out=s_ret[:, :, :], in0=s_ret[:, :, :],
                                             scalar=hc[:, H_CDEC:H_CDEC + 1], in1=ps[:, 0:2, :],
                                             op0=ALU.mult, op1=ALU.add).then_inc(s_upd, 1)

            def inverse_rms(h, c):
                i = h * (CH + 1) + c
                rows = NS if c == CH else P
                qdec = hc[0:rows, H_QDS:H_QDS + 1] if c == CH else hc[0:rows, H_QDEC:H_QDEC + 1]
                dve.wait_ge(rs_done, i + 1)
                link(h, dve.reciprocal(stat[0:rows, 2:3], stat[0:rows, 1:2]))
                dve.tensor_tensor(stat[0:rows, 3:4], stat[0:rows, 2:3], qdec, ALU.mult).then_inc(rr_done, 1)

            def ret_head(h, first, last):
                quad = h * (RET_SLABS // 4)
                n = h * RET_SLABS
                mt = h * RET_MT
                seq[0] = 0
                for m in range(4):
                    split(quad, 1 if first and m == 0 else 2 * m, 2 * m + 2)
                    if first and m == 0:
                        norm(0)
                    read_normed(m, n + (3 if first and m == 0 else 2 * m + 2), tmp[:, m % 2, :])
                    if m % 2:
                        rope(h, m // 2, mt)
                odd = (slice(32, 64), slice(96, 128))
                for m in range(4, 8):
                    split(quad, 2 * m, 2 * m + 2)
                    if m == 4:
                        dve.wait_ge(dve_seq, h * N_SEQ + seq[0])
                        dve.tensor_copy(k4[:, :, :, :], qk[:, 2:4, SEQ:TOK].unsqueeze(2).to_broadcast([P, 2, 4, NS])
                                        ).then_inc(four_ready, 1)
                    elif m == 5:
                        mask_scores(h, CH)
                        decay_keys(h, CH)
                        dve.wait_ge(sc_kept, h * (CH + 1) + 1)
                        stack(h, sc_t[:, 0, 0:NS], sc_smp[:, :], odd).then_inc(sel_ready, 1)
                        dve.wait_ge(kt_kept, h * (CH + 1) + 1)
                        link(h, stack(h, k_tok[:, 0, :], k_smp[:, :], odd))
                    read_normed(m, n + (2 * m + 2), tmp[:, m - 4, :])
                    dve.wait_ge(mt_free, mt + (m + 1))
                    dve.tensor_copy(v4[:, m - 4, :, :], tmp[:, m - 4, SEQ:TOK].unsqueeze(1).to_broadcast([P, 4, NS])
                                    ).then_inc(four_ready, 1)
                mask_scores(h, 0)
                decay_keys(h, 0)
                dve.wait_ge(v_kept, h * 9 + 9)
                low = slice(64, 128)
                dve.tensor_tensor(v_smp[low, :], ps[low, 4, :], f32(v_smp[low, :]), ALU.subtract).then_inc(vs_ready, 1)
                select(h, 0)
                for c in range(CH):
                    update_state(h, c)
                    if c + 1 < CH:
                        mask_scores(h, c + 1)
                        decay_keys(h, c + 1)
                        select(h, c + 1)
                    inverse_rms(h, c)
                    update_sample(h, c)
                inverse_rms(h, CH)
                assert seq[0] == N_SEQ

                def gate(m):
                    dve.wait_ge(g_silu, h * 4 + (m + 1))
                    dve.wait_ge(ot_kept, (h + 1) * (CH + 1))
                    dve.tensor_tensor(qk[:, m % 2, :], qk[:, 2 + m % 2, :], o_t[:, m, :], ALU.mult).then_inc(g_of, 1)

                def gate_lo(m):
                    if m == 0:
                        for i in range(S0_RING):
                            dve.wait_ge(s0_out[i], s0_count(h, i) + 16 * S0_USES[i])
                    dve.wait_ge(a_hi, h * 4 + (m + 1))
                    dve.tensor_tensor(alo[:, m, :], qk[:, m % 2, :], f32(ahi[:, m, :]), ALU.subtract
                                      ).then_inc(a_lo, 1)

                for m in range(4):
                    split(quad, 16 + 2 * m, 18 + 2 * m)
                    read_normed(8 + m, n + (18 + 2 * m), qk[:, m % 2, :])
                    gate(m)
                    gate_lo(m)
                for m in range(DT):
                    split(quad, 24 + m, 25 + m)
                    add_x(m, 12 + m, n + (25 + m))
                    if last and m:
                        gain_x(m - 1, 1)
                if last:
                    gain_x(DT - 1, 1)

            ret_head(0, True, False)
            with dve.Fori(1, RH - 1) as h:
                ret_head(h, False, False)
            ret_head(RH - 1, False, True)

            def ffn(c, slab0, mt0, a0, up0, phase, next_phase):
                quad = c * (FFN_SLABS // 4) + slab0 // 4
                n = c * FFN_SLABS + slab0

                def squares_lo(m):
                    dve.wait_ge(a_hi, c * 4 + (a0 + m + 1))
                    dve.tensor_tensor(alo[:, m, :], a2[:, m % 2, :], f32(ahi[:, m, :]), ALU.subtract
                                      ).then_inc(a_lo, 1)

                for m in range(4):
                    split(quad, 2 * m, 2 * m + 2)
                    if m == 0 and phase is not None:
                        norm(phase)
                    up = c * 4 + (up0 + m)
                    dve.wait_ge(slab_used, n + (2 * m + 2))
                    if not (isinstance(up, int) and up < 2):
                        dve.wait_ge(a2_done, up - 1)
                    dve.scalar_tensor_tensor(out=blocks(relu[:, m % 2, :]), in0=bank_set(m), scalar=0.0,
                                             in1=blocks(rst[:, :]), op0=ALU.max, op1=ALU.mult).then_inc(mt_free, 1)
                    if m:
                        squares_lo(m - 1)
                for m in range(DT):
                    split(quad, 8 + m, 9 + m)
                    if m == 0:
                        squares_lo(3)
                    add_x(m, 4 + m, n + (9 + m))
                    if next_phase is not None and m:
                        gain_x(m - 1, next_phase)
                if next_phase is not None:
                    gain_x(DT - 1, next_phase)

            def mlp(slab0, mt0, a0, up0, phase, next_phase):
                ffn(0, slab0, mt0, a0, up0, phase, None)
                with dve.Fori(1, FFC - 1) as c:
                    ffn(c, slab0, mt0, a0, up0, None, None)
                ffn(FFC - 1, slab0, mt0, a0, up0, None, next_phase)

            mlp(FFN0_SLAB, FFN0_MT, FFN0_A, 0, 1, 2)

            total = [RH * N_SEQ]

            def chain(ins):
                total[0] += 1
                ins.then_inc(dve_seq, 1)
                dve.wait_ge(dve_seq, total[0])

            def rope_head(p, m):
                z = z_a[:, m % 2, :]
                gain, exchanged = (C_QN, C_QX) if m < GR else (C_KN, C_KX)
                dve.wait_ge(zz_done, 5 * p + m + 1)
                dve.wait_ge(zs_done, 5 * p + m + 1)
                if m == 0:
                    dve.wait_ge(tab_in, 48 * RH + 16 * (p + 1))
                chain(dve.scalar_tensor_tensor(out=z, in0=z, scalar=cst[:, gain:gain + 1], in1=atab[:, 0, :],
                                               op0=ALU.mult, op1=ALU.mult))
                chain(dve.scalar_tensor_tensor(out=z, in0=zr[:, m % 2, :], scalar=cst[:, exchanged:exchanged + 1],
                                               in1=z, op0=ALU.mult, op1=ALU.add))

            def finish_head(p, m, part):
                tok = PARTS[part][1]
                dve.wait_ge(spread_done, 3 * tile_use(p, m) + part + 1)
                if m < GR:
                    dve.tensor_tensor(q_a[:, m, tok], z_a[:, m % 2, tok], wide_part(part), ALU.mult
                                      ).then_inc(zq_done, 1)
                else:
                    for s in range(2):
                        half = slice(HD * s, HD * (s + 1))
                        dve.tensor_tensor(k_z[half, s, tok], z_a[half, m % 2, tok], wide_part(part)[half], ALU.mult
                                          ).then_inc(zq_done, 1)

            def scale_scores(p, k):
                u = p * HU + k
                slot, lo = u % 4, P if k < 2 else 0
                st = 32 + 16 * slot
                dve.wait_ge(s_done, u + 1)
                if k >= 4:
                    dve.wait_ge(pt_done, turned(p, k - 3))
                scores = ps[:, 2 * (k % 2):2 * (k % 2) + 2, :].rearrange("p b (j n) -> p (b j) n", j=2)
                mask = acst[:, A_MASK + lo:A_MASK + 2 * P].unsqueeze(1).to_broadcast([P, GR, 2 * P - lo])
                dve.scalar_tensor_tensor(out=p_a[:, slot, :, lo:], in0=scores[:, :, lo:], scalar=HD ** -0.5,
                                         in1=mask, op0=ALU.mult, op1=ALU.add).then_inc(s_kept, 1)
                dve.wait_ge(s_kept, u + 1)
                sink = cst[:, C_SINK + PH * p + GR * (k % 2):C_SINK + PH * p + GR * (k % 2) + GR]
                chain(dve.tensor_reduce(ast[:, st + 12:st + 16], p_a[:, slot, :, lo:], AX.X, ALU.max))
                chain(dve.tensor_tensor(ast[:, st + 4:st + 8], ast[:, st + 12:st + 16], sink, ALU.max))
                chain(dve.tensor_scalar(ast[:, st:st + 4], ast[:, st + 4:st + 8], -1.0, None, ALU.mult))
                dve.tensor_tensor(ast[:, st + 8:st + 12], ast[:, st:st + 4], sink, ALU.add).then_inc(m_ready, 1)

            def denominators(p, k):
                u = p * HU + k
                st = 32 + 16 * (u % 4)
                dve.wait_ge(p_done, 5 * (u + 1))
                chain(dve.tensor_tensor(ast[:, st + 4:st + 8], ast[:, st + 4:st + 8], ast[:, st + 8:st + 12], ALU.add))
                dve.reciprocal(ast[:, st + 12:st + 16], ast[:, st + 4:st + 8]).then_inc(den_ready, 1)

            def sample_queries(p):
                chain(dve.memset(q_bd[:, :, :], 0.0))
                dve.wait_ge(zq_done, kept_before(p) + 3 * GR)
                for s in range(2):
                    part = slice(HD * s, HD * (s + 1))
                    dve.tensor_copy(q_bd[part, :, 16 * s:16 * s + 16].rearrange("p b (r t) -> p r b t", r=GR),
                                    q_a[part, :, SEQ:TOK].rearrange("p r (b t) -> p r b t", b=NB)
                                    ).then_inc(qbd_ready, 1)

            def sample_scores(p):
                dve.wait_ge(sm_in, 16 * (p + 1))
                dve.wait_ge(sas_done, p + 1)
                for k in range(3):
                    nb = min(3, NB - 3 * k)
                    view = ps[0:NS, 4 + k, 0:nb * KEYS].rearrange("p (b n) -> p b n", b=nb)
                    dve.scalar_tensor_tensor(out=sa[0:NS, 3 * k:3 * k + nb, :], in0=view, scalar=HD ** -0.5,
                                             in1=sa[0:NS, 3 * k:3 * k + nb, :], op0=ALU.mult, op1=ALU.add
                                             ).then_inc(sas_kept, 1)
                dve.wait_ge(sas_kept, 3 * (p + 1))
                sink = cst[0:NS, C_SINKS + p:C_SINKS + p + 1]
                chain(dve.tensor_reduce(ast[0:NS, 0:8], sa[0:NS, :, :], AX.X, ALU.max))
                chain(dve.tensor_scalar(ast[0:NS, 8:16], ast[0:NS, 0:8], sink, -1.0, ALU.max, ALU.mult))
                dve.tensor_scalar(ast[0:NS, 24:32], ast[0:NS, 8:16], sink, None, ALU.add).then_inc(sa_max, 1)

            def sample_probs(p):
                dve.wait_ge(sa_exp, 9 * (p + 1))
                chain(dve.tensor_tensor(ast[0:NS, 16:24], ast[0:NS, 16:24], ast[0:NS, 24:32], ALU.add))
                chain(dve.reciprocal(ast[0:NS, 0:8], ast[0:NS, 16:24]))
                dve.tensor_tensor(sa[0:NS, :, :], sa[0:NS, :, :],
                                  ast[0:NS, 0:8].unsqueeze(2).to_broadcast([NS, NB, KEYS]), ALU.mult
                                  ).then_inc(sa_ready, 1)

            def sample_out(p):
                dve.wait_ge(os_done, p + 1)
                for s in range(2):
                    part = slice(HD * s, HD * (s + 1))
                    view = ps[part, 7, 0:NB * NS].rearrange("p (b n) -> p b n", b=NB)[:, :, 16 * s:16 * s + 16]
                    dve.tensor_copy(q_a[part, :, SEQ:TOK].rearrange("p r (b t) -> p r b t", b=NB),
                                    view.rearrange("p b (r t) -> p r b t", r=GR)).then_inc(os_kept, 1)

            def pair(p):
                n = SWA_SLAB + p * SWA_SLABS
                quad = n // 4
                if p == 0:
                    for s in range(2):
                        dve.memset(k_z[HD * (1 - s):HD * (2 - s), s, :], 0.0).then_inc(kz_zero, 1)
                for m in range(6):
                    split(quad, 2 * m, 2 * m + 1)
                    early = p or m > 1
                    if m == 2 and p == 0:
                        for part in range(3):
                            finish_head(0, 0, part)
                    if m and early:
                        inverses(tile_use(p, m - 1))
                    split(quad, 2 * m + 1, 2 * m + 2)
                    if m == 0 and p == 0:
                        norm(2)
                    if m > 2 or m == 2 and p:
                        finish_head(p, m - 2, 2)
                    if m and early:
                        rope_head(p, m - 1)
                    read_normed(m, n + 2 * m + 2, z_a[:, m % 2, :] if m < 5 else vt_a[:, :])
                    if m == 5:
                        sample_queries(p)
                    if m and early:
                        finish_head(p, m - 1, 0)
                        finish_head(p, m - 1, 1)
                    elif m:
                        inverses(tile_use(0, 0))
                        rope_head(0, 0)
                finish_head(p, 4, 2)
                scale_scores(p, 0)
                scale_scores(p, 1)
                denominators(p, 0)
                sample_scores(p)
                denominators(p, 1)
                scale_scores(p, 2)
                for k in range(HU):
                    u = p * HU + k
                    if k + 3 < HU:
                        scale_scores(p, k + 3)
                    if k == 3:
                        sample_out(p)
                    if k + 2 < HU:
                        denominators(p, k + 2)
                    if k == 1:
                        sample_probs(p)
                    if k >= 2:
                        dve.wait_ge(pt_done, turned(p, k) + 1)
                        dve.wait_ge(pv_done, u - 1)
                        dve.tensor_copy(pt_a[:, u % 2, 0, :], ps[:, 4, :]).then_inc(pt0_kept, 1)
                for r in range(GR):
                    dve.wait_ge(a_hi, SWA_A + 4 * p + r + 1)
                    dve.tensor_tensor(alo[:, r, :], q_a[:, r, :], f32(ahi[:, r, :]), ALU.subtract).then_inc(a_lo, 1)
                for m in range(DT):
                    split(quad, 12 + m, 13 + m)
                    add_x(m, 6 + m, n + 13 + m)
                    if p == NPAIR - 1 and m:
                        gain_x(m - 1, 3)
                if p == NPAIR - 1:
                    gain_x(DT - 1, 3)

            dve.wait_ge(ac_in, 16)
            for p in range(NPAIR):
                pair(p)
            mlp(FFN1_SLAB, FFN1_MT, FFN1_A, FFC * 4, 3, None)

        @block.tensor
        def _(pe):
            def passes(m, slot, s, k, hi, lo, first, last):
                w = slice(k * P, (k + 1) * P)
                for j, (a, b) in enumerate(((whi, hi), (whi, lo), (wlo, hi))):
                    for t in range(NTB):
                        mm = pe.matmul(ps[:, 3 * (m % 2) + t, 0:TB], a[:, slot, w],
                                       b[:, s * KG + k, t * TB:(t + 1) * TB],
                                       start=(first and j == 0), stop=(last and j == 2))
                return mm

            def product(m, mt, quad, i0, n_slabs, hi, lo, k_ready=None, between=None):
                for s in range(n_slabs):
                    i = i0 + s
                    pe.wait_ge(w_lo, quad * 4 + (i + 1))
                    if s == 0 and not (isinstance(mt, int) and mt < 2):
                        pe.wait_ge(mt_free, mt - 1)
                    for k in range(KG):
                        if k_ready is not None:
                            pe.wait_ge(k_ready[0], k_ready[1] + (s * KG + k + 1))
                        mm = passes(m, i % RING, s, k, hi, lo, s == 0 and k == 0, s == n_slabs - 1 and k == KG - 1)
                    mm.then_inc(slab_used, 1)
                    if between is not None:
                        between(s)

            def products(m, mt, quad, i0, a0):
                for j in range(2):
                    pe.wait_ge(w_lo, quad * 4 + (i0 + j + 1))
                    pe.wait_ge(mt_free, mt + (j - 1))
                    for k in range(KG - 1):
                        if j == 0:
                            pe.wait_ge(a_lo, a0 + (k + 1))
                        passes(m + j, (i0 + j) % RING, 0, k, ahi, alo, k == 0, False)
                pe.wait_ge(a_lo, a0 + KG)
                for j in range(2):
                    passes(m + j, (i0 + j) % RING, 0, KG - 1, ahi, alo, False, True).then_inc(slab_used, 1)
                for j in range(2, DT):
                    product(m + j, mt + j, quad, i0 + j, 1, ahi, alo)

            def mean_squares(i, squares, select):
                for c in range(CH + 1):
                    t = min(c * P, TOK - P)
                    mm = pe.matmul(ps[:, 7, 2 * c:2 * c + 2], squares[:, t:t + P], select, start=True, stop=True)
                mm.then_inc(msum_done, 1)

            def spread(i, part):
                pe.wait_ge(wide_done, i + 1)
                for c in ((0, 1, 2, 3), (4, 5, 6, 7), (8,))[part]:
                    mm = pe.transpose(ps[:, PARTS[part][0], c % 4 * P:(c % 4 + 1) * P],
                                      wide[:, 2 * c:2 * c + 2, :].rearrange("p s f -> p (s f)"), ident)
                mm.then_inc(spread_done, 1)

            def norm(phase, step):
                if step < 0:
                    pe.wait_ge(sum_done, (phase + 1) * DT)
                    mean_squares(norm_use(phase), ssum, ones[:, 0:2])
                else:
                    spread(norm_use(phase), 0)
                    spread(norm_use(phase), 1)
                    pe.wait_ge(rst_done, 3 * phase + 1)
                    spread(norm_use(phase), 2)

            def first_products():
                for k in range(DT):
                    pe.wait_ge(h_lo, k + 1)
                    for m in range(2 if k < KG else 1):
                        if k % KG == 0:
                            pe.wait_ge(w_lo, (k // KG) * 2 + m + 1)
                        mm = passes(m, (k // KG) * 2 + m, k // KG, k % KG, hhi, hlo, k == 0, k == DT - 1)
                        if k % KG == KG - 1:
                            mm.then_inc(slab_used, 1)
                pe.wait_ge(w_lo, 4)
                for k in range(KG, DT):
                    mm = passes(1, 3, 1, k % KG, hhi, hlo, False, k == DT - 1)
                    if k == KG + 1:
                        norm(0, -1)
                mm.then_inc(slab_used, 1)
                norm(0, 0)

            def turn_v(h, e):
                pe.wait_ge(mt_free, h * RET_MT + (4 + e + 1))
                for half in range(2):
                    if e:
                        pe.wait_ge(v_kept, h * 9 + (2 * e + half - 1))
                    elif half:
                        pe.wait_ge(kt_kept, h * (CH + 1) + 1)
                        pe.wait_ge(sc_kept, h * (CH + 1) + 1)
                    for c in range(4):
                        t = (4 * half + c) * P
                        mm = pe.transpose(ps[:, 6 + half, c * P:(c + 1) * P], tmp[:, e, t:t + P], ident)
                    mm.then_inc(v_turned, 1)

            def keys_and_scores(h, c):
                first = h * (CH + 1)
                rows = NS if c == CH else P
                tok = slice(c * P, c * P + rows)
                if c == CH:
                    pe.wait_ge(four_ready, h * 5 + 1)
                elif c == 0:
                    pe.wait_ge(v_kept, h * 9 + 7)
                else:
                    pe.wait_ge(sc_kept, first + c)
                    pe.wait_ge(kt_kept, first + c)
                keys = [k4[:, j, :, :].rearrange("p r t -> p (r t)") if c == CH else qk[:, 2 + j, tok]
                        for j in range(2)]
                for j in range(2):
                    pe.matmul(ps[:, score_bank(c), DK:DK + rows], keys[j], qk[:, j, tok],
                                   start=(j == 0), stop=(j == 1))
                for j in range(2):
                    mm = pe.transpose(ps[:, score_bank(c), j * P:(j + 1) * P], keys[j], ident)
                mm.then_inc(kt_done, 1)

            def turn_o(h, c):
                i = h * (CH + 1) + c
                pe.wait_ge(o_kept, i + 1)
                if c == 0:
                    pe.wait_ge(vs_ready, h + 1)
                else:
                    pe.wait_ge(ot_kept, i)
                for e in range(4):
                    mm = pe.transpose(ps[:, 4, e * P:(e + 1) * P], o_tok[:, e * P:(e + 1) * P], ident)
                mm.then_inc(ot_done, 1)

            def chunk(h, c):
                i = h * (CH + 1) + c
                tok = slice(c * P, (c + 1) * P)
                bank = 2 + c % 2
                if c >= 2:
                    pe.wait_ge(o_kept, i - 1)
                if c:
                    pe.wait_ge(s_upd, h * CH + c)
                    for j in range(2):
                        pe.matmul(ps[:, bank, :], qk[:, j, tok], s_ret[:, j, :], start=(j == 0), stop=False)
                pe.wait_ge(kt_kept, i + 2)
                if c:
                    pe.wait_ge(s0_upd, h * NB + c)
                for j in range(2):
                    mm = pe.matmul(ps[:, j, :], k_tok[:, c % 2, j * P:(j + 1) * P], v_tok[:, c, :],
                                   start=True, stop=True)
                mm.then_inc(st_done, 1)
                if c + 1 < CH:
                    keys_and_scores(h, c + 1)
                pe.wait_ge(sc_kept, i + 2)
                pe.matmul(ps[:, bank, :], sc_t[:, c % 2, :], v_tok[:, c, :], start=(c == 0), stop=True
                          ).then_inc(o_done, 1)
                if c:
                    turn_o(h, c - 1)

            def sample_within(h):
                pe.wait_ge(v_kept, h * 9 + 8)
                pe.wait_ge(vs_ready, h + 1)
                pe.wait_ge(sel_ready, h * (1 + 2 * NB) + 1)
                pe.matmul(ps[0:NS, 7, :], sc_smp[:, :], v_smp[:, :], start=True, stop=False)

            def sample_head(h, b):
                pe.wait_ge(sel_ready, h * (1 + 2 * NB) + (1 + 2 * (b + 1)))
                pe.wait_ge(s0_in[b % S0_RING], s0_count(h, b) + 16)
                for j in range(2):
                    mm = pe.matmul(ps[0:NS, 7, :], q_sel[:, b % 2, j, :], s0[:, b % S0_RING, j, :],
                                   start=False, stop=(b == NB - 1 and j == 1))
                if b == NB - 1:
                    mm.then_inc(o_done, 1)
                pe.wait_ge(s_upd, h * CH + (b + 1))
                for j in range(2):
                    mm = pe.matmul(ps[:, j, :], k_sel[:, b % 2, j * P:(j + 1) * P], v_smp[:, :],
                                   start=True, stop=True)
                mm.then_inc(sts_done, 1)

            def ret_head(h, first):
                quad = h * (RET_SLABS // 4)
                mt = h * RET_MT
                if first:
                    first_products()
                for m in range(2 if first else 0, 8):
                    product(m, mt + m, quad, 2 * m, 2, hhi, hlo)
                    if m == 4:
                        keys_and_scores(h, CH)
                    elif m > 4:
                        turn_v(h, m - 5)
                pe.wait_ge(mt_free, mt + 8)
                turn_v(h, 3)
                pe.wait_ge(four_ready, h * 5 + 5)
                for e in range(4):
                    mm = pe.transpose(ps[:, 4, e * P:(e + 1) * P], v4[:, e, :, :].rearrange("p r t -> p (r t)"), ident)
                mm.then_inc(v_turned, 1)
                keys_and_scores(h, 0)
                for c in range(CH):
                    chunk(h, c)
                    if c == 0:
                        sample_within(h)
                    sample_head(h, c)
                turn_o(h, CH - 1)
                pe.wait_ge(s0_upd, (h + 1) * NB)
                product(8, mt + 8, quad, 16, 2, hhi, hlo, None, lambda s: s or turn_o(h, CH))
                pe.wait_ge(ot_kept, (h + 1) * (CH + 1))
                for m in range(9, 12):
                    product(m, mt + m, quad, 2 * m, 2, hhi, hlo)
                products(12, mt + 12, quad, 24, h * 4)

            ret_head(0, True)
            with pe.Fori(1, RH) as h:
                ret_head(h, False)

            def ffn(c, slab0, mt0, a0, phase):
                quad = c * (FFN_SLABS // 4) + slab0 // 4
                mt = c * FFN_MT + mt0
                for m in range(4):
                    first = m == 0 and phase is not None
                    product(m, mt + m, quad, 2 * m, 2, hhi, hlo, (h_lo, phase * DT) if first else None,
                            (lambda s: s or norm(phase, 0)) if phase is not None and m == 1 else None)
                    if first:
                        norm(phase, -1)
                products(4, mt + 4, quad, 8, c * 4 + a0)

            def mlp(slab0, mt0, a0, phase):
                ffn(0, slab0, mt0, a0, phase)
                with pe.Fori(1, FFC) as c:
                    ffn(c, slab0, mt0, a0, None)

            mlp(FFN0_SLAB, FFN0_MT, FFN0_A, 1)

            def tile_squares(p, m):
                if m == 0 and p == 0:
                    pe.wait_ge(rst_done, 9)
                elif m == 0:
                    pe.wait_ge(kct_kept, 2 * (p + 1))
                pe.wait_ge(zz_done, 5 * p + m + 1)
                mean_squares(tile_use(p, m), zz, head_sel)

            def spread_tile(p, m, part):
                if part == 0 and m:
                    pe.wait_ge(zq_done, kept_before(p) + 3 * m)
                elif part == 2:
                    pe.wait_ge(zq_done, kept_before(p) + (3 * m + 1 if m < GR else 3 * m + 2))
                spread(tile_use(p, m), part)

            def heads_rms(p, m):
                def between(step):
                    if step == 0:
                        if m == 1 and p == 0:
                            norm(2, 0)
                            return
                        if m == 2 and p == 0:
                            spread_tile(p, 0, 0)
                            spread_tile(p, 0, 1)
                        if m > 1:
                            spread_tile(p, m - 2, 2)
                            pe.wait_ge(zq_done, kept_before(p) + 3 * (m - 2) + 2)
                        tile_squares(p, m - 1)
                    elif m == 1 and p == 0:
                        tile_squares(p, 0)
                    else:
                        spread_tile(p, m - 1, 0)
                        spread_tile(p, m - 1, 1)
                return between

            def turn_cache(p):
                pe.wait_ge(kc_in, 32 * (p + 1))
                for half in range(2):
                    for b in range(4):
                        mm = pe.transpose(ps[:, 6 + half, b * P:(b + 1) * P], kc[:, 4 * half + b, :], ident)
                    mm.then_inc(kct_done, 1)

            def sample_scores(p):
                pe.wait_ge(qbd_ready, 2 * (p + 1))
                pe.wait_ge(kct_kept, 2 * (p + 1))
                for b in range(NB):
                    col = (b % 3) * KEYS
                    pe.matmul(ps[0:NS, 4 + b // 3, col:col + P], q_bd[:, b, :], kc[:, b, :], start=True, stop=True)
                    for s in range(2):
                        mm = pe.matmul(ps[0:NS, 4 + b // 3, col + P:col + KEYS], q_bd[:, b, :], k_z[:, s, SEQ:TOK],
                                       start=(s == 0), stop=(s == 1))
                mm.then_inc(sas_done, 1)

            def sample_turn(p):
                pe.wait_ge(sa_ready, p + 1)
                for b in range(NB):
                    pe.transpose(ps[:, 7, b * NS:(b + 1) * NS], sa[0:NS, b, 0:P], ident[0:NS, 0:NS])
                for b in range(NB, 2 * NB):
                    mm = pe.transpose(ps[0:NS, 7, b * NS:(b + 1) * NS], sa[0:NS, b - NB, P:KEYS],
                                      ident[0:NS, 0:NS])
                mm.then_inc(pts_done, 1)

            def sample_out(p):
                pe.wait_ge(pts_kept, 2 * (p + 1))
                for b in range(NB):
                    out = ps[:, 7, b * NS:(b + 1) * NS]
                    pe.matmul(out, vc[:, b, :], pts[:, 0, b, :], start=True, stop=False)
                    mm = pe.matmul(out, v_a[0:NS, CH, :], pts[0:NS, 1, b, :], start=False, stop=True)
                mm.then_inc(os_done, 1)

            def block_scores(p, k):
                u, c, s = p * HU + k, k // 2, k % 2
                if k >= 2:
                    pe.wait_ge(s_kept, u - 1)
                lo = P if c == 0 else 0
                keys = slice((c - 1) * P + lo, (c + 1) * P)
                for r in range(GR):
                    col = (r % 2) * 2 * P
                    mm = pe.matmul(ps[:, 2 * s + r // 2, col + lo:col + 2 * P], q_a[:, r, c * P:(c + 1) * P],
                                   k_z[:, s, keys], start=True, stop=True)
                mm.then_inc(s_done, 1)

            def turn_probs(p, k):
                u = p * HU + k
                pe.wait_ge(pn_done, u + 1)
                for t in range(0 if k >= 2 else 1, 2):
                    if t == 0 and k > 2:
                        pe.wait_ge(pt0_kept, p * (HU - 2) + k - 2)
                    if t == 1 and k:
                        pe.wait_ge(pt1_kept, u)
                    for r in range(GR):
                        mm = pe.transpose(ps[:, 4 + t, r * P:(r + 1) * P], p_a[:, u % 4, r, t * P:(t + 1) * P], ident)
                    mm.then_inc(pt_done, 1)

            def block_out(p, k):
                u, c, s = p * HU + k, k // 2, k % 2
                pe.wait_ge(pt1_kept, u + 1)
                if k >= 2:
                    pe.wait_ge(pt0_kept, p * (HU - 2) + k - 1)
                    pe.wait_ge(out_kept, u - 1)
                elif k == 1:
                    pe.wait_ge(os_kept, 2 * (p + 1))
                for t in range(0 if c else 1, 2):
                    mm = pe.matmul(ps[:, 6 + s, :], v_a[:, c - 1 + t, :], pt_a[:, u % 2, t, :],
                                   start=(t == 0 or c == 0), stop=(t == 1))
                mm.then_inc(pv_done, 1)

            def pair(p):
                n = SWA_SLAB + p * SWA_SLABS
                mt = SWA_MT0 + p * SWA_MT
                for m in range(6):
                    first = p == 0 and m == 0
                    product(m, mt + m, n // 4, 2 * m, 2, hhi, hlo, (h_lo, 2 * DT) if first else None,
                            heads_rms(p, m) if m else None)
                    if m == 0:
                        turn_cache(p)
                        if first:
                            pe.wait_ge(kct_kept, 2)
                            norm(2, -1)
                pe.wait_ge(mt_free, mt + 6)
                for half in range(2):
                    for c in range(4):
                        t = (4 * half + c) * P
                        mm = pe.transpose(ps[:, half, c * P:(c + 1) * P], vt_a[:, t:t + P], ident)
                    mm.then_inc(av_turned, 1)
                spread_tile(p, 4, 2)
                pe.transpose(ps[0:NS, 2, 0:P], vt_a[:, SEQ:TOK], ident).then_inc(av_turned, 1)
                pe.wait_ge(av_kept, 3 * (p + 1))
                pe.wait_ge(zq_done, kept_before(p + 1))
                pe.wait_ge(kz_zero, 2)
                block_scores(p, 0)
                block_scores(p, 1)
                for s in range(2):
                    pe.transpose(ps[:, 7, s * P:(s + 1) * P], k_z[:, s, SEQ - P:SEQ], ident)
                    mm = pe.transpose(ps[0:NS, 7, (2 + s) * P:(3 + s) * P], k_z[:, s, SEQ:TOK], ident)
                mm.then_inc(nk_done, 1)
                sample_scores(p)
                block_scores(p, 2)
                pe.wait_ge(sas_kept, 3 * (p + 1))
                for k in range(HU):
                    if k + 3 < HU:
                        block_scores(p, k + 3)
                    if k == 3:
                        sample_out(p)
                    turn_probs(p, k)
                    if k == 2:
                        pe.wait_ge(nk_kept, 4 * (p + 1))
                        sample_turn(p)
                    elif k == 3:
                        block_out(p, 1)
                        block_out(p, 2)
                    elif k:
                        block_out(p, k - 1)
                block_out(p, HU - 1)
                products(6, mt + 6, n // 4, 12, SWA_A + 4 * p)

            pe.wait_ge(ac_in, 16)
            for p in range(NPAIR):
                pair(p)
            mlp(FFN1_SLAB, FFN1_MT, FFN1_A, 3)


def _slab(w, rows, cols):
    return w[rows][:, cols].reshape(KG, P, P).transpose(1, 0, 2).reshape(P, KG * P)


def _weights(inputs):
    w_in, w_out = inputs["ret_w_in"][0], inputs["ret_w_out"][0]
    w_qkv, w_o = inputs["swa_w_qkv"][0], inputs["swa_w_o"][0]
    half = [np.arange(0, D // 2), np.arange(D // 2, D)]
    tile = [np.arange(m * P, (m + 1) * P) for m in range(DT)]
    slabs = []
    for h in range(RH):
        starts = [h * DK, h * DK + P, D + h * DK, D + h * DK + P]
        starts += [2 * D + h * DV + m * P for m in range(4)] + [4 * D + h * DV + m * P for m in range(4)]
        slabs += [_slab(w_in, rows, np.arange(s, s + P)) for s in starts for rows in half]
        slabs += [_slab(w_out, np.arange(h * DV, (h + 1) * DV), cols) for cols in tile]

    def ffn(layer):
        up, down = inputs["ffn_w_up"][layer], inputs["ffn_w_down"][layer]
        for c in range(FFC):
            yield from (_slab(up, rows, np.arange(c * 512 + m * P, c * 512 + (m + 1) * P))
                        for m in range(4) for rows in half)
            yield from (_slab(down, np.arange(c * 512, (c + 1) * 512), cols) for cols in tile)

    slabs[1], slabs[2] = slabs[2], slabs[1]
    slabs += ffn(0)
    for p in range(NPAIR):
        heads = [np.concatenate([np.arange((GR * (2 * p + s) + r) * HD, (GR * (2 * p + s) + r + 1) * HD)
                                 for s in range(2)]) for r in range(GR)]
        kv = [D + KVH * HD * j + np.arange(2 * p * HD, (2 * p + 2) * HD) for j in range(2)]
        slabs += [_slab(w_qkv, rows, cols) for cols in heads + kv for rows in half]
        slabs += [_slab(w_o, np.concatenate(heads), cols) for cols in tile]
    slabs += ffn(1)
    return np.stack(slabs)


def _rope(width):
    half = width // 2
    inv = np.float32(THETA) ** (-np.arange(half, dtype=np.float32) / np.float32(half))
    pos = np.concatenate([np.arange(SEQ), np.tile(PAST + np.arange(NT), NB)]).astype(np.float32)
    ang = (inv[:, None] * pos[None, :]).astype(np.float32).astype(np.float64)
    return np.cos(ang).astype(np.float32), np.sin(ang).astype(np.float32)


def _constants():
    lg = np.log1p(-np.exp2(-5.0 - np.arange(RH)))
    i = np.arange(P)
    t, seq = np.arange(NS) % NT, np.arange(NS) // NT
    t4 = np.tile(t, 4)
    cols = np.zeros((P, C_N), np.float32)
    cols[:, C_ID:C_ID + P] = np.eye(P)
    cols[:, C_ONE:C_ONE + P] = 1.0
    cols[:, C_EPS] = EPS
    scale = DK ** -0.5
    decays = np.zeros((RH, P, 6), np.float32)
    decays[:, :, H_QDEC] = np.exp(lg[:, None] * (i + 1))
    decays[:, :, H_KDEC] = np.exp(lg[:, None] * (P - 1 - i)) * scale
    decays[:, :, H_CDEC] = np.exp(lg * P)[:, None]
    decays[:, :NS, H_QDS] = np.exp(lg[:, None] * (t + 1))
    decays[:, :, H_KDS] = np.exp(lg[:, None] * (NT - 1 - t4)) * scale
    decays[:, :, H_CDS] = np.exp(lg * NT)[:, None]
    cols[:, C_BM:C_BM + NB] = np.tile(seq, 4)[:, None] == np.arange(NB)
    masks = np.zeros((RH, P, P + NS), np.float32)
    for h in range(RH):
        masks[h, :, :P] = np.where(i[None, :] >= i[:, None], np.exp(-(i + 1.0) * lg[h])[:, None] * scale, 0.0)
        own = (seq[:, None] == seq[None, :]) & (t[None, :] >= t[:, None])
        masks[h, :, P:] = np.tile(np.where(own, np.exp(-(t + 1.0) * lg[h])[:, None] * scale, 0.0), (4, 1))
    attn = np.zeros((P, A_N), np.float32)
    attn[:, A_SEL:A_SEL + 2] = (i[:, None] // HD) == np.arange(2)
    d = i[:, None] + P - np.arange(2 * P)[None, :]
    attn[:, A_MASK:A_MASK + 2 * P] = np.where((d >= 0) & (d < WIN), 0.0, NEG)
    tq = np.arange(NS) % NT
    s_mask = np.full((NS, NB, KEYS), NEG, np.float32)
    d = tq[:, None] + WIN - np.arange(WIN)[None, :]
    s_mask[:, :, :WIN] = np.where((d >= 0) & (d < WIN), 0.0, NEG)[:, None, :]
    for b in range(NB):
        for j in range(NT):
            s_mask[tq >= j, b, WIN + NT * b + j] = 0.0
    cos, sin = _rope(DK)
    tables = np.stack([cos, sin], axis=1)
    cos, sin = _rope(HD)
    attn_tables = np.stack([np.concatenate([cos] * 4), np.concatenate([-sin, sin] * 2)], axis=1)
    return cols, masks, decays, attn, s_mask, tables, attn_tables


def kernel(**inputs):
    import concourse.bacc as _bacc
    from concourse.bass_utils import run_bass_kernel_spmd as _run

    inputs = {k: np.asarray(v) for k, v in inputs.items()}
    cols, masks, decays, attn, s_mask, tables, attn_tables = _constants()
    gains = [inputs["norm_mix"][0], inputs["norm_ffn"][0], inputs["norm_mix"][1], inputs["norm_ffn"][1]]
    for phase, g in enumerate(gains):
        cols[:, C_GAIN + phase * DT:C_GAIN + (phase + 1) * DT] = g.reshape(DT, P).T
    for plain, exchanged, g in ((C_QN, C_QX, inputs["swa_q_norm"][0]), (C_KN, C_KX, inputs["swa_k_norm"][0])):
        cols[:, plain] = np.concatenate([g, g])
        cols[:, exchanged] = np.concatenate([g[HD // 2:], g[:HD // 2]] * 2)
    sinks = inputs["swa_sinks"][0]
    cols[:, C_SINK:C_SINK + NPAIR * PH] = sinks[None, :]
    for p in range(NPAIR):
        cols[:NS, C_SINKS + p] = np.repeat(sinks[PH * p:PH * (p + 1)], NT)
    xs = np.concatenate([inputs["x_prompt"][0], inputs["x_sample"].reshape(NS, D)])
    data = {
        "xT": xs.T.reshape(DT, P, TOK).transpose(1, 0, 2), "weights": _weights(inputs), "tables": tables,
        "attn_tables": attn_tables, "consts": cols, "ret_masks": masks, "ret_decays": decays,
        "attn_consts": attn, "sample_mask": s_mask,
        "state_in": inputs["state_ret"][0], "cache_k": inputs["cache_swa_k"][0].reshape(NB, WIN, KVH * HD),
        "cache_v": inputs["cache_swa_v"][0].reshape(NB, WIN, KVH * HD),
    }
    outs = {
        "yT": (P, DT, TOK), "state_p": (RH, DK, DV), "kp_out": (WIN, KVH * HD), "vp_out": (WIN, KVH * HD),
        "state_s": (NB, RH, DK, DV), "ks_out": (NB, WIN, KVH * HD), "vs_out": (NB, WIN, KVH * HD),
    }
    nc = _bacc.Bacc("TRN2", target_bir_lowering=False, num_devices=1)
    arrays, args = {}, []
    for name, a in data.items():
        a = np.ascontiguousarray(a)
        arrays[f"in_{name}"] = a
        args.append(nc.dram_tensor(f"in_{name}", a.shape, mybir.dt.from_np(a.dtype), kind="ExternalInput").ap())
    for name, shape in outs.items():
        args.append(nc.dram_tensor(f"out_{name}", shape, F32, kind="ExternalOutput").ap())
    trunk(nc, *args)
    r = _run(nc, [arrays], core_ids=[0]).results[0]
    got = {name: np.asarray(r[f"out_{name}"]) for name in outs}
    y = got["yT"].transpose(1, 0, 2).reshape(D, TOK).T
    return (y[:SEQ].reshape(1, SEQ, D), y[SEQ:].reshape(NB, NT, D), got["state_p"].reshape(1, 1, RH, DK, DV),
            got["kp_out"].reshape(1, 1, WIN, KVH, HD), got["vp_out"].reshape(1, 1, WIN, KVH, HD),
            got["state_s"].reshape(1, NB, RH, DK, DV), got["ks_out"].reshape(1, NB, WIN, KVH, HD),
            got["vs_out"].reshape(1, NB, WIN, KVH, HD))
```
